# Optimizing a Trainium2 kernel written in Bass

```python
import jax, jax.numpy as jnp
from jax import lax
import numpy as np
import math

D_MODEL = 1024
BATCH = 1
SEQ = 256
DEPTH = 1

HEAD_DIM = 64
NSA_HEADS = 8
NSA_KV = 2
DSA_HEADS = 8
IDX_HEADS = 4
IDX_DIM = 64
CMP_LEN = 32
CMP_STRIDE = 16
CMP_HIDDEN = 2 * HEAD_DIM
SLC_LEN = 64
SLC_TOPN = 16
WIN = 512
DSA_TOPK = 256
D_FF = 4 * D_MODEL
D_MIX = (NSA_HEADS + DSA_HEADS) * HEAD_DIM
ROPE_THETA = 10000.0
EPS = 1e-6
Q_BLOCK = 128
SLC_Q_BLOCK = 16
NEG = -1e30
NSA_COLS = [NSA_HEADS * HEAD_DIM] + [NSA_KV * HEAD_DIM] * 6 + [NSA_HEADS * 3]
DSA_COLS = [DSA_HEADS * HEAD_DIM, HEAD_DIM, HEAD_DIM, IDX_HEADS * IDX_DIM, IDX_DIM, IDX_HEADS]
IN_COLS = NSA_COLS + DSA_COLS
D_IN = sum(IN_COLS)


def rms_norm(x, g):
    xf = x.astype(jnp.float32)
    y = xf * lax.rsqrt(jnp.mean(xf * xf, axis=-1, keepdims=True) + EPS)
    return (y * g.astype(jnp.float32)).astype(x.dtype)

def rope(x, pos):
    half = x.shape[-1] // 2
    inv = ROPE_THETA ** (-jnp.arange(half, dtype=jnp.float32) / half)
    ang = pos.astype(jnp.float32)[:, :, None] * inv
    cos = jnp.cos(ang)[:, :, None, :]
    sin = jnp.sin(ang)[:, :, None, :]
    xf = x.astype(jnp.float32)
    x1, x2 = xf[..., :half], xf[..., half:]
    return jnp.concatenate([x1 * cos - x2 * sin, x2 * cos + x1 * sin], axis=-1).astype(x.dtype)

def masked_softmax(s, mask):
    s = jnp.where(mask, s.astype(jnp.float32), NEG)
    return jax.nn.softmax(s, axis=-1) * mask.astype(jnp.float32)

def compress(kv, pe, w1, w2):
    B, T, G, dh = kv.shape
    n_cmp = (T - CMP_LEN) // CMP_STRIDE + 1
    blk = np.arange(n_cmp)[:, None] * CMP_STRIDE + np.arange(CMP_LEN)[None, :]
    blocks = kv[:, blk] + pe[None, None, :, None, :]
    flat = blocks.transpose(0, 1, 3, 2, 4).reshape(B, n_cmp, G, CMP_LEN * dh)
    return jax.nn.gelu(flat @ w1) @ w2

def nsa_attention(q, kc, vc, ks, vs, kw, vw, gate_logits, pe_k, pe_v, w1k, w2k, w1v, w2v):
    B, T, H, dh = q.shape
    G = kc.shape[2]
    R = H // G
    scale = dh ** -0.5
    q_t = q.reshape(B, T, G, R, dh).transpose(0, 2, 3, 1, 4)
    t_idx = np.arange(T)

    k_cmp = compress(kc, pe_k, w1k, w2k)
    v_cmp = compress(vc, pe_v, w1v, w2v)
    n_cmp = k_cmp.shape[1]
    cmp_start = np.arange(n_cmp) * CMP_STRIDE
    cmp_end = cmp_start + CMP_LEN - 1
    mask_c = jnp.asarray(cmp_end[None, :] <= t_idx[:, None])
    s_c = jnp.einsum('bgrtd,bngd->bgrtn', q_t, k_cmp) * scale
    p_c = masked_softmax(s_c, mask_c)
    o_cmp = jnp.einsum('bgrtn,bngd->bgrtd', p_c.astype(v_cmp.dtype), v_cmp)

    n_slc = T // SLC_LEN
    n_sel = min(SLC_TOPN, n_slc)
    slc_start = np.arange(n_slc) * SLC_LEN
    slc_end = slc_start + SLC_LEN - 1
    overlap = ((cmp_start[:, None] <= slc_end[None, :]) & (cmp_end[:, None] >= slc_start[None, :])).astype(np.float32)
    imp = jnp.einsum('bgrtn,nj->bgtj', p_c, jnp.asarray(overlap))
    j = np.arange(n_slc)[None, :]
    cur = (t_idx // SLC_LEN)[:, None]
    valid = jnp.asarray(j <= cur)
    forced = jnp.asarray((j == 0) | (j == cur) | (j == cur - 1))
    sel_score = jnp.where(valid, jnp.where(forced, jnp.inf, imp), -jnp.inf)
    _, sel = lax.top_k(sel_score, n_sel)

    kb = ks.reshape(B, n_slc, SLC_LEN, G, dh).transpose(0, 3, 1, 2, 4)
    vb = vs.reshape(B, n_slc, SLC_LEN, G, dh).transpose(0, 3, 1, 2, 4)
    nq = T // SLC_Q_BLOCK
    n_key = n_sel * SLC_LEN
    q_ch = q_t.reshape(B, G, R, nq, SLC_Q_BLOCK, dh).transpose(3, 0, 1, 2, 4, 5)
    i_ch = sel.reshape(B, G, nq, SLC_Q_BLOCK, n_sel).transpose(2, 0, 1, 3, 4)
    t_ch = jnp.arange(T, dtype=jnp.int32).reshape(nq, SLC_Q_BLOCK)
    bi = jnp.arange(B)[:, None, None, None]
    gi = jnp.arange(G)[None, :, None, None]

    def sel_chunk(args):
        qc, ic, tc = args
        kg = kb[bi, gi, ic].reshape(B, G, SLC_Q_BLOCK, n_key, dh)
        vg = vb[bi, gi, ic].reshape(B, G, SLC_Q_BLOCK, n_key, dh)
        kpos = (ic[..., None] * SLC_LEN + jnp.arange(SLC_LEN)).reshape(B, G, SLC_Q_BLOCK, n_key)
        mask = (kpos <= tc[None, None, :, None])[:, :, None]
        s = jnp.einsum('bgrqd,bgqkd->bgrqk', qc, kg) * scale
        p = masked_softmax(s, mask)
        return jnp.einsum('bgrqk,bgqkd->bgrqd', p.astype(vg.dtype), vg)

    o_slc = lax.map(sel_chunk, (q_ch, i_ch, t_ch))
    o_slc = o_slc.transpose(1, 2, 3, 0, 4, 5).reshape(B, G, R, T, dh)

    kp = jnp.pad(kw, ((0, 0), (WIN, 0), (0, 0), (0, 0)))
    vp = jnp.pad(vw, ((0, 0), (WIN, 0), (0, 0), (0, 0)))
    nb = T // Q_BLOCK
    span = WIN + Q_BLOCK
    q_b = q_t.reshape(B, G, R, nb, Q_BLOCK, dh).transpose(3, 0, 1, 2, 4, 5)

    def win_block(args):
        qb, bidx = args
        s0 = bidx * Q_BLOCK
        kk = lax.dynamic_slice_in_dim(kp, s0, span, axis=1)
        vv = lax.dynamic_slice_in_dim(vp, s0, span, axis=1)
        kpos = s0 - WIN + jnp.arange(span)
        tq = s0 + jnp.arange(Q_BLOCK)
        mask = (kpos[None, :] <= tq[:, None]) & (kpos[None, :] > tq[:, None] - WIN) & (kpos[None, :] >= 0)
        s = jnp.einsum('bgrqd,bsgd->bgrqs', qb, kk) * scale
        p = masked_softmax(s, mask)
        return jnp.einsum('bgrqs,bsgd->bgrqd', p.astype(vv.dtype), vv)

    o_win = lax.map(win_block, (q_b, jnp.arange(nb)))
    o_win = o_win.transpose(1, 2, 3, 0, 4, 5).reshape(B, G, R, T, dh)

    g = jax.nn.sigmoid(gate_logits.astype(jnp.float32)).reshape(B, T, G, R, 3)
    g = g.transpose(0, 2, 3, 1, 4).astype(q.dtype)
    o = g[..., 0:1] * o_cmp + g[..., 1:2] * o_slc + g[..., 2:3] * o_win
    return o.transpose(0, 3, 1, 2, 4).reshape(B, T, H * dh)

def dsa_attention(q, k, v, q_idx, k_idx, w_idx):
    B, T, H, dh = q.shape
    k_top = min(DSA_TOPK, T // 4)
    scale = dh ** -0.5
    idx_scale = (IDX_HEADS ** -0.5) * (IDX_DIM ** -0.5)
    nb = T // Q_BLOCK
    bi = jnp.arange(B)[:, None, None]
    key_pos = jnp.arange(T)

    def blocks(a):
        return a.reshape((B, nb, Q_BLOCK) + a.shape[2:]).swapaxes(0, 1)

    def dsa_block(args):
        qb, qib, wb, bidx = args
        tq = bidx * Q_BLOCK + jnp.arange(Q_BLOCK)
        logits = jnp.einsum('bqhd,bsd->bqhs', qib, k_idx).astype(jnp.float32)
        score = jnp.einsum('bqh,bqhs->bqs', wb.astype(jnp.float32) * idx_scale, jax.nn.relu(logits))
        score = jnp.where(key_pos[None, None, :] <= tq[None, :, None], score, -jnp.inf)
        _, sel = lax.top_k(score, k_top)
        kg = k[bi, sel]
        vg = v[bi, sel]
        mask = (sel <= tq[None, :, None])[:, None]
        s = jnp.einsum('bqhd,bqkd->bhqk', qb, kg) * scale
        p = masked_softmax(s, mask)
        return jnp.einsum('bhqk,bqkd->bqhd', p.astype(vg.dtype), vg)

    o = lax.map(dsa_block, (blocks(q), blocks(q_idx), blocks(w_idx), jnp.arange(nb)))
    return o.swapaxes(0, 1).reshape(B, T, H * dh)

def first_inputs(seed: int = 0) -> dict:
    key = jax.random.key(seed)
    ks = jax.random.split(key, 20)

    def nrm(k, shape, s):
        return jax.random.normal(k, shape, jnp.float32) * s

    x = nrm(ks[0], (BATCH, SEQ, D_MODEL), 1.0)
    c = nrm(ks[1], (BATCH, D_MODEL), 1.0)
    start = jax.random.randint(ks[2], (BATCH, 1), 0, 4096, dtype=jnp.int32)
    positions = start + jnp.arange(SEQ, dtype=jnp.int32)[None, :]
    return {
        'x': x,
        'c': c,
        'positions': positions,
        'w_ada': nrm(ks[3], (DEPTH, D_MODEL, 6 * D_MODEL), 0.1 * D_MODEL ** -0.5),
        'b_ada': nrm(ks[4], (DEPTH, 6 * D_MODEL), 0.01),
        'g_pre_mix': 1.0 + nrm(ks[5], (DEPTH, D_MODEL), 0.05),
        'g_post_mix': 1.0 + nrm(ks[6], (DEPTH, D_MODEL), 0.05),
        'g_pre_ffn': 1.0 + nrm(ks[7], (DEPTH, D_MODEL), 0.05),
        'g_post_ffn': 1.0 + nrm(ks[8], (DEPTH, D_MODEL), 0.05),
        'w_in': nrm(ks[9], (DEPTH, D_MODEL, D_IN), D_MODEL ** -0.5),
        'cmp_pe_k': nrm(ks[10], (DEPTH, CMP_LEN, HEAD_DIM), 0.02),
        'cmp_pe_v': nrm(ks[11], (DEPTH, CMP_LEN, HEAD_DIM), 0.02),
        'cmp_w1_k': nrm(ks[12], (DEPTH, CMP_LEN * HEAD_DIM, CMP_HIDDEN), (CMP_LEN * HEAD_DIM) ** -0.5),
        'cmp_w2_k': nrm(ks[13], (DEPTH, CMP_HIDDEN, HEAD_DIM), CMP_HIDDEN ** -0.5),
        'cmp_w1_v': nrm(ks[14], (DEPTH, CMP_LEN * HEAD_DIM, CMP_HIDDEN), (CMP_LEN * HEAD_DIM) ** -0.5),
        'cmp_w2_v': nrm(ks[15], (DEPTH, CMP_HIDDEN, HEAD_DIM), CMP_HIDDEN ** -0.5),
        'w_out': nrm(ks[16], (DEPTH, D_MIX, D_MODEL), D_MIX ** -0.5),
        'w_up': nrm(ks[17], (DEPTH, D_MODEL, D_FF), D_MODEL ** -0.5),
        'w_down': nrm(ks[18], (DEPTH, D_FF, D_MODEL), D_FF ** -0.5),
    }

def first_block(x, c, positions, w_ada, b_ada, g_pre_mix, g_post_mix, g_pre_ffn, g_post_ffn,
              w_in, cmp_pe_k, cmp_pe_v, cmp_w1_k, cmp_w2_k, cmp_w1_v, cmp_w2_v,
              w_out, w_up, w_down):
    B, T, _ = x.shape
    splits = np.cumsum(IN_COLS)[:-1].tolist()

    def heads(a, n):
        return a.reshape(B, T, n, -1)

    for l in range(DEPTH):
        mod = c @ w_ada[l] + b_ada[l]
        sh1, sc1, gt1, sh2, sc2, gt2 = jnp.split(mod, 6, axis=-1)

        h = rms_norm(x, g_pre_mix[l]) * (1.0 + sc1[:, None]) + sh1[:, None]
        proj = h @ w_in[l]
        (q_n, kc, vc, ksl, vsl, kw, vw, gl,
         q_d, k_d, v_d, qi, ki, wi) = jnp.split(proj, splits, axis=-1)

        o_nsa = nsa_attention(
            rope(heads(q_n, NSA_HEADS), positions),
            rope(heads(kc, NSA_KV), positions), heads(vc, NSA_KV),
            rope(heads(ksl, NSA_KV), positions), heads(vsl, NSA_KV),
            rope(heads(kw, NSA_KV), positions), heads(vw, NSA_KV),
            gl, cmp_pe_k[l], cmp_pe_v[l], cmp_w1_k[l], cmp_w2_k[l], cmp_w1_v[l], cmp_w2_v[l])

        o_dsa = dsa_attention(
            rope(heads(q_d, DSA_HEADS), positions),
            rope(k_d[:, :, None, :], positions)[:, :, 0],
            v_d,
            rope(heads(qi, IDX_HEADS), positions),
            rope(ki[:, :, None, :], positions)[:, :, 0],
            wi)

        o = jnp.concatenate([o_nsa, o_dsa], axis=-1) @ w_out[l]
        x = x + gt1[:, None] * rms_norm(o, g_post_mix[l])

        h = rms_norm(x, g_pre_ffn[l]) * (1.0 + sc2[:, None]) + sh2[:, None]
        y = jnp.square(jax.nn.relu(h @ w_up[l])) @ w_down[l]
        x = x + gt2[:, None] * rms_norm(y, g_post_ffn[l])
    return x


CHUNK = 64
N_MEM = 256
SB_HEADS = 8
SB_WIDTH = SB_HEADS * HEAD_DIM
HG_HEADS = 4
HG_KEY_DIM = 128
HG_VAL_DIM = 64
HG_KWIDTH = HG_HEADS * HG_KEY_DIM
HG_VWIDTH = HG_HEADS * HG_VAL_DIM
MEM_HEADS = 4
MEM_WIDTH = MEM_HEADS * HEAD_DIM
MIX_WIDTH = SB_WIDTH + HG_VWIDTH + MEM_WIDTH
SPLIT_SIZES = (SB_WIDTH, SB_WIDTH, SB_WIDTH, HG_KWIDTH, HG_KWIDTH, HG_VWIDTH, HG_VWIDTH, MEM_WIDTH)
IN_WIDTH = 3 * SB_WIDTH + 2 * HG_KWIDTH + 2 * HG_VWIDTH + MEM_WIDTH
PEER_HEADS = 8
N_KEYS = 128
N_EXPERTS = N_KEYS * N_KEYS
PEER_TOPK = 16
D_KEY = 256
HALF_KEY = D_KEY // 2
PEER_TOKEN_BLOCK = 128


def rms_norm_2(x, gain):
    xf = x.astype(jnp.float32)
    y = xf * lax.rsqrt(jnp.mean(xf * xf, axis=-1, keepdims=True) + EPS)
    return (y * gain.astype(jnp.float32)).astype(x.dtype)

def stick_breaking_attention(q, k, v):
    b, s, h, d = q.shape
    nb = s // Q_BLOCK
    qb = q.reshape(b, nb, Q_BLOCK, h, d).transpose(1, 0, 3, 2, 4)
    kh = k.transpose(0, 2, 1, 3)
    vh = v.transpose(0, 2, 1, 3)
    key_pos = jnp.arange(s)
    scale = 1.0 / math.sqrt(d)

    def block(args):
        q_blk, i = args
        q_pos = i * Q_BLOCK + jnp.arange(Q_BLOCK)
        z = jnp.einsum('bhqd,bhkd->bhqk', q_blk, kh).astype(jnp.float32) * scale
        mask = key_pos[None, :] < q_pos[:, None]
        log_1m = jnp.where(mask, jax.nn.log_sigmoid(-z), 0.0)
        tail = lax.cumsum(log_1m, axis=3, reverse=True) - log_1m
        log_a = jax.nn.log_sigmoid(z) + tail
        a = jnp.where(mask, jnp.exp(log_a), 0.0)
        return jnp.einsum('bhqk,bhkd->bhqd', a.astype(vh.dtype), vh)

    out = lax.map(block, (qb, jnp.arange(nb)))
    return out.transpose(1, 0, 3, 2, 4).reshape(b, s, h, d)

def hgrn2_recurrence(q, f_logit, i, lower_bound):
    b, s, h, dk = q.shape
    dv = i.shape[-1]
    nc = s // CHUNK
    f = lower_bound + (1.0 - lower_bound) * jax.nn.sigmoid(f_logit.astype(jnp.float32))
    log_f = jnp.log(f)
    k = 1.0 - f
    qf = jax.nn.silu(q.astype(jnp.float32))
    vf = i.astype(jnp.float32)

    def to_chunks(t):
        return t.reshape(b, nc, CHUNK, h, t.shape[-1]).transpose(1, 0, 3, 2, 4)

    causal = jnp.tril(jnp.ones((CHUNK, CHUNK), dtype=bool))[:, :, None]

    def step(state, inp):
        qc, kc, vc, gc = inp
        bcum = jnp.cumsum(gc, axis=2)
        diff = bcum[:, :, :, None, :] - bcum[:, :, None, :, :]
        decay = jnp.where(causal, jnp.exp(jnp.where(causal, diff, 0.0)), 0.0)
        scores = jnp.einsum('bhtk,bhtsk,bhsk->bhts', qc, decay, kc)
        intra = jnp.einsum('bhts,bhsv->bhtv', scores, vc)
        inter = jnp.einsum('bhtk,bhkv->bhtv', qc * jnp.exp(bcum), state)
        last = bcum[:, :, -1:, :]
        new_state = (jnp.exp(last[:, :, 0, :])[..., None] * state
                     + jnp.einsum('bhsk,bhsv->bhkv', kc * jnp.exp(last - bcum), vc))
        return new_state, intra + inter

    state0 = jnp.zeros((b, h, dk, dv), jnp.float32)
    _, out = lax.scan(step, state0, (to_chunks(qf), to_chunks(k), to_chunks(vf), to_chunks(log_f)))
    return out.transpose(1, 0, 3, 2, 4).reshape(b, s, h, dv)

def memory_attention(q, mem_k, mem_v, q_gain, k_gain):
    qn = rms_norm_2(q, q_gain)
    kn = rms_norm_2(mem_k, k_gain)
    scale = 1.0 / math.sqrt(q.shape[-1])
    logits = jnp.einsum('bshd,bmhd->bhsm', qn, kn).astype(jnp.float32) * scale
    p = jax.nn.softmax(logits, axis=-1)
    return jnp.einsum('bhsm,bmhd->bshd', p.astype(mem_v.dtype), mem_v)

def peer_ffn(h, w_query, sub_keys, expert_u, expert_v):
    b, s, d = h.shape
    nb = s // PEER_TOKEN_BLOCK
    hb = h.reshape(b, nb, PEER_TOKEN_BLOCK, d).transpose(1, 0, 2, 3)

    def block(x_blk):
        t = x_blk.shape[1]
        q = (x_blk @ w_query).reshape(b, t, PEER_HEADS, 2, HALF_KEY)
        scores = jnp.einsum('bthcd,hcnd->bthcn', q, sub_keys).astype(jnp.float32)
        top_s, top_i = lax.top_k(scores, PEER_TOPK)
        cand_s = top_s[..., 0, :, None] + top_s[..., 1, None, :]
        cand_i = top_i[..., 0, :, None] * N_KEYS + top_i[..., 1, None, :]
        cand_s = cand_s.reshape(b, t, PEER_HEADS, PEER_TOPK * PEER_TOPK)
        cand_i = cand_i.reshape(b, t, PEER_HEADS, PEER_TOPK * PEER_TOPK)
        best_s, pos = lax.top_k(cand_s, PEER_TOPK)
        expert_idx = jnp.take_along_axis(cand_i, pos, axis=-1)
        gate = jax.nn.softmax(best_s, axis=-1)
        u = expert_u[expert_idx]
        v = expert_v[expert_idx]
        act = jax.nn.gelu(jnp.einsum('btd,bthkd->bthk', x_blk, u).astype(jnp.float32), approximate=False)
        return jnp.einsum('bthk,bthkd->btd', (gate * act).astype(v.dtype), v)

    out = lax.map(block, hb)
    return out.transpose(1, 0, 2, 3).reshape(b, s, d)

def second_inputs(seed: int = 0) -> dict:
    key = jax.random.key(seed)
    ks = jax.random.split(key, 20)
    f32 = jnp.float32
    nrm = lambda k, shape, scale: jax.random.normal(k, shape, f32) * scale
    gain = lambda k, shape: 1.0 + 0.02 * jax.random.normal(k, shape, f32)
    return {
        "x": jax.random.normal(ks[0], (BATCH, SEQ, D_MODEL), f32),
        "mem": jax.random.normal(ks[1], (BATCH, N_MEM, D_MODEL), f32),
        "norm_mix_gain": gain(ks[2], (DEPTH, D_MODEL)),
        "w_in": nrm(ks[3], (DEPTH, D_MODEL, IN_WIDTH), D_MODEL ** -0.5),
        "gamma_lb": nrm(ks[4], (DEPTH + 1, HG_KWIDTH), 0.5),
        "sb_out_gain": gain(ks[5], (DEPTH, SB_HEADS, HEAD_DIM)),
        "hg_out_gain": gain(ks[6], (DEPTH, HG_HEADS, HG_VAL_DIM)),
        "mem_norm_gain": gain(ks[7], (D_MODEL,)),
        "w_mem_kv": nrm(ks[8], (DEPTH, D_MODEL, 2 * MEM_WIDTH), D_MODEL ** -0.5),
        "mem_q_gain": gain(ks[9], (DEPTH, HEAD_DIM)),
        "mem_k_gain": gain(ks[10], (DEPTH, HEAD_DIM)),
        "w_out": nrm(ks[11], (DEPTH, MIX_WIDTH, D_MODEL), MIX_WIDTH ** -0.5),
        "norm_ffn_gain": gain(ks[12], (DEPTH, D_MODEL)),
        "peer_w_query": nrm(ks[13], (DEPTH, D_MODEL, PEER_HEADS * D_KEY), D_MODEL ** -0.5),
        "peer_sub_keys": nrm(ks[14], (DEPTH, PEER_HEADS, 2, N_KEYS, HALF_KEY), HALF_KEY ** -0.5),
        "peer_u": nrm(ks[15], (DEPTH, N_EXPERTS, D_MODEL), D_MODEL ** -0.5),
        "peer_v": nrm(ks[16], (DEPTH, N_EXPERTS, D_MODEL), PEER_HEADS ** -0.5),
    }

def second_block(x, mem, norm_mix_gain, w_in, gamma_lb, sb_out_gain, hg_out_gain, mem_norm_gain,
              w_mem_kv, mem_q_gain, mem_k_gain, w_out, norm_ffn_gain, peer_w_query,
              peer_sub_keys, peer_u, peer_v):
    b, s, _ = x.shape
    m = mem.shape[1]
    lb_all = jnp.cumsum(jax.nn.softmax(gamma_lb.astype(jnp.float32), axis=0), axis=0)
    mem_n = rms_norm_2(mem, mem_norm_gain)
    split_points = [int(v) for v in np.cumsum(SPLIT_SIZES)[:-1]]
    for l in range(DEPTH):
        h = rms_norm_2(x, norm_mix_gain[l])
        proj = h @ w_in[l]
        sb_q, sb_k, sb_v, hg_q, hg_f, hg_i, hg_g, mem_q = jnp.split(proj, split_points, axis=-1)

        sb_o = stick_breaking_attention(sb_q.reshape(b, s, SB_HEADS, HEAD_DIM),
                                        sb_k.reshape(b, s, SB_HEADS, HEAD_DIM),
                                        sb_v.reshape(b, s, SB_HEADS, HEAD_DIM))
        sb_o = rms_norm_2(sb_o, sb_out_gain[l]).reshape(b, s, SB_WIDTH)

        lb = lb_all[l].reshape(HG_HEADS, HG_KEY_DIM)
        hg_o = hgrn2_recurrence(hg_q.reshape(b, s, HG_HEADS, HG_KEY_DIM),
                                hg_f.reshape(b, s, HG_HEADS, HG_KEY_DIM),
                                hg_i.reshape(b, s, HG_HEADS, HG_VAL_DIM), lb).astype(x.dtype)
        hg_o = rms_norm_2(hg_o, hg_out_gain[l]).reshape(b, s, HG_VWIDTH) * jax.nn.silu(hg_g)

        mem_kv = mem_n @ w_mem_kv[l]
        mem_k, mem_v = jnp.split(mem_kv, 2, axis=-1)
        mem_o = memory_attention(mem_q.reshape(b, s, MEM_HEADS, HEAD_DIM),
                                 mem_k.reshape(b, m, MEM_HEADS, HEAD_DIM),
                                 mem_v.reshape(b, m, MEM_HEADS, HEAD_DIM),
                                 mem_q_gain[l], mem_k_gain[l]).reshape(b, s, MEM_WIDTH)

        mixed = jnp.concatenate([sb_o, hg_o, mem_o], axis=-1)
        x = x + mixed @ w_out[l]

        x = x + peer_ffn(rms_norm_2(x, norm_ffn_gain[l]), peer_w_query[l], peer_sub_keys[l],
                         peer_u[l], peer_v[l])
    return x


def setup_inputs(seed=0):
    out = dict(first_inputs(seed))
    for name, value in second_inputs(seed + 1).items():
        if name != "x":
            out[name + "_2"] = value
    return out


def reference(
    x, c, positions, w_ada, b_ada, g_pre_mix, g_post_mix, g_pre_ffn, g_post_ffn, w_in, cmp_pe_k,
    cmp_pe_v, cmp_w1_k, cmp_w2_k, cmp_w1_v, cmp_w2_v, w_out, w_up, w_down, mem_2,
    norm_mix_gain_2, w_in_2, gamma_lb_2, sb_out_gain_2, hg_out_gain_2, mem_norm_gain_2,
    w_mem_kv_2, mem_q_gain_2, mem_k_gain_2, w_out_2, norm_ffn_gain_2, peer_w_query_2,
    peer_sub_keys_2, peer_u_2, peer_v_2,
):
    x = first_block(
        x, c, positions, w_ada, b_ada, g_pre_mix, g_post_mix, g_pre_ffn, g_post_ffn, w_in,
        cmp_pe_k, cmp_pe_v, cmp_w1_k, cmp_w2_k, cmp_w1_v, cmp_w2_v, w_out, w_up, w_down,
    )
    return second_block(
        x, mem_2, norm_mix_gain_2, w_in_2, gamma_lb_2, sb_out_gain_2, hg_out_gain_2,
        mem_norm_gain_2, w_mem_kv_2, mem_q_gain_2, mem_k_gain_2, w_out_2, norm_ffn_gain_2,
        peer_w_query_2, peer_sub_keys_2, peer_u_2, peer_v_2,
    )


_drawn_inputs = setup_inputs


def setup_inputs(seed=0):
    import zlib

    import numpy as np

    out = dict(_drawn_inputs(seed))
    spreads = {}
    factors = {'g_post_mix': 3.749,
     'g_pre_ffn': 3.998,
     'g_post_ffn': 4.55,
     'cmp_pe_k': 8.0,
     'cmp_pe_v': 6.657,
     'gamma_lb_2': 2.689,
     'sb_out_gain_2': 56.703,
     'hg_out_gain_2': 131.231,
     'mem_norm_gain_2': 8.0,
     'mem_q_gain_2': 8.0,
     'mem_k_gain_2': 8.0,
     'norm_ffn_gain_2': 25.378}
    for name, (base, spread) in spreads.items():
        noise = np.random.default_rng([zlib.crc32(name.encode()), seed]).standard_normal(out[name].shape)
        drawn = base * np.exp(spread * noise) if base else spread * noise
        out[name] = __import__('jax').numpy.asarray(drawn.astype(out[name].dtype))
    for name, factor in factors.items():
        out[name] = (out[name] * factor).astype(out[name].dtype)
    return out
```

```python
from contextlib import ExitStack
import math

import numpy as np

import concourse.bass as bass
from concourse import mybir

ALU = mybir.AluOpType
ACT = mybir.ActivationFunctionType
AX = mybir.AxisListType
F32 = mybir.dt.float32
BF16 = mybir.dt.bfloat16
I32 = mybir.dt.int32
U32 = mybir.dt.uint32

P = 128
T = 256
TB = T // P
D = 1024
KD = D // P
HD = 64
HEADS = 8
EPS = 1e-6
NEG = -1e30
TAKEN = -3e38
D_FF = 4 * D

CMP_LEN, CMP_STRIDE = 32, 16
N_CMP = (T - CMP_LEN) // CMP_STRIDE + 1
IDX_HEADS = 4
IDX_SCALE = (IDX_HEADS ** -0.5) * (HD ** -0.5)
DSA_K = min(256, T // 4)
SCALE = HD ** -0.5
N_ROT = 28
ROT_KC, ROT_KD, ROT_KI = 20, 26, 27
PAIR_QN, PAIR_QD, PAIR_QI, PAIR_KS, PAIR_KW, PAIR_KD, PAIR_KI = 0, 4, 8, 10, 11, 12, 13
N_PAIR = 14
PL_VC, PL_VS, PL_VW, PL_VD, PL_GL, PL_WI, N_PLAIN = 0, 128, 256, 384, 448, 472, 476

HG_HEADS = 4
PEER_HEADS = 8
N_KEYS = 128
TOPK = 16
SLOTS = PEER_HEADS * TOPK

_V = {}


def _columns(table, widths):
    at = 0
    for name, w in widths:
        table[name] = (at, at + w)
        at += w
    return at


N_VEC = _columns(_V, [
    ("c", 8), ("b_ada", 48), ("g_pre_mix", 8), ("g_post_mix", 8), ("g_pre_ffn", 8),
    ("g_post_ffn", 8), ("mix2", 8), ("ffn2", 8), ("memg", 8), ("headg", 6), ("qg", 1), ("kg", 1),
    ("gamma", 8), ("pe_k", 16), ("pe_v", 16), ("w2k", 64), ("w2v", 64)])

_C = {}
HG_LEVELS = (1, 2, 4, 8, 16, 32, 64)
N_CONST = _columns(_C, [
    ("tri", P), ("causal", P), ("strict", P), ("strict01", P), ("hgmask", 8 * P),
    ("blk", HEADS), ("cmpadd", TB * 16), ("cmp01", TB * 16), ("invf", HD // 2)])

PI2_A = 6.28125
PI2_B = round((2 * math.pi - PI2_A) * 2 ** 21) / 2 ** 21
PI2_C = 2 * math.pi - PI2_A - PI2_B
ROUND = 1.5 * 2 ** 23
PI_IN = 3.1415925

SLOTW = 2048
RING = 6


def weight_tiles():
    tiles = [("mem_kv", 0, k) for k in range(2)]
    tiles += [("ada", n, k) for n in range(4) for k in range(2)]
    tiles += [("in", n, k) for n in range(5) for k in range(2)]
    tiles += [("cmp1", n, 0) for n in range(2)]
    tiles += [("ada", n, k) for n in range(4, 12) for k in range(2)]
    tiles += [("out", n, k) for n in range(2) for k in range(2)]
    tiles += [("up", n, k) for n in range(8) for k in range(2)]
    tiles += [("down", kg, n) for kg in range(8) for n in range(2)]
    tiles += [("in2", n, k) for n in range(6) for k in range(2)] + [("in2m", 0, 0)]
    tiles += [("out2", n, k) for n in range(2) for k in range(2)]
    tiles += [("wq", n, k) for n in range(4) for k in range(2)]
    tiles += [("keys", 0, 0)]
    return tiles


TILES = weight_tiles()
TILE_AT = {t: n for n, t in enumerate(TILES)}
N_TILES = len(TILES)
N_PAIRS = N_KEYS // 2


def psum_plan():
    used, plan = [0] * 8, {}

    def group(name, bank):
        used[bank] += 1
        plan[name] = (bank, used[bank])

    turn = [0]

    def rotate(name, banks):
        group(name, banks[turn[0] % len(banks)])
        turn[0] += 1

    every = list(range(8))

    def transposed(what):
        for q in range(4):
            rotate((what, q), every)

    transposed("memT")
    for tb in range(TB):
        rotate(("mkv", tb), every)
    rotate(("mkT",), every)
    rotate(("ada", 0), every)
    transposed("h1T")
    for n in range(5):
        for tb in range(TB):
            rotate(("in", n, tb), every)
    for n in range(7):
        rotate(("pairT", n), every)
    rotate(("kcT",), every)
    rotate(("vcT",), every)
    rotate(("cmp", 0), every)
    rotate(("cmp", 1), every)
    rotate(("kcmp",), every)
    rotate(("vblk",), every)
    rotate(("Sc", 0), every)
    rotate(("Sc", 1), every)
    for n in range(4):
        rotate(("L", n), every)
    rotate(("ada", 1), every)
    rotate(("pcT",), every)
    group(("Oc", 0), 6)
    group(("Oc", 1), 7)
    attention_groups(group, UNITS1)
    transposed("oT")
    for n in range(2):
        for tb in range(TB):
            rotate(("out", n, tb), every)
    for n in range(4):
        rotate(("gg", n), every)
    transposed("h2T")
    for n in range(16):
        rotate(("up", n), [0, 1, 2, 3])
    for tb in range(TB):
        for n in range(2):
            group(("down", n, tb), 4 + 2 * tb + n)
    transposed("h3T")
    for name in ("sbq", "sbk"):
        for n in range(2):
            rotate((name, n), every)
    for tb in range(TB):
        rotate(("sbv", tb), every)
    for name in ("hgq", "hgf"):
        for n in range(2):
            rotate((name, n), every)
    for tb in range(TB):
        rotate(("hig", tb), every)
    for tb in range(TB):
        rotate(("mq", tb), every)
    rotate(("mqT",), every)
    for i in range(HEADS + 2):
        if i < HEADS:
            group(("z", i), i % 2)
        if 1 <= i <= HEADS:
            group(("ca", i - 1), 2 + i % 2)
        if i == 2:
            group(("sbo", 0), 4)
            group(("sbo", 1), 5)
    for lv in range(len(HG_LEVELS) + 2):
        if lv < 8:
            group(("hg", lv, 0), 2 * (lv % 2))
            group(("hg", lv, 1), 2 * (lv % 2) + 1)
        else:
            group(("hgx",), 0)
    group(("hgo", 0), 6)
    group(("hgo", 1), 7)
    attention_groups(group, UNITS2)
    transposed("mixT")
    for n in range(2):
        for tb in range(TB):
            rotate(("out2", n, tb), every)
    transposed("h4T")
    for n in range(8):
        rotate(("wq", n), every)
    for n in range(8):
        rotate(("keys", n), every)
    rotate(("idT", 0), every)
    rotate(("idT", 1), every)
    return plan, used


UNITS1 = [(kind, h) for kind in ("slc", "win", "dsa") for h in range(HEADS)]
UNITS2 = [("mem", h) for h in range(4)]
O_BANK = {"slc": 4, "win": 6, "dsa": 4, "mem": 4}


def attention_groups(group, units):
    n = len(units)
    for i in range(n + 2):
        if i < n:
            group(("S", *units[i]), i % 2)
        if 1 <= i <= n:
            group(("PT", *units[i - 1]), 2 + (i - 1) % 2)
        if i >= 2 and units[i - 2][1] == 0:
            for tb in range(TB):
                group(("O", units[i - 2][0], tb), O_BANK[units[i - 2][0]] + tb)


PLAN, USED = psum_plan()


def build(nc, x_in, mem_in, pos_in, vec_in, ident_in, const_in, w_in, u_in, v_in, out):
    with ExitStack() as ctx:
        def sb(name, shape, dt=F32):
            return ctx.enter_context(nc.sbuf_tensor(name, [P] + shape, dt))

        def sem(name):
            return ctx.enter_context(nc.semaphore(name))

        ring = sb("ring", [RING, SLOTW])
        x = sb("x", [TB, D])
        hT = sb("hT", [KD, T])
        ident = sb("ident", [P])
        iota = sb("iota", [P])
        slotT = sb("slotT", [3, T])
        onehot = sb("onehot", [2, 8, P])
        stat = sb("stat", [160])
        arena = sb("arena", [P * T])
        gates = arena[:, :].rearrange("p (t j) -> p t j", t=T)
        mixw = onehot[:, :, :, :].rearrange("p a b c -> p (a b c)")

        where = [0]

        def take(*shape, at=None):
            if at is not None:
                where[0] = at
            n = int(np.prod(shape))
            start = where[0]
            where[0] += n
            assert where[0] <= P * T, where[0]
            v = arena[:, start:start + n]
            if len(shape) == 2:
                v = v.rearrange("p (a b) -> p a b", a=shape[0])
            if len(shape) == 3:
                v = v.rearrange("p (a b c) -> p a b c", a=shape[0], b=shape[1])
            return v

        const = take(N_CONST)
        vec = take(N_VEC)
        mkv = take(TB, 512)
        mkT = take(2, T)
        tmp = take(TB, D)
        junk = take(D)
        negones = take(P)
        identb = take(P // 2).bitcast(BF16)
        causalb = take(P // 2).bitcast(BF16)
        strictb = take(P // 2).bitcast(BF16)
        mod = take(48)
        gain1 = take(KD)
        gain2 = take(KD)
        gg = take(2 * KD)
        prob = take(2, 512)
        probT = take(2, 512)
        osum = take(TB, D)
        common = where[0]
        rot = take(TB, N_ROT * HD)
        plain = take(TB, N_PLAIN)
        pairT = take(N_PAIR, T)
        kvT = [take(3, T), take(3, T)]
        trig = take(8, HD)
        cosd = take(TB, HD)
        sind = take(TB, HD)
        rtmp = take(2, 512)
        hidk = take(2, 16)
        hidv = take(HEADS, 16)
        hbias = take(2)
        kcmpT = take(16)
        vblk = take(HEADS, HD)
        sc = take(TB * HEADS, 16)
        pcT = take(TB, P)
        relu = take(4, 512)
        score = take(TB, T)
        work = take(TB, T)
        maskd = take(TB, T // 2).bitcast(BF16)
        otmp = take(HEADS * HD)
        sig = take(TB, 24)
        wsc = take(TB, 4)
        posf = take(TB)
        posi = take(TB).bitcast(I32)
        ggb = take(2, D)
        block1_end = where[0]
        upT = take(D_FF // P, T, at=common)
        assert where[0] <= block1_end - 2 * D
        sbqT = take(4, T, at=common)
        sbkT = take(4, T)
        sbv = take(TB, 512)
        hq = take(4 * T)
        hf = take(4 * T)
        hk = take(4 * T)
        hb = take(4 * T)
        hsig = take(4 * T)
        hones = take(T)
        hig = take(TB, 512)
        mqn = take(TB, T)
        mqT = take(2, T)
        zabs = take(2, 384)
        zexp = take(2, 384)
        zsp = take(2, 384)
        aT = take(2, 384)
        harg = take(4 * T)
        hqe = take(2, 4 * T)
        hke = take(2, 4 * T)
        hacc = take(TB, 512)
        hx = take(512)
        htmp = take(512)
        lb = take(16)
        pqT = take(16, T, at=common)
        keytmp = take(2, P)
        best1 = take(TB, 16, TOPK)
        idx1 = take(TB, 16 * TOPK).bitcast(U32)
        idx1f = take(TB, 16, TOPK)
        cand = take(PEER_HEADS, T)
        candtmp = take(2, T)
        best2 = take(TB, SLOTS)
        idx2 = take(TB, SLOTS).bitcast(U32)
        idx2p = take(2 * TB, SLOTS).bitcast(U32)
        idx2f = take(2 * TB, SLOTS)
        pick = take(2048)
        slot = take(TB, 3, SLOTS)
        gsum = take(TB, PEER_HEADS)

        def vcol(name, i=0, n=1):
            return vec[:, _V[name][0] + i:_V[name][0] + i + n]

        def vall(name):
            return vec[:, _V[name][0]:_V[name][1]]

        def con(name):
            return const[:, _C[name][0]:_C[name][1]]

        ssq = stat[:, 0:12]
        rms = stat[:, 12:24]
        rstd = stat[:, 24:36]
        nmax = stat[:, 36:44]
        lsum = stat[:, 44:100]
        eps = stat[:, 100:101]
        one = stat[:, 101:102]
        cmax = stat[:, 104:120]
        coef = stat[:, 120:136]
        rl = stat[:, 136:152]
        KINDS = {"cmp": 0, "slc": 16, "win": 32, "dsa": 0, "mem": 16}
        hstat = [zabs[:, 0, 0:48], zabs[:, 0, 48:96], zabs[:, 0, 96:144]]

        banks = [ctx.enter_context(nc.psum_tensor(f"bank{i}", [P, 512], F32)) for i in range(8)]

        full = [sem(f"bank{i}_full") for i in range(8)]
        drained = [sem(f"bank{i}_drained") for i in range(8)]
        loaded = [sem(f"slot{i}_loaded") for i in range(RING)]
        w_used = sem("w_used")
        s_small = sem("small_loaded")
        s_x = sem("x_loaded")
        s_mem = sem("mem_loaded")
        s_const = sem("const_ready")
        s_ssq = sem("norm_root")
        s_xn = sem("norm_rows")
        s_mkn = sem("mem_keys_normed")
        s_mksq = sem("mem_keys_root")
        s_gain = sem("gains_ready")
        s_trig = sem("trig_args")
        s_sin = sem("trig_ready")
        s_rot = sem("rotated")
        s_vblk = sem("cmp_values")
        s_sc = sem("cmp_scores")
        s_pc = sem("cmp_exp")
        s_pcz = sem("cmp_probs")
        s_pv = sem("values_copied")
        s_maskd = sem("dsa_mask")
        s_sig = sem("gate_sigmoid")
        s_nmax = sem("row_max")
        s_probT = sem("probT_ready")
        s_pvd = sem("unit_done")
        s_o = sem("heads_summed")
        s_y = sem("rows_out")
        s_ggf = sem("post_gain")
        s_x1 = sem("residual")
        s_up = sem("up_relu")
        s_upsq = sem("up_squared")
        s_lb1 = sem("lb_max")
        s_lb2 = sem("lb_exp")
        s_hq1 = sem("hgq_copied")
        s_hsg = sem("hg_sigmoids")
        s_hf = sem("hg_forget")
        s_hlog = sem("hg_log")
        s_harg = sem("hg_arg")
        s_hexp = sem("hg_decay")
        s_hqe = sem("hg_operands")
        s_hsc = sem("hg_scores")
        s_zln = sem("z_log")
        s_zsp = sem("z_softplus")
        s_sbd = sem("stick_done")
        s_hsq = sem("head_sumsq")
        s_hrt = sem("head_root")
        s_mix = sem("mixed_ready")
        s_mqs = sem("mem_q_normed")
        s_gsig = sem("hg_gate_sig")
        s_slot = sem("slots_ready")
        s_gexp = sem("gate_args")
        s_gex2 = sem("gate_exp")
        s_oh = sem("onehots_ready")
        s_gfull = sem("gate_tokens_full")
        s_gdr = sem("gate_tokens_drained")
        s_sfull = sem("expert_scores_full")
        s_gelu = sem("expert_gelu")
        s_w = sem("expert_weights")
        s_vused = sem("v_used")
        s_res = sem("result_ready")
        s_out = sem("result_stored")
        v_step = sem("vector_step")
        a_step = sem("scalar_step")
        p_step = sem("gpsimd_step")

        block = ctx.enter_context(nc.Block())

        def tokens(tb):
            return slice(tb * P, (tb + 1) * P)

        def wait_full(eng, name):
            bank, use = PLAN[name]
            eng.wait_ge(full[bank], use)
            return banks[bank]

        def free(ins, name):
            ins.then_inc(drained[PLAN[name][0]], 1)

        def wait_read(eng, name):
            bank, use = PLAN[name]
            eng.wait_ge(drained[bank], use)

        def tile(name):
            n = TILE_AT[name]
            return ring[:, n % RING, :]

        def km(name, n=512):
            return tile(name).rearrange("p (k n) -> p k n", n=n)

        NORMS = ["mem", "h1", "post1", "h2", "post2", "h3", "h4"]

        @block.sync
        def _(sp):
            sp.dma_start(x[:, :, :], x_in.rearrange("(b p) d -> p b d", p=P)).then_inc(s_x, 16)
            for n in range(RING):
                sp.dma_start(ring[:, n, :], w_in[n]).then_inc(loaded[n], 16)
            rounds = N_TILES // RING
            with sp.Fori(1, rounds, 1) as r:
                for n in range(RING):
                    sp.wait_ge(w_used, (r - 1) * RING + n + 1)
                    sp.dma_start(ring[:, n, :], w_in[bass.ds(r * RING + n, 1)].rearrange("o p n -> p (o n)")
                                 ).then_inc(loaded[n], 16)
            for n in range(rounds * RING, N_TILES):
                sp.wait_ge(w_used, n - RING + 1)
                sp.dma_start(ring[:, n % RING, :], w_in[n]).then_inc(loaded[n % RING], 16)

            def expert_tiles(p, turn, waits):
                for src, which, used in ((u_in, 0, s_sfull), (v_in, 1, s_vused)):
                    n = N_TILES + 2 * turn + which
                    if waits:
                        sp.wait_ge(used, p - 2)
                    else:
                        sp.wait_ge(w_used, min(n - RING + 1, N_TILES))
                    piece = src[p] if isinstance(p, int) else \
                        src[bass.ds(p, 1)].rearrange("o p n -> p (o n)")
                    sp.dma_start(ring[:, n % RING, :], piece).then_inc(loaded[n % RING], 16)

            for p in range(3):
                expert_tiles(p, p, False)
            with sp.Fori(1, N_PAIRS // 3, 1) as r:
                for turn in range(3):
                    expert_tiles(r * 3 + turn, turn, True)
            expert_tiles(N_PAIRS - 1, (N_PAIRS - 1) % 3, True)
            sp.wait_ge(s_res, 4)
            sp.dma_start(out.rearrange("(b p) d -> p b d", p=P), x[:, :, :]).then_inc(s_out, 16)
            sp.wait_ge(s_out, 16)

        @block.gpsimd
        def _(pool):
            pool.dma_start(tmp[:, :, :], mem_in.rearrange("(b p) d -> p b d", p=P)).then_inc(s_mem, 16)
            pool.dma_start(ident[:, :], ident_in[:, 0:P]).then_inc(s_small, 16)
            pool.dma_start(iota[:, :], ident_in[:, P:2 * P]).then_inc(s_small, 16)
            pool.dma_start(vec, vec_in).then_inc(s_small, 16)
            pool.dma_start(const, const_in).then_inc(s_small, 16)
            pool.dma_start(posi, pos_in).then_inc(s_small, 16)

        SMALL = 5 * 16

        @block.tensor
        def _(pe):
            order = iter(PLAN)

            def begin(name):
                assert next(order) == name, name
                bank, use = PLAN[name]
                if use > 1:
                    pe.wait_ge(drained[bank], use - 1)
                return banks[bank]

            def end(ins, name):
                ins.then_inc(full[PLAN[name][0]], 1)

            def arrived(*names):
                for name in names:
                    n = TILE_AT[name]
                    pe.wait_ge(loaded[n % RING], 16 * (n // RING + 1))

            def mm(out_, lhsT, rhs, start=True, stop=True):
                return nc.tensor.matmul(out_, lhsT, rhs, start=start, stop=stop)

            def both_halves(ps, cols, head):
                mm(ps[0:HD, cols], head, ident[:, :])
                return mm(ps[HD:P, cols], head, ident[:, :])

            def rows_to_features(what, src):
                for q in range(4):
                    ps = begin((what, q))
                    for kk in range(2):
                        for tb in range(TB):
                            k = 2 * q + kk
                            last = nc.tensor.transpose(ps[:, kk * T + tb * P:kk * T + (tb + 1) * P],
                                                       src[:, tb, k * P:(k + 1) * P], ident[:, :])
                    end(last, (what, q))

            def wait_hT(what):
                for q in range(4):
                    wait_read(pe, (what, q))

            def project_rows(what, group, n, width=512):
                out_ = [begin((group, n, tb)) for tb in range(TB)]
                for half in range(2):
                    arrived((what, n, half))
                    w = km((what, n, half))
                    for tb in range(TB):
                        for kk in range(4):
                            k = 4 * half + kk
                            last = mm(out_[tb][:, 0:width], hT[:, k, tokens(tb)], w[:, kk, 0:width],
                                      start=(k == 0), stop=(k == KD - 1))
                        if half == 1:
                            end(last, (group, n, tb))
                    if half == 0:
                        last.then_inc(w_used, 1)
                    else:
                        pe.drain().then_inc(w_used, 1)

            def project_features(what, n, groups):
                arrived((what, n, 0), (what, n, 1))
                w = [km((what, n, half)) for half in range(2)]
                for g in range(2):
                    ps = begin(groups[g])
                    for s in range(2):
                        c = (2 * g + s) * P
                        for k in range(KD):
                            last = mm(ps[:, s * T:(s + 1) * T], w[k // 4][:, k % 4, c:c + P],
                                      hT[:, k, :], start=(k == 0), stop=(k == KD - 1))
                    end(last, groups[g])
                pe.drain().then_inc(w_used, 2)

            def modulation(first, count):
                ps = begin(("ada", 0 if first == 0 else 1))
                for n in range(first, first + count):
                    arrived(("ada", n, 0), ("ada", n, 1))
                    w = [km(("ada", n, half)) for half in range(2)]
                    for s in range(4):
                        for k in range(KD):
                            last = mm(ps[:, 4 * n + s:4 * n + s + 1], w[k // 4][:, k % 4, s * P:(s + 1) * P],
                                      vcol("c", k), start=(k == 0), stop=(k == KD - 1))
                    if n < first + count - 1:
                        pe.drain().then_inc(w_used, 2)
                end(last, ("ada", 0 if first == 0 else 1))
                pe.drain().then_inc(w_used, 2)

            def attention(units, operands, v_of, cols, mask):
                n = len(units)

                def scores(i):
                    ps = begin(("S", *units[i]))
                    for tb in range(TB):
                        q, k = operands(units[i], tb)
                        a, b = cols[tb]
                        m = mask(units[i], tb)
                        last = mm(ps[:, a:b], q, k, stop=(m is None))
                        if m is not None:
                            lo, mat = m
                            last = mm(ps[:, a + lo:b], identb, mat, start=False)
                    end(last, ("S", *units[i]))

                def turn(i):
                    wait_read(pe, ("S", *units[i]))
                    ps = begin(("PT", *units[i]))
                    for c in range(cols[1][1] // P):
                        last = nc.tensor.transpose(ps[:, c * P:(c + 1) * P],
                                                   prob[:, i % 2, c * P:(c + 1) * P], ident[:, :])
                    end(last, ("PT", *units[i]))

                def values(i):
                    kind, h = units[i]
                    if h == 0:
                        for tb in range(TB):
                            begin(("O", kind, tb))
                    wait_read(pe, ("PT", kind, h))
                    for tb in range(TB):
                        ps = banks[PLAN[("O", kind, tb)][0]]
                        a, b = cols[tb]
                        for c in range(a // P, b // P):
                            last = mm(ps[:, h * HD:(h + 1) * HD], probT[:, i % 2, c * P:(c + 1) * P],
                                      v_of(units[i], c - a // P), start=(c == a // P), stop=(c == b // P - 1))
                        if i + 1 == n or units[i + 1][0] != kind:
                            end(last, ("O", kind, tb))
                    pe.drain().then_inc(s_pvd, 1)

                base = 0 if units is UNITS1 else len(UNITS1)
                for i in range(n + 2):
                    if i < n:
                        scores(i)
                    if 1 <= i <= n:
                        turn(i - 1)
                    if i >= 2:
                        values(i - 2)

            pe.wait_ge(s_small, SMALL)
            pe.wait_ge(s_const, 1)
            pe.wait_ge(s_xn, 1)
            rows_to_features("memT", tmp)
            wait_hT("memT")
            out_ = [begin(("mkv", tb)) for tb in range(TB)]
            for half in range(2):
                arrived(("mem_kv", 0, half))
                for tb in range(TB):
                    for kk in range(4):
                        k = 4 * half + kk
                        last = mm(out_[tb][:, :], hT[:, k, tokens(tb)], km(("mem_kv", 0, half))[:, kk, :],
                                  start=(k == 0), stop=(k == KD - 1))
                    if half == 1:
                        end(last, ("mkv", tb))
            pe.drain().then_inc(w_used, 2)
            pe.wait_ge(s_mkn, 1)
            ps = begin(("mkT",))
            for pr in range(2):
                for tb in range(TB):
                    last = nc.tensor.transpose(ps[:, pr * T + tb * P:pr * T + (tb + 1) * P],
                                               mkv[:, tb, pr * P:(pr + 1) * P], ident[:, :])
            end(last, ("mkT",))

            modulation(0, 4)
            pe.wait_ge(s_xn, 2)
            rows_to_features("h1T", tmp)
            wait_hT("h1T")
            for n in range(5):
                project_rows("in", "in", n, 512 if n < 4 else 220)
            pe.wait_ge(s_rot, 1)
            for n in range(7):
                ps = begin(("pairT", n))
                for s in range(2):
                    pair = 2 * n + s
                    for tb in range(TB):
                        cols = slice(s * T + tb * P, s * T + (tb + 1) * P)
                        if pair < PAIR_KD:
                            first = 2 * pair if pair < PAIR_KS else 2 * pair + 2
                            last = nc.tensor.transpose(ps[:, cols], rot[:, tb, first * HD:(first + 2) * HD],
                                                       ident[:, :])
                        else:
                            r = ROT_KD if pair == PAIR_KD else ROT_KI
                            last = both_halves(ps, cols, rot[:, tb, r * HD:(r + 1) * HD])
                end(last, ("pairT", n))
            pe.wait_ge(s_pv, 4)
            for which, src, first in (("kcT", rot, ROT_KC * HD), ("vcT", plain, PL_VC)):
                ps = begin((which,))
                for g in range(2):
                    for tb in range(TB):
                        a = first + g * HD
                        last = both_halves(ps, slice(g * T + tb * P, g * T + (tb + 1) * P), src[:, tb, a:a + HD])
                end(last, (which,))
            for which in range(2):
                arrived(("cmp1", which, 0))
                wait_read(pe, (("kcT",), ("vcT",))[which])
                w1 = km(("cmp1", which, 0), P)
                ps = begin(("cmp", which))
                for m in range(16):
                    last = mm(ps[:, 0:45], w1[:, m, :], kvT[which][:, :, 2 * m:2 * m + 225:16],
                              start=(m == 0), stop=(m == 15))
                end(last, ("cmp", which))
            pe.drain().then_inc(w_used, 2)
            wait_read(pe, ("cmp", 0))
            ps = begin(("kcmp",))
            for g in range(2):
                last = mm(ps[g * HD:(g + 1) * HD, 0:N_CMP], vall("w2k"), hidk[:, g, 0:N_CMP])
            end(last, ("kcmp",))
            wait_read(pe, ("cmp", 1))
            ps = begin(("vblk",))
            end(mm(ps[:, 0:HD], hidv.rearrange("p h n -> p (h n)"), vall("w2v")), ("vblk",))
            wait_read(pe, ("kcmp",))
            for n in range(7):
                wait_read(pe, ("pairT", n))
            for g in range(2):
                ps = begin(("Sc", g))
                rows = slice(g * HD, (g + 1) * HD)
                for tb in range(TB):
                    for r in range(4):
                        c = (tb * 4 + r) * 16
                        last = mm(ps[:, c:c + N_CMP], pairT[rows, PAIR_QN + r, tokens(tb)], kcmpT[rows, 0:N_CMP])
                end(last, ("Sc", g))
            for n in range(4):
                tb, odd = n // 2, n % 2
                width = (tb + 1) * P
                ps = begin(("L", n))
                rows = slice(odd * HD, (odd + 1) * HD)
                for i in range(2):
                    last = mm(ps[:, i * width:(i + 1) * width], pairT[rows, PAIR_QI + i, tokens(tb)],
                              pairT[rows, PAIR_KI, 0:width])
                end(last, ("L", n))
            modulation(4, 8)
            pe.wait_ge(s_pcz, 1)
            ps = begin(("pcT",))
            for tb in range(TB):
                last = nc.tensor.transpose(ps[:, tb * P:(tb + 1) * P],
                                           sc[:, tb * HEADS:(tb + 1) * HEADS, :].rearrange("p h n -> p (h n)"),
                                           ident[:, :])
            end(last, ("pcT",))
            wait_read(pe, ("pcT",))
            pe.wait_ge(s_vblk, 1)
            for tb in range(TB):
                ps = begin(("Oc", tb))
                end(mm(ps[:, :], pcT[:, tb, :], vblk.rearrange("p h d -> p (h d)")), ("Oc", tb))

            def operands1(unit, tb):
                kind, h = unit
                if kind == "dsa":
                    rows, q, k = slice((h % 2) * HD, (h % 2 + 1) * HD), PAIR_QD + h // 2, PAIR_KD
                else:
                    g, r = h // 4, h % 4
                    rows, q = slice(g * HD, (g + 1) * HD), PAIR_QN + r
                    k = PAIR_KS if kind == "slc" else PAIR_KW
                return pairT[rows, q, tokens(tb)], pairT[rows, k, 0:(tb + 1) * P]

            def values1(unit, c):
                kind, h = unit
                a = {"slc": PL_VS + (h // 4) * HD, "win": PL_VW + (h // 4) * HD, "dsa": PL_VD}[kind]
                return plain[:, c, a:a + HD]

            def mask1(unit, tb):
                if unit == ("dsa", 0):
                    pe.wait_ge(s_maskd, tb + 1)
                if unit[0] == "dsa":
                    return 0, maskd[:, tb, 0:(tb + 1) * P]
                return tb * P, causalb

            attention(UNITS1, operands1, values1, [(0, P), (P, P + T)], mask1)
            pe.wait_ge(s_o, 1)
            rows_to_features("oT", osum)
            wait_hT("oT")
            for n in range(2):
                project_rows("out", "out", n)
            pe.wait_ge(s_ggf, 1)
            for n in range(4):
                ps = begin(("gg", n))
                for k in range(4):
                    last = mm(ps[:, k * P:(k + 1) * P],
                              gg[:, 4 * n + k:4 * n + k + 1].to_broadcast([P, P]), ident[:, :])
                end(last, ("gg", n))
            pe.wait_ge(s_xn, 3)
            rows_to_features("h2T", tmp)
            wait_hT("h2T")
            for n in range(8):
                project_features("up", n, [("up", 2 * n), ("up", 2 * n + 1)])
            out_ = {}
            for tb in range(TB):
                for n in range(2):
                    out_[n, tb] = begin(("down", n, tb))
            for kg in range(8):
                pe.wait_ge(s_upsq, 2 * kg + 2)
                for n in range(2):
                    arrived(("down", kg, n))
                    for tb in range(TB):
                        for kk in range(4):
                            k = 4 * kg + kk
                            last = mm(out_[n, tb][:, :], upT[:, k, tokens(tb)], km(("down", kg, n))[:, kk, :],
                                      start=(k == 0), stop=(k == D_FF // P - 1))
                        if kg == 7:
                            end(last, ("down", n, tb))
                    pe.drain().then_inc(w_used, 1)

            pe.wait_ge(s_xn, 4)
            rows_to_features("h3T", tmp)
            wait_hT("h3T")
            project_features("in2", 0, [("sbq", 0), ("sbq", 1)])
            project_features("in2", 1, [("sbk", 0), ("sbk", 1)])

            def rows2(n, group):
                out_ = [begin((group, tb)) for tb in range(TB)]
                arrived(("in2", n, 0), ("in2", n, 1))
                for tb in range(TB):
                    for k in range(KD):
                        last = mm(out_[tb][:, :], hT[:, k, tokens(tb)], km(("in2", n, k // 4))[:, k % 4, :],
                                  start=(k == 0), stop=(k == KD - 1))
                    end(last, (group, tb))
                pe.drain().then_inc(w_used, 2)

            rows2(2, "sbv")
            project_features("in2", 3, [("hgq", 0), ("hgq", 1)])
            project_features("in2", 4, [("hgf", 0), ("hgf", 1)])
            rows2(5, "hig")
            arrived(("in2m", 0, 0))
            for tb in range(TB):
                ps = begin(("mq", tb))
                for k in range(KD):
                    last = mm(ps[:, 0:T], hT[:, k, tokens(tb)], km(("in2m", 0, 0), T)[:, k, :],
                              start=(k == 0), stop=(k == KD - 1))
                end(last, ("mq", tb))
            pe.drain().then_inc(w_used, 1)
            pe.wait_ge(s_mqs, 1)
            ps = begin(("mqT",))
            for pr in range(2):
                for tb in range(TB):
                    last = nc.tensor.transpose(ps[:, pr * T + tb * P:pr * T + (tb + 1) * P],
                                               mqn[:, tb, pr * P:(pr + 1) * P], ident[:, :])
            end(last, ("mqT",))
            for name in (("sbq", 0), ("sbq", 1), ("sbk", 0), ("sbk", 1), ("sbv", 0), ("sbv", 1)):
                wait_read(pe, name)
            for i in range(HEADS + 2):
                if i < HEADS:
                    rows, pr = slice((i % 2) * HD, (i % 2 + 1) * HD), i // 2
                    ps = begin(("z", i))
                    mm(ps[:, 0:T], sbkT[rows, pr, 0:P], sbqT[rows, pr, :])
                    end(mm(ps[:, T:T + P], sbkT[rows, pr, P:T], sbqT[rows, pr, P:T]), ("z", i))
                if 1 <= i <= HEADS:
                    h = i - 1
                    rows, pr = slice((h % 2) * HD, (h % 2 + 1) * HD), h // 2
                    ps = begin(("ca", h))
                    pe.wait_ge(s_zsp, h + 1)
                    L = zsp[:, h % 2, :]
                    mm(ps[:, 0:P], sbkT[rows, pr, 0:P], sbqT[rows, pr, 0:P], stop=False)
                    mm(ps[:, 0:P], con("tri"), L[:, 0:P], start=False, stop=False)
                    mm(ps[:, 0:P], identb, strictb, start=False)
                    mm(ps[:, P:T], sbkT[rows, pr, 0:P], sbqT[rows, pr, P:T], stop=False)
                    mm(ps[:, P:T], con("tri"), L[:, P:T], start=False, stop=False)
                    mm(ps[:, P:T], negones, L[:, T:T + P], start=False)
                    mm(ps[:, T:T + P], sbkT[rows, pr, P:T], sbqT[rows, pr, P:T], stop=False)
                    mm(ps[:, T:T + P], con("tri"), L[:, T:T + P], start=False, stop=False)
                    end(mm(ps[:, T:T + P], identb, strictb, start=False), ("ca", h))
                if i >= 2:
                    h = i - 2
                    if h == 0:
                        so = [begin(("sbo", tb)) for tb in range(TB)]
                    wait_read(pe, ("ca", h))
                    col = slice(h * HD, (h + 1) * HD)
                    a = aT[:, h % 2, :]
                    m0 = mm(so[0][:, col], a[:, 0:P], sbv[:, 0, col])
                    mm(so[1][:, col], a[:, P:T], sbv[:, 0, col], stop=False)
                    m1 = mm(so[1][:, col], a[:, T:T + P], sbv[:, 1, col], start=False)
                    if h == HEADS - 1:
                        end(m0, ("sbo", 0))
                        end(m1, ("sbo", 1))
                    pe.drain().then_inc(s_sbd, 1)
            for lv in range(9):
                pe.wait_ge(s_hqe, lv + 1)
                q = hqe[:, lv % 2, :].rearrange("p (h t) -> p h t", h=HG_HEADS)
                k = hke[:, lv % 2, :].rearrange("p (h t) -> p h t", h=HG_HEADS)
                if lv < 8:
                    for tb in range(TB):
                        ps = begin(("hg", lv, tb))
                        for h in range(HG_HEADS):
                            last = mm(ps[:, h * P:(h + 1) * P], k[:, h, tokens(tb)], q[:, h, tokens(tb)])
                        end(last, ("hg", lv, tb))
                else:
                    ps = begin(("hgx",))
                    for h in range(HG_HEADS):
                        last = mm(ps[:, h * P:(h + 1) * P], k[:, h, 0:P], q[:, h, P:T])
                    end(last, ("hgx",))
            pe.wait_ge(s_hsc, 1)
            wait_read(pe, ("hig", 0))
            wait_read(pe, ("hig", 1))
            for tb in range(TB):
                ps = begin(("hgo", tb))
                for h in range(HG_HEADS):
                    col = slice(h * HD, (h + 1) * HD)
                    last = mm(ps[:, col], hacc[:, tb, h * P:(h + 1) * P], hig[:, tb, col], stop=(tb == 0))
                    if tb == 1:
                        last = mm(ps[:, col], hx[:, h * P:(h + 1) * P], hig[:, 0, col], start=False)
                end(last, ("hgo", tb))
            wait_read(pe, ("mqT",))
            wait_read(pe, ("mkT",))

            def operands2(unit, tb):
                h = unit[1]
                rows = slice((h % 2) * HD, (h % 2 + 1) * HD)
                return mqT[rows, h // 2, tokens(tb)], mkT[rows, h // 2, :]

            attention(UNITS2, operands2, lambda unit, c: mkv[:, c, T + unit[1] * HD:T + (unit[1] + 1) * HD],
                      [(0, T), (T, 2 * T)], lambda unit, tb: None)
            pe.wait_ge(s_mix, 1)
            rows_to_features("mixT", osum)
            wait_hT("mixT")
            for n in range(2):
                project_rows("out2", "out2", n)
            pe.wait_ge(s_xn, 5)
            rows_to_features("h4T", tmp)
            wait_hT("h4T")
            for n in range(4):
                project_features("wq", n, [("wq", 2 * n), ("wq", 2 * n + 1)])
            arrived(("keys", 0, 0))
            for n in range(8):
                wait_read(pe, ("wq", n))
            keysT = km(("keys", 0, 0), N_KEYS)
            for tb in range(TB):
                for q in range(4):
                    ps = begin(("keys", 4 * tb + q))
                    for i in range(4):
                        hc = 4 * q + i
                        last = mm(ps[:, i * P:(i + 1) * P], pqT[:, hc, tokens(tb)], keysT[:, hc, :])
                    end(last, ("keys", 4 * tb + q))
            pe.drain().then_inc(w_used, 1)
            pe.wait_ge(s_slot, 1)
            ps = begin(("idT", 0))
            for r in range(2):
                for tb in range(TB):
                    last = nc.tensor.transpose(ps[:, r * T + tb * P:r * T + (tb + 1) * P],
                                               slot[:, tb, r, :], ident[:, :])
            end(last, ("idT", 0))
            ps = begin(("idT", 1))
            for tb in range(TB):
                last = nc.tensor.transpose(ps[:, tb * P:(tb + 1) * P], slot[:, tb, 2, :], ident[:, :])
            end(last, ("idT", 1))
            for b in range(8):
                pe.wait_ge(drained[b], USED[b])

            def gate_tokens(it, waits):
                for half in range(2):
                    pe.wait_ge(s_oh, it * 2 + half + 1)
                    if waits:
                        pe.wait_ge(s_gdr, it * 2 + half - 1)
                    for i in range(4):
                        last = mm(banks[half][:, i * P:(i + 1) * P], onehot[:, 0, 4 * half + i, :],
                                  onehot[:, 1, 4 * half + i, :])
                    last.then_inc(s_gfull, 1)

            gate_tokens(0, False)
            with pe.Fori(1, T // 8, 1) as it:
                gate_tokens(it, True)

            def slot_of(turn, which):
                return (N_TILES + 2 * turn + which) % RING

            def times_loaded(turn, which):
                return (N_TILES + 2 * turn + which) // RING

            def expert_scores(r, turn, first=False):
                n = slot_of(turn, 0)
                later = 1 if turn == 0 and not first else 0
                pe.wait_ge(loaded[n], r * 16 + 16 * (times_loaded(turn, 0) + later + 1))
                u = ring[:, n, :].rearrange("p (j k i) -> p j k i", j=2, k=KD)
                for jj in range(2):
                    for k in range(KD):
                        last = mm(banks[turn][:, jj * T:(jj + 1) * T], u[:, jj, k, :], hT[:, k, :],
                                  start=(k == 0), stop=(k == KD - 1))
                last.then_inc(s_sfull, 1)

            acc = {(tb, c): banks[4 + 2 * tb + c] for tb in range(TB) for c in range(2)}

            def expert_values(r, turn, first=False, stop=False):
                n = slot_of(turn, 1)
                pe.wait_ge(s_w, r * 3 + turn + 1)
                pe.wait_ge(loaded[n], r * 16 + 16 * (times_loaded(turn, 1) + 1))
                v = ring[:, n, :].rearrange("p (j d) -> p j d", j=2)
                w = mixw[:, turn * 512:(turn + 1) * 512].rearrange("p (j t) -> p j t", j=2)
                for jj in range(2):
                    for tb in range(TB):
                        for c in range(2):
                            last = nc.tensor.matmul(acc[tb, c][:, :], w[:, jj, tokens(tb)],
                                                    v[:, jj, c * 512:(c + 1) * 512],
                                                    start=first and jj == 0, stop=stop and jj == 1,
                                                    skip_group_check=True)
                last.then_inc(s_vused, 1)

            pe.wait_ge(s_gdr, T // 4)
            expert_scores(0, 0, first=True)

            def expert_round(r, first=False):
                for turn in range(3):
                    expert_scores(r, (turn + 1) % 3)
                    expert_values(r, turn, first=first and turn == 0)

            expert_round(0, first=True)
            with pe.Fori(1, N_PAIRS // 3, 1) as r:
                expert_round(r)
            expert_values(N_PAIRS // 3, 0, stop=True)

        @block.scalar
        def _(act):
            steps = [0]

            def link(ins):
                steps[0] += 1
                ins.then_inc(a_step, 1)
                act.wait_ge(a_step, steps[0])

            def root(i, src):
                for tb in range(TB):
                    link(nc.scalar.activation(junk, src[:, tb, :], ACT.Square,
                                              accum_out=ssq[:, 2 * i + tb:2 * i + tb + 1]))
                nc.scalar.activation(rms[:, 2 * i:2 * i + 2], ssq[:, 2 * i:2 * i + 2], ACT.Sqrt,
                                     bias=eps, scale=1.0 / D).then_inc(s_ssq, 1)

            def features_out(what, gain, bias=None, plain_from=KD):
                for q in (0, 2):
                    ps = wait_full(act, (what, q))
                    for kk in range(2):
                        k = 2 * q + kk
                        src = ps[:, kk * T:(kk + 1) * T]
                        if gain is None or k >= plain_from:
                            ins = nc.scalar.copy(hT[:, k, :], src)
                        elif bias is None:
                            ins = nc.scalar.activation(hT[:, k, :], src, ACT.Copy, scale=gain[:, k:k + 1])
                        else:
                            ins = nc.scalar.activation(hT[:, k, :], src, ACT.Identity,
                                                       scale=gain[:, k:k + 1], bias=bias[:, k:k + 1])
                    free(ins, (what, q))

            def attention(units, l_col, cols):
                base = 0 if units is UNITS1 else len(UNITS1)
                for i, unit in enumerate(units):
                    ps = wait_full(act, ("S", *unit))
                    act.wait_ge(s_nmax, base + i + 1)
                    if i >= 2:
                        wait_full(act, ("PT", *units[i - 2]))
                    for tb in range(TB):
                        a, b = cols[tb]
                        c = l_col(unit, tb)
                        ins = nc.scalar.activation(
                            prob[:, i % 2, a:b], ps[:, a:b], ACT.Exp,
                            bias=nmax[:, 2 * (i % 4) + tb:2 * (i % 4) + tb + 1],
                            accum_out=lsum[:, c:c + 1])
                    free(ins, ("S", *unit))

            act.wait_ge(s_const, 1)
            act.wait_ge(s_mem, 16)
            root(0, tmp)
            act.wait_ge(s_x, 16)
            act.wait_ge(s_ssq, 1)
            root(1, x)
            features_out("memT", vall("memg"))
            for tb in range(TB):
                ps = wait_full(act, ("mkv", tb))
                free(nc.scalar.copy(mkv[:, tb, :], ps[:, :]), ("mkv", tb))
            act.wait_ge(s_mksq, 1)
            nc.scalar.activation(stat[:, 104:112], stat[:, 104:112], ACT.Sqrt, bias=eps,
                                 scale=1.0 / HD).then_inc(s_hrt, 1)
            ps = wait_full(act, ("mkT",))
            free(nc.scalar.activation(mkT.rearrange("p a t -> p (a t)"), ps[:, :], ACT.Copy,
                                      scale=vcol("kg")), ("mkT",))
            act.wait_ge(s_trig, 1)
            for src, dst, scale in ((trig[:, 3, :], sind[:, :, 32:64], 1.0), (trig[:, 3, :], sind[:, :, 0:32], -1.0),
                                    (trig[:, 5, :], cosd[:, :, 0:32], 1.0), (trig[:, 5, :], cosd[:, :, 32:64], 1.0)):
                nc.scalar.activation(dst, src.rearrange("p (b f) -> p b f", b=TB), ACT.Sin,
                                     scale=scale).then_inc(s_sin, 1)
            act.wait_ge(s_gain, 1)
            features_out("h1T", gain1, mod[:, 0:KD])
            for tb in range(TB):
                ps = wait_full(act, ("in", 3, tb))
                nc.scalar.copy(plain[:, tb, 0:256], ps[:, 256:512]).then_inc(s_pv, 1)
            for tb in range(TB):
                ps = wait_full(act, ("in", 4, tb))
                ins = nc.scalar.copy(plain[:, tb, 256:476], ps[:, 0:220])
                ins.then_inc(s_pv, 1)
                act.wait_ge(s_pv, 3 + tb)
                free(nc.scalar.activation(sig[:, tb, :], plain[:, tb, PL_GL:PL_WI], ACT.Sigmoid), ("in", 4, tb))
            for n in range(7):
                ps = wait_full(act, ("pairT", n))
                dst = pairT[:, 2 * n:2 * n + 2, :].rearrange("p a t -> p (a t)")
                if 2 * n < PAIR_QI:
                    ins = nc.scalar.mul(dst, ps[:, :], SCALE)
                else:
                    ins = nc.scalar.copy(dst, ps[:, :])
                free(ins, ("pairT", n))
            for which in range(2):
                ps = wait_full(act, ("cmp", which))
                link(nc.scalar.copy(hbias[:, which:which + 1], ps[:, 30:31]))
                for g in range(2):
                    src = ps[:, g * N_CMP:(g + 1) * N_CMP]
                    if which == 0:
                        dst = hidk[:, g, 0:N_CMP]
                    else:
                        dst = hidv[:, 4 * g:4 * g + 4, 0:N_CMP]
                        src = src.unsqueeze(1).to_broadcast([P, 4, N_CMP])
                    ins = nc.scalar.activation(dst, src, ACT.Gelu_apprx_tanh, bias=hbias[:, which:which + 1])
                free(ins, ("cmp", which))
            ps = wait_full(act, ("kcmp",))
            free(nc.scalar.copy(kcmpT[:, 0:N_CMP], ps[:, 0:N_CMP]), ("kcmp",))
            act.wait_ge(s_sc, 1)
            nc.scalar.activation(sc[:, :, 0:N_CMP], sc[:, :, 0:N_CMP], ACT.Exp).then_inc(s_pc, 1)
            for n in range(4):
                ps = wait_full(act, ("L", n))
                w = (n // 2 + 1) * T
                free(nc.scalar.activation(relu[:, n, 0:w], ps[:, 0:w], ACT.Relu), ("L", n))
            ps = wait_full(act, ("pcT",))
            free(nc.scalar.copy(pcT.rearrange("p b t -> p (b t)"), ps[:, 0:T]), ("pcT",))
            attention(UNITS1, lambda u, tb: KINDS[u[0]] + tb * HEADS + u[1], [(0, P), (P, P + T)])
            features_out("oT", None)

            def rows_out(what, i):
                for n in range(2):
                    for tb in range(TB):
                        ps = wait_full(act, (what, n, tb))
                        ins = nc.scalar.copy(tmp[:, tb, n * 512:(n + 1) * 512], ps[:, :])
                        free(ins, (what, n, tb))
                for n in range(2):
                    for tb in range(TB):
                        wait_read(act, (what, n, tb))
                root(i, tmp)

            rows_out("out", 2)
            for n in range(4):
                ps = wait_full(act, ("gg", n))
                free(nc.scalar.copy(ggb[:, n // 2, (n % 2) * 512:(n % 2 + 1) * 512], ps[:, :]), ("gg", n))
            act.wait_ge(s_x1, 1)
            root(3, x)
            features_out("h2T", gain2, mod[:, 24:32])
            for n in range(16):
                ps = wait_full(act, ("up", n))
                free(nc.scalar.activation(upT[:, 2 * n:2 * n + 2, :].rearrange("p a t -> p (a t)"),
                                          ps[:, :], ACT.Relu), ("up", n))
            rows_out("down", 4)
            act.wait_ge(s_x1, 2)
            root(5, x)
            features_out("h3T", vall("mix2"))
            for name, dst, scale in (("sbq", sbqT, SCALE), ("sbk", sbkT, 1.0)):
                for n in range(2):
                    ps = wait_full(act, (name, n))
                    free(nc.scalar.mul(dst[:, 2 * n:2 * n + 2, :].rearrange("p a t -> p (a t)"), ps[:, :], scale),
                         (name, n))
            for tb in range(TB):
                ps = wait_full(act, ("sbv", tb))
                free(nc.scalar.copy(sbv[:, tb, :], ps[:, :]), ("sbv", tb))
            for n in range(2):
                ps = wait_full(act, ("hgq", n))
                link(nc.scalar.copy(hq[:, n * 512:(n + 1) * 512], ps[:, :]))
                free(nc.scalar.activation(hsig[:, n * 512:(n + 1) * 512], ps[:, :], ACT.Sigmoid), ("hgq", n))
            for n in range(2):
                ps = wait_full(act, ("hgf", n))
                free(nc.scalar.activation(hf[:, n * 512:(n + 1) * 512], ps[:, :], ACT.Sigmoid), ("hgf", n))
            for tb in range(TB):
                ps = wait_full(act, ("hig", tb))
                free(nc.scalar.copy(hig[:, tb, :], ps[:, :]), ("hig", tb))
            for tb in range(TB):
                wait_read(act, ("hig", tb))
                ins = nc.scalar.activation(tmp[:, tb, 0:256], hig[:, tb, 256:512], ACT.Sigmoid)
            ins.then_inc(s_gsig, 1)
            for tb in range(TB):
                ps = wait_full(act, ("mq", tb))
                free(nc.scalar.copy(mqn[:, tb, :], ps[:, 0:T]), ("mq", tb))
            act.wait_ge(s_mksq, 2)
            nc.scalar.activation(stat[:, 104:112], stat[:, 104:112], ACT.Sqrt, bias=eps,
                                 scale=1.0 / HD).then_inc(s_hrt, 1)
            ps = wait_full(act, ("mqT",))
            free(nc.scalar.activation(mqT.rearrange("p a t -> p (a t)"), ps[:, :], ACT.Copy,
                                      scale=vcol("qg")), ("mqT",))
            act.wait_ge(s_lb1, 1)
            nc.scalar.activation(lb[:, 0:8], lb[:, 0:8], ACT.Exp).then_inc(s_lb2, 1)
            act.wait_ge(s_hf, 1)
            nc.scalar.activation(hb, hf, ACT.Ln).then_inc(s_hlog, 1)
            for i in range(HEADS + 1):
                if i < HEADS:
                    ps = wait_full(act, ("z", i))
                    if i >= 2:
                        act.wait_ge(s_zsp, i - 1)
                    link(nc.scalar.activation(zabs[:, i % 2, :], ps[:, 0:384], ACT.Abs))
                    link(nc.scalar.activation(zexp[:, i % 2, :], zabs[:, i % 2, :], ACT.Exp, scale=-1.0))
                    nc.scalar.activation(zexp[:, i % 2, :], zexp[:, i % 2, :], ACT.Ln, bias=one).then_inc(s_zln, 1)
                if i >= 1:
                    h = i - 1
                    ps = wait_full(act, ("ca", h))
                    if h >= 2:
                        act.wait_ge(s_sbd, h - 1)
                    free(nc.scalar.activation(aT[:, h % 2, :], ps[:, 0:384], ACT.Exp), ("ca", h))
            for lv in range(1, 9):
                act.wait_ge(s_harg, lv)
                nc.scalar.activation(harg, harg, ACT.Exp).then_inc(s_hexp, 1)
            attention(UNITS2, lambda u, tb: KINDS["mem"] + tb * 4 + u[1], [(0, T), (T, 2 * T)])
            act.wait_ge(s_hsq, 1)
            nc.scalar.activation(hstat[1][:, 0:24], hstat[0][:, 0:24], ACT.Sqrt, bias=eps,
                                 scale=1.0 / HD).then_inc(s_hrt, 1)
            features_out("mixT", vall("headg"), plain_from=6)
            act.wait_ge(s_x1, 3)
            root(0, x)
            features_out("h4T", vall("ffn2"))
            for n in range(0, 8, 2):
                ps = wait_full(act, ("wq", n))
                free(nc.scalar.copy(pqT[:, 2 * n:2 * n + 2, :].rearrange("p a t -> p (a t)"), ps[:, :]), ("wq", n))
            act.wait_ge(s_gexp, 1)
            nc.scalar.activation(best2, best2, ACT.Exp).then_inc(s_gex2, 1)
            for n in range(2):
                ps = wait_full(act, ("idT", n))
                if n == 0:
                    dst, src = slotT[:, 0:2, :].rearrange("p r t -> p (r t)"), ps[:, :]
                else:
                    dst, src = slotT[:, 2, :], ps[:, 0:T]
                free(nc.scalar.copy(dst, src), ("idT", n))

            wait_read(act, ("idT", 0))
            wait_read(act, ("idT", 1))

            def gate_tokens(it):
                for half in range(2):
                    act.wait_ge(s_gfull, it * 2 + half + 1)
                    t0 = it * 8 + half * 4
                    nc.scalar.copy(gates[:, bass.ds(t0, 4), :],
                                   banks[half][:, :].rearrange("p (t j) -> p t j", t=4)).then_inc(s_gdr, 1)

            with act.Fori(0, T // 8, 1) as it:
                gate_tokens(it)

            def gelu(p, turn, waits):
                act.wait_ge(s_sfull, p + 1)
                if waits:
                    act.wait_ge(s_vused, p - 2)
                nc.scalar.activation(mixw[:, turn * 512:(turn + 1) * 512], banks[turn][:, :],
                                     ACT.Gelu).then_inc(s_gelu, 1)

            for p in range(3):
                gelu(p, p, False)
            with act.Fori(1, N_PAIRS // 3, 1) as r:
                for turn in range(3):
                    gelu(r * 3 + turn, turn, True)
            gelu(N_PAIRS - 1, 0, True)

        @block.vector
        def _(dve):
            steps = [0]

            def link(ins):
                steps[0] += 1
                ins.then_inc(v_step, 1)
                dve.wait_ge(v_step, steps[0])

            tt = nc.vector.tensor_tensor
            ts = nc.vector.tensor_scalar
            stt = nc.vector.scalar_tensor_tensor

            def normed(i, src, dst=tmp):
                j = i % 6
                dve.wait_ge(s_ssq, i + 1)
                link(nc.vector.reciprocal(rstd[:, 2 * j:2 * j + 2], rms[:, 2 * j:2 * j + 2]))
                for tb in range(TB):
                    ins = ts(dst[:, tb, :], src[:, tb, :], rstd[:, 2 * j + tb:2 * j + tb + 1], None, ALU.mult)
                    if tb == 0:
                        link(ins)
                ins.then_inc(s_xn, 1)

            def features_out(what, gain, bias=None, plain_from=KD):
                for q in (1, 3):
                    ps = wait_full(dve, (what, q))
                    for kk in range(2):
                        k = 2 * q + kk
                        src = ps[:, kk * T:(kk + 1) * T]
                        if gain is None or k >= plain_from:
                            ins = nc.vector.tensor_copy(hT[:, k, :], src)
                        elif bias is None:
                            ins = ts(hT[:, k, :], src, gain[:, k:k + 1], None, ALU.mult)
                        else:
                            ins = ts(hT[:, k, :], src, gain[:, k:k + 1], bias[:, k:k + 1], ALU.mult, ALU.add)
                    free(ins, (what, q))

            def head_norm(src, n_heads, stats):
                sq = junk[:, 0:n_heads * HD].rearrange("p (h d) -> p h d", h=n_heads)
                link(tt(sq, src, src, ALU.mult))
                link(nc.vector.tensor_reduce(stats, sq, AX.X, ALU.add))

            def residual(i, ggrow):
                dve.wait_ge(s_ssq, i + 1)
                j = i % 6
                link(nc.vector.reciprocal(rstd[:, 2 * j:2 * j + 2], rms[:, 2 * j:2 * j + 2]))
                for tb in range(TB):
                    link(stt(tmp[:, tb, :], tmp[:, tb, :], rstd[:, 2 * j + tb:2 * j + tb + 1], ggrow,
                             ALU.mult, ALU.mult))
                    link(tt(x[:, tb, :], x[:, tb, :], tmp[:, tb, :], ALU.add))
                nc.vector.memset(coef[:, 0:1], 0.0).then_inc(s_x1, 1)

            link(nc.vector.memset(eps, EPS))
            link(nc.vector.memset(one, 1.0))
            link(nc.vector.memset(negones, -1.0))
            for w in range(2):
                link(nc.vector.memset(kvT[w], 0.0))
            link(nc.vector.memset(hidv, 0.0))
            link(nc.vector.memset(sc, 0.0))
            dve.wait_ge(s_small, SMALL)
            link(nc.vector.tensor_copy(identb, ident[:, :]))
            link(nc.vector.tensor_copy(causalb, con("causal")))
            link(nc.vector.tensor_copy(strictb, con("strict")))
            for w, name in enumerate(("pe_k", "pe_v")):
                link(nc.vector.tensor_copy(kvT[w][:, 2, 0:32:2], vall(name)))
            link(nc.vector.tensor_copy(posf, posi))
            nc.vector.memset(coef[:, 0:1], 0.0).then_inc(s_const, 1)

            def tr(i):
                return trig[:, i, :]
            for tb in range(TB):
                link(ts(tr(0)[:, tb * 32:(tb + 1) * 32], con("invf"), posf[:, tb:tb + 1], None, ALU.mult))
            link(ts(tr(1), tr(0), 1.0 / (2 * math.pi), ROUND, ALU.mult, ALU.add))
            link(ts(tr(2), tr(1), -ROUND, None, ALU.add))
            link(stt(tr(3), tr(2), -PI2_A, tr(0), ALU.mult, ALU.add))
            link(stt(tr(3), tr(2), -PI2_B, tr(3), ALU.mult, ALU.add))
            link(stt(tr(3), tr(2), -PI2_C, tr(3), ALU.mult, ALU.add))
            link(ts(tr(5), tr(3), math.pi / 2, None, ALU.add))
            link(ts(tr(6), tr(5), math.pi, -2 * math.pi, ALU.is_gt, ALU.mult))
            link(tt(tr(5), tr(5), tr(6), ALU.add))
            link(ts(tr(3), tr(3), PI_IN, -PI_IN, ALU.min, ALU.max))
            ts(tr(5), tr(5), PI_IN, -PI_IN, ALU.min, ALU.max).then_inc(s_trig, 1)

            dve.wait_ge(s_mem, 16)
            normed(0, tmp)
            features_out("memT", vall("memg"))
            for tb in range(TB):
                wait_read(dve, ("mkv", tb))
                head_norm(mkv[:, tb, 0:T].rearrange("p (h d) -> p h d", h=4), 4, stat[:, 104 + 4 * tb:108 + 4 * tb])
            nc.vector.memset(coef[:, 0:1], 0.0).then_inc(s_mksq, 1)
            dve.wait_ge(s_hrt, 1)
            link(nc.vector.reciprocal(stat[:, 112:120], stat[:, 104:112]))
            for tb in range(TB):
                v = mkv[:, tb, 0:T].rearrange("p (h d) -> p h d", h=4)
                ins = tt(v, v, stat[:, 112 + 4 * tb:116 + 4 * tb].unsqueeze(2).to_broadcast([P, 4, HD]), ALU.mult)
                if tb == 0:
                    link(ins)
            ins.then_inc(s_mkn, 1)
            ps = wait_full(dve, ("ada", 0))
            link(tt(mod[:, 0:16], ps[:, 0:16], vcol("b_ada", 0, 16), ALU.add))
            free(stt(gain1, mod[:, 8:16], 1.0, vall("g_pre_mix"), ALU.add, ALU.mult), ("ada", 0))
            wait_read(dve, ("ada", 0))
            nc.vector.memset(coef[:, 0:1], 0.0).then_inc(s_gain, 1)
            wait_full(dve, ("memT", 3))
            normed(1, x)
            features_out("h1T", gain1, mod[:, 0:KD])
            dve.wait_ge(s_sin, 4)
            for n in range(4):
                nh = 8 if n < 3 else 4
                for tb in range(TB):
                    name = ("in", n, tb)
                    ps = wait_full(dve, name)
                    if n == 3:
                        dve.wait_ge(s_pv, tb + 1)
                    src = ps[:, 0:nh * HD].rearrange("p (h d) -> p h d", h=nh)
                    dst = rot[:, tb, n * 512:n * 512 + nh * HD].rearrange("p (h d) -> p h d", h=nh)
                    t2 = rtmp[:, tb, 0:nh * HD].rearrange("p (h d) -> p h d", h=nh)

                    def table(t, a, b):
                        return t[:, tb, a:b].unsqueeze(1).to_broadcast([P, nh, b - a])

                    tt(dst, src, table(cosd, 0, HD), ALU.mult)
                    tt(t2[:, :, 0:32], src[:, :, 32:64], table(sind, 0, 32), ALU.mult)
                    link(tt(t2[:, :, 32:64], src[:, :, 0:32], table(sind, 32, 64), ALU.mult))
                    ins = tt(dst, dst, t2, ALU.add)
                    free(ins, name)
                    wait_read(dve, name)
            nc.vector.memset(coef[:, 0:1], 0.0).then_inc(s_rot, 1)
            for which, name in enumerate((("kcT",), ("vcT",))):
                ps = wait_full(dve, name)
                v = ps[:, :].rearrange("p (g t) -> p g t", g=2)
                nc.vector.tensor_copy(kvT[which][0:HD, 0:2, :], v[0:HD, :, :])
                free(nc.vector.tensor_copy(kvT[which][HD:P, 0:2, 0:T - 1], v[HD:P, :, 1:T]), name)
            ps = wait_full(dve, ("vblk",))
            ins = tt(vblk, ps[:, 0:HD].unsqueeze(1).to_broadcast([P, HEADS, HD]),
                     con("blk").unsqueeze(2).to_broadcast([P, HEADS, HD]), ALU.mult)
            free(ins, ("vblk",))
            wait_read(dve, ("vblk",))
            nc.vector.memset(coef[:, 0:1], 0.0).then_inc(s_vblk, 1)
            sv = sc[:, :, 0:N_CMP]

            def per_block(name):
                return con(name).rearrange("p (b n) -> p b n", b=TB)[:, :, 0:N_CMP]
            for g in range(2):
                ps = wait_full(dve, ("Sc", g))
                for tb in range(TB):
                    hs = slice(tb * HEADS + 4 * g, tb * HEADS + 4 * g + 4)
                    ins = tt(sv[:, hs, :],
                             ps[:, tb * 64:(tb + 1) * 64].rearrange("p (h n) -> p h n", h=4)[:, :, 0:N_CMP],
                             per_block("cmpadd")[:, tb, :].unsqueeze(1).to_broadcast([P, 4, N_CMP]), ALU.add)
                free(ins, ("Sc", g))
                wait_read(dve, ("Sc", g))
            link(nc.vector.tensor_reduce(cmax, sv, AX.X, ALU.max))
            tt(sv, sv, cmax.unsqueeze(2).to_broadcast([P, 16, N_CMP]), ALU.subtract).then_inc(s_sc, 1)
            for tb in range(TB):
                link(ts(wsc[:, tb, :], plain[:, tb, PL_WI:PL_WI + 4], IDX_SCALE, None, ALU.mult))
            for tb in range(TB):
                width = (tb + 1) * P
                wait_read(dve, ("L", 2 * tb))
                wait_read(dve, ("L", 2 * tb + 1))
                for h in range(IDX_HEADS):
                    r = relu[:, 2 * tb + h % 2, (h // 2) * width:(h // 2 + 1) * width]
                    if h == 0:
                        ins = ts(score[:, tb, 0:width], r, wsc[:, tb, h:h + 1], None, ALU.mult)
                    else:
                        ins = stt(score[:, tb, 0:width], r, wsc[:, tb, h:h + 1], score[:, tb, 0:width],
                                  ALU.mult, ALU.add)
                    link(ins)
            dve.wait_ge(s_pc, 1)
            link(nc.vector.tensor_reduce(lsum[:, 0:16], sv, AX.X, ALU.add))
            for tb in range(TB):
                hs = slice(tb * HEADS, (tb + 1) * HEADS)
                ins = tt(sv[:, hs, :], sv[:, hs, :],
                         per_block("cmp01")[:, tb, :].unsqueeze(1).to_broadcast([P, HEADS, N_CMP]), ALU.mult)
            ins.then_inc(s_pcz, 1)
            ps = wait_full(dve, ("ada", 1))
            link(tt(mod[:, 16:48], ps[:, 16:48], vcol("b_ada", 16, 32), ALU.add))
            link(stt(gain2, mod[:, 32:40], 1.0, vall("g_pre_ffn"), ALU.add, ALU.mult))
            link(tt(gg[:, 0:8], mod[:, 16:24], vall("g_post_mix"), ALU.mult))
            free(tt(gg[:, 8:16], mod[:, 40:48], vall("g_post_ffn"), ALU.mult), ("ada", 1))
            wait_read(dve, ("ada", 1))
            nc.vector.memset(coef[:, 0:1], 0.0).then_inc(s_ggf, 1)

            def top_keys():
                for tb in range(TB):
                    width = (tb + 1) * P
                    s, w = score[:, tb, 0:width], work[:, tb, 0:width]
                    link(tt(score[:, tb, tb * P:width], score[:, tb, tb * P:width], con("causal"), ALU.add))
                    for r in range(DSA_K // 8):
                        src = s if r == 0 else w
                        link(nc.vector.max(cmax[:, 0:8], src))
                        link(nc.vector.match_replace(w, cmax[:, 0:8], src, TAKEN))
                    link(ts(w, w, 0.5 * TAKEN, NEG, ALU.is_ge, ALU.mult))
                    if tb:
                        nc.vector.tensor_copy(maskd[:, tb, 0:P], w[:, 0:P])
                    tt(maskd[:, tb, tb * P:width], w[:, tb * P:width], con("causal"), ALU.add).then_inc(s_maskd, 1)

            def weighted(kind, psname, tb, col, add, gated=True):
                ps = wait_full(dve, psname)
                dst = osum[:, tb, col:col + 512].rearrange("p (h d) -> p h d", h=HEADS)
                src = ps[:, :].rearrange("p (h d) -> p h d", h=HEADS)
                c = coef[:, tb * 8:(tb + 1) * 8].unsqueeze(2).to_broadcast([P, HEADS, HD])
                if not add:
                    free(tt(dst, src, c, ALU.mult), psname)
                    wait_read(dve, psname)
                else:
                    t = otmp.rearrange("p (h d) -> p h d", h=HEADS)
                    free(tt(t, src, c, ALU.mult), psname)
                    wait_read(dve, psname)
                    link(tt(dst, dst, t, ALU.add))

            def coefficients(kind, gate):
                a = KINDS[kind]
                link(nc.vector.reciprocal(rl, lsum[:, a:a + 16]))
                if gate is None:
                    link(nc.vector.tensor_copy(coef, rl))
                else:
                    g = sig.rearrange("p b (h c) -> p b h c", c=3)[:, :, :, gate]
                    link(tt(coef.rearrange("p (b h) -> p b h", b=TB), rl.rearrange("p (b h) -> p b h", b=TB), g,
                            ALU.mult))

            def attention(units, cols, after):
                base = 0 if units is UNITS1 else len(UNITS1)
                for i in range(len(units) + 3):
                    if i < len(units):
                        ps = wait_full(dve, ("S", *units[i]))
                        if i >= 4:
                            wait_read(dve, ("S", *units[i - 4]))
                        for tb in range(TB):
                            a, b = cols[tb]
                            ins = nc.vector.tensor_reduce(nmax[:, 2 * (i % 4) + tb:2 * (i % 4) + tb + 1],
                                                          ps[:, a:b], AX.X, ALU.max, negate=True)
                        ins.then_inc(s_nmax, 1)
                    if 1 <= i <= len(units):
                        ps = wait_full(dve, ("PT", *units[i - 1]))
                        if i >= 3:
                            dve.wait_ge(s_pvd, base + i - 2)
                        w = cols[1][1]
                        free(nc.vector.tensor_copy(probT[:, (i - 1) % 2, 0:w], ps[:, 0:w]), ("PT", *units[i - 1]))
                    after(i - 2)

            wait_read(dve, ("in", 4, 0))
            wait_read(dve, ("in", 4, 1))
            coefficients("cmp", 0)
            for tb in range(TB):
                weighted("cmp", ("Oc", tb), tb, 0, False)
            top_keys()

            def after1(i):
                if i in (8, 16):
                    kind = UNITS1[i - 1][0]
                    coefficients(kind, 1 if kind == "slc" else 2)
                    for tb in range(TB):
                        weighted(kind, ("O", kind, tb), tb, 0, True)

            attention(UNITS1, [(0, P), (P, P + T)], after1)
            coefficients("dsa", None)
            for tb in range(TB):
                weighted("dsa", ("O", "dsa", tb), tb, 512, False)
            nc.vector.memset(coef[:, 0:1], 0.0).then_inc(s_o, 1)
            features_out("oT", None)
            for n in range(2):
                wait_read(dve, ("gg", n))
            residual(2, ggb[:, 0, :])
            normed(3, x)
            features_out("h2T", gain2, mod[:, 24:32])
            for n in range(16):
                wait_read(dve, ("up", n))
                v = upT[:, 2 * n:2 * n + 2, :]
                tt(v, v, v, ALU.mult).then_inc(s_upsq, 1)
            for n in range(2, 4):
                wait_read(dve, ("gg", n))
            residual(4, ggb[:, 1, :])
            normed(5, x)
            features_out("h3T", vall("mix2"))
            link(nc.vector.memset(hones, 1.0))
            g0, g1 = vcol("gamma", 0, 4), vcol("gamma", 4, 4)
            link(tt(lb[:, 8:12], g0, g1, ALU.max))
            link(tt(lb[:, 0:4], g0, lb[:, 8:12], ALU.subtract))
            tt(lb[:, 4:8], g1, lb[:, 8:12], ALU.subtract).then_inc(s_lb1, 1)
            for tb in range(TB):
                wait_read(dve, ("mq", tb))
                head_norm(mqn[:, tb, :].rearrange("p (h d) -> p h d", h=4), 4, stat[:, 104 + 4 * tb:108 + 4 * tb])
            nc.vector.memset(coef[:, 0:1], 0.0).then_inc(s_mksq, 1)
            dve.wait_ge(s_hrt, 2)
            link(nc.vector.reciprocal(stat[:, 112:120], stat[:, 104:112]))
            link(ts(stat[:, 112:120], stat[:, 112:120], SCALE, None, ALU.mult))
            for tb in range(TB):
                v = mqn[:, tb, :].rearrange("p (h d) -> p h d", h=4)
                ins = tt(v, v, stat[:, 112 + 4 * tb:116 + 4 * tb].unsqueeze(2).to_broadcast([P, 4, HD]), ALU.mult)
                if tb == 0:
                    link(ins)
            ins.then_inc(s_mqs, 1)
            dve.wait_ge(s_lb2, 1)
            link(tt(lb[:, 8:12], lb[:, 0:4], lb[:, 4:8], ALU.add))
            link(nc.vector.reciprocal(lb[:, 8:12], lb[:, 8:12]))
            link(tt(lb[:, 8:12], lb[:, 0:4], lb[:, 8:12], ALU.mult))
            link(ts(lb[:, 12:16], lb[:, 8:12], -1.0, 1.0, ALU.mult, ALU.add))
            for n in range(2):
                wait_read(dve, ("hgf", n))
                wait_read(dve, ("hgq", n))
            for h in range(HG_HEADS):
                cols = slice(h * T, (h + 1) * T)
                link(ts(hf[:, cols], hf[:, cols], lb[:, 12 + h:13 + h], lb[:, 8 + h:9 + h], ALU.mult, ALU.add))
            nc.vector.memset(coef[:, 0:1], 0.0).then_inc(s_hf, 1)
            link(ts(hk, hf, -1.0, 1.0, ALU.mult, ALU.add))
            link(tt(hq, hq, hsig, ALU.mult))

            for i in range(HEADS + 1):
                if i < HEADS:
                    ps = wait_full(dve, ("z", i))
                    dve.wait_ge(s_zln, i + 1)
                    if i >= 2:
                        wait_full(dve, ("ca", i - 2))
                    z = zsp[:, i % 2, :]
                    free(stt(z, ps[:, 0:384], 0.0, zexp[:, i % 2, :], ALU.max, ALU.add), ("z", i))
                    wait_read(dve, ("z", i))
                    tt(z[:, 0:P], z[:, 0:P], con("strict01"), ALU.mult)
                    tt(z[:, T:T + P], z[:, T:T + P], con("strict01"), ALU.mult).then_inc(s_zsp, 1)

            dve.wait_ge(s_hlog, 1)
            for h in range(HG_HEADS):
                cols = slice(h * T, (h + 1) * T)
                link(nc.vector.tensor_tensor_scan(hsig[:, cols], hones, hb[:, cols], 0.0, ALU.mult, ALU.add))
            cum = hsig
            for lv in range(9):
                if lv >= 2:
                    wait_full(dve, ("hg", lv - 2, 1))
                if lv == 0:
                    link(nc.vector.tensor_copy(hqe[:, 0, :], hq))
                    nc.vector.tensor_copy(hke[:, 0, :], hk).then_inc(s_hqe, 1)
                else:
                    m = 1 << (lv - 1)
                    ns = 4 * T // (2 * m)
                    c = cum.rearrange("p (s w m) -> p s w m", w=2, m=m)
                    a = harg.rearrange("p (s w m) -> p s w m", w=2, m=m)
                    ref = c[:, :, 0, m - 1:m].to_broadcast([P, ns, m])
                    tt(a[:, :, 1, :], c[:, :, 1, :], ref, ALU.subtract)
                    tt(a[:, :, 0, :], ref, c[:, :, 0, :], ALU.subtract).then_inc(s_harg, 1)
                    dve.wait_ge(s_hexp, lv)
                    link(tt(hqe[:, lv % 2, :], hq, harg, ALU.mult))
                    tt(hke[:, lv % 2, :], hk, harg, ALU.mult).then_inc(s_hqe, 1)
                    dve.wait_ge(s_hqe, lv + 1)
                if lv >= 1:
                    masked(dve, lv - 1, link, tt, stt, hacc, htmp, con, wait_full, wait_read, free)
            ps = wait_full(dve, ("hgx",))
            free(nc.vector.tensor_copy(hx, ps[:, :]), ("hgx",))
            wait_read(dve, ("hgx",))
            nc.vector.memset(coef[:, 0:1], 0.0).then_inc(s_hsc, 1)
            for tb in range(TB):
                ps = wait_full(dve, ("sbo", tb))
                free(nc.vector.tensor_copy(osum[:, tb, 0:512], ps[:, :]), ("sbo", tb))
            for tb in range(TB):
                ps = wait_full(dve, ("hgo", tb))
                free(nc.vector.tensor_copy(osum[:, tb, 512:768], ps[:, 0:256]), ("hgo", tb))
            for name in ("sbo", "hgo"):
                for tb in range(TB):
                    wait_read(dve, (name, tb))
            attention(UNITS2, [(0, T), (T, 2 * T)], lambda i: None)
            link(nc.vector.reciprocal(rl[:, 0:8], lsum[:, 16:24]))
            for tb in range(TB):
                ps = wait_full(dve, ("O", "mem", tb))
                free(tt(osum[:, tb, 768:1024].rearrange("p (h d) -> p h d", h=4),
                        ps[:, 0:256].rearrange("p (h d) -> p h d", h=4),
                        rl[:, tb * 4:(tb + 1) * 4].unsqueeze(2).to_broadcast([P, 4, HD]), ALU.mult),
                     ("O", "mem", tb))
            for tb in range(TB):
                head_norm(osum[:, tb, 0:768].rearrange("p (h d) -> p h d", h=12), 12, hstat[0][:, 12 * tb:12 * tb + 12])
            nc.vector.memset(coef[:, 0:1], 0.0).then_inc(s_hsq, 1)
            dve.wait_ge(s_hrt, 3)
            link(nc.vector.reciprocal(hstat[2][:, 0:24], hstat[1][:, 0:24]))
            dve.wait_ge(s_gsig, 1)
            for tb in range(TB):
                v = osum[:, tb, 0:768].rearrange("p (h d) -> p h d", h=12)
                link(tt(v, v, hstat[2][:, 12 * tb:12 * tb + 12].unsqueeze(2).to_broadcast([P, 12, HD]), ALU.mult))
                link(tt(tmp[:, tb, 0:256], tmp[:, tb, 0:256], hig[:, tb, 256:512], ALU.mult))
                link(tt(osum[:, tb, 512:768], osum[:, tb, 512:768], tmp[:, tb, 0:256], ALU.mult))
            for tb in range(TB):
                wait_read(dve, ("O", "mem", tb))
            nc.vector.memset(coef[:, 0:1], 0.0).then_inc(s_mix, 1)
            features_out("mixT", vall("headg"), plain_from=6)
            for n in range(2):
                for tb in range(TB):
                    ps = wait_full(dve, ("out2", n, tb))
                    v = x[:, tb, n * 512:(n + 1) * 512]
                    free(tt(v, v, ps[:, :], ALU.add), ("out2", n, tb))
            for n in range(2):
                for tb in range(TB):
                    wait_read(dve, ("out2", n, tb))
            nc.vector.memset(coef[:, 0:1], 0.0).then_inc(s_x1, 1)
            normed(6, x)
            features_out("h4T", vall("ffn2"))
            for n in range(1, 8, 2):
                ps = wait_full(dve, ("wq", n))
                free(nc.vector.tensor_copy(pqT[:, 2 * n:2 * n + 2, :].rearrange("p a t -> p (a t)"), ps[:, :]),
                     ("wq", n))

            def top16(src, values, index, scratch):
                v = [values[:, 0:8], values[:, 8:16]]
                i = [index[:, 0:8], index[:, 8:16]]
                link(nc.vector.max(v[0], src))
                nc.vector.max_index(i[0], v[0], src)
                link(nc.vector.match_replace(scratch, v[0], src, TAKEN))
                link(nc.vector.max(v[1], scratch))
                return nc.vector.max_index(i[1], v[1], scratch)

            for tb in range(TB):
                for q in range(4):
                    name = ("keys", 4 * tb + q)
                    ps = wait_full(dve, name)
                    for i in range(4):
                        hc = 4 * q + i
                        ins = top16(ps[:, i * P:(i + 1) * P], best1[:, tb, hc, :],
                                    idx1[:, tb, hc * TOPK:(hc + 1) * TOPK], keytmp[:, i % 2, :])
                        if i < 3:
                            link(ins)
                    free(ins, name)
                    wait_read(dve, name)
                link(nc.vector.tensor_copy(idx1f[:, tb, :, :].rearrange("p a b -> p (a b)"), idx1[:, tb, :]))
                halves = best1[:, tb, :, :].rearrange("p (h c) a -> p h c a", c=2)
                link(tt(cand.rearrange("p h (a b) -> p h a b", a=TOPK),
                        halves[:, :, 0, :].unsqueeze(3).to_broadcast([P, PEER_HEADS, TOPK, TOPK]),
                        halves[:, :, 1, :].unsqueeze(2).to_broadcast([P, PEER_HEADS, TOPK, TOPK]), ALU.add))
                for h in range(PEER_HEADS):
                    link(top16(cand[:, h, :], best2[:, tb, h * TOPK:(h + 1) * TOPK],
                               idx2[:, tb, h * TOPK:(h + 1) * TOPK], candtmp[:, h % 2, :]))
                link(ts(idx2p[:, 2 * tb, :], idx2[:, tb, :], 4, None, ALU.logical_shift_right))
                link(ts(idx2p[:, 2 * tb + 1, :], idx2[:, tb, :], TOPK - 1, None, ALU.bitwise_and))
                for c in range(2):
                    link(nc.vector.tensor_copy(idx2f[:, 2 * tb + c, :], idx2p[:, 2 * tb + c, :]))
                    pk = pick.rearrange("p (h k a) -> p h k a", h=PEER_HEADS, k=TOPK)
                    full_shape = [P, PEER_HEADS, TOPK, TOPK]
                    pos = idx2f[:, 2 * tb + c, :].rearrange("p (h k) -> p h k", h=PEER_HEADS)
                    link(tt(pk.rearrange("p h k a -> p (h k) a"),
                            idx2f[:, 2 * tb + c, :].unsqueeze(2).to_broadcast([P, SLOTS, TOPK]),
                            iota[:, 0:TOPK].unsqueeze(1).to_broadcast([P, SLOTS, TOPK]), ALU.is_equal))
                    keys = idx1f[:, tb, :, :].rearrange("p (h c) a -> p h c a", c=2)[:, :, c, :]
                    link(tt(pk, pk, keys.unsqueeze(2).to_broadcast(full_shape), ALU.mult))
                    link(nc.vector.tensor_reduce(slot[:, tb, c, :], pk.rearrange("p h k a -> p (h k) a"),
                                                 AX.X, ALU.add))
                b2 = best2[:, tb, :].rearrange("p (h k) -> p h k", h=PEER_HEADS)
                link(nc.vector.tensor_copy(gsum[:, tb, :], b2[:, :, 0]))
                link(tt(b2, b2, gsum[:, tb, :].unsqueeze(2).to_broadcast([P, PEER_HEADS, TOPK]), ALU.subtract))
            nc.vector.memset(coef[:, 0:1], 0.0).then_inc(s_gexp, 1)
            dve.wait_ge(s_gex2, 1)
            for tb in range(TB):
                b2 = best2[:, tb, :].rearrange("p (h k) -> p h k", h=PEER_HEADS)
                link(nc.vector.tensor_reduce(gsum[:, tb, :], b2, AX.X, ALU.add))
                link(nc.vector.reciprocal(gsum[:, tb, :], gsum[:, tb, :]))
                link(tt(slot[:, tb, 2, :].rearrange("p (h k) -> p h k", h=PEER_HEADS), b2,
                        gsum[:, tb, :].unsqueeze(2).to_broadcast([P, PEER_HEADS, TOPK]), ALU.mult))
            nc.vector.memset(coef[:, 0:1], 0.0).then_inc(s_slot, 1)
            wait_read(dve, ("idT", 0))
            wait_read(dve, ("idT", 1))

            def one_hots(it, waits):
                for half in range(2):
                    if waits:
                        dve.wait_ge(s_gfull, it * 2 + half - 1)
                    for i in range(4):
                        t = it * 8 + half * 4 + i
                        ts(onehot[:, 0, 4 * half + i, :], iota[:, :], slotT[:, 0, bass.ds(t, 1)],
                           slotT[:, 2, bass.ds(t, 1)], ALU.is_equal, ALU.mult)
                        ins = ts(onehot[:, 1, 4 * half + i, :], iota[:, :], slotT[:, 1, bass.ds(t, 1)], None,
                                 ALU.is_equal)
                    ins.then_inc(s_oh, 1)

            one_hots(0, False)
            with dve.Fori(1, T // 8, 1) as it:
                one_hots(it, True)
            dve.wait_ge(s_gdr, T // 4)

            by_key = arena[:, :].rearrange("p (t j) -> p j t", t=T)

            def gated(p, turn):
                dve.wait_ge(s_gelu, p + 1)
                w = mixw[:, turn * 512:(turn + 1) * 512].rearrange("p (j t) -> p j t", j=2)
                tt(w, w, by_key[:, bass.ds(p * 2, 2), :], ALU.mult).then_inc(s_w, 1)

            with dve.Fori(0, N_PAIRS // 3, 1) as r:
                for turn in range(3):
                    gated(r * 3 + turn, turn)
            gated(N_PAIRS - 1, 0)
            dve.wait_ge(s_vused, N_PAIRS)
            for tb in range(TB):
                for c in range(2):
                    v = x[:, tb, c * 512:(c + 1) * 512]
                    tt(v, v, banks[4 + 2 * tb + c][:, :], ALU.add).then_inc(s_res, 1)


def masked(dve, lv, link, tt, stt, hacc, htmp, con, wait_full, wait_read, free):
    m = con("hgmask").rearrange("p (l t) -> p l t", l=8)[:, lv, :]
    m = m.unsqueeze(1).to_broadcast([P, HG_HEADS, P])
    for tb in range(TB):
        name = ("hg", lv, tb)
        ps = wait_full(dve, name)
        src = ps[:, :].rearrange("p (h t) -> p h t", h=HG_HEADS)
        acc = hacc[:, tb, :].rearrange("p (h t) -> p h t", h=HG_HEADS)
        if lv == 0:
            free(tt(acc, src, m, ALU.mult), name)
            wait_read(dve, name)
        else:
            t = htmp.rearrange("p (h t) -> p h t", h=HG_HEADS)
            free(tt(t, src, m, ALU.mult), name)
            wait_read(dve, name)
            link(tt(acc, acc, t, ALU.add))


def _chunks(w, cols, kgroups):
    k, n = w.shape
    pad = -n % cols
    if pad:
        w = np.concatenate([w, np.zeros((k, pad), w.dtype)], 1)
        n += pad
    t = w.reshape(kgroups, k // P // kgroups, P, n // cols, cols)
    return t.transpose(3, 0, 2, 1, 4).reshape(n // cols, kgroups, P, -1)


def _features(v):
    return v.reshape(-1, P).T


def _constants():
    c = np.zeros((P, N_CONST), np.float32)
    p, q = np.arange(P)[:, None], np.arange(P)[None, :]

    def put(name, a):
        c[:, _C[name][0]:_C[name][1]] = a
    put("tri", -(p >= q).astype(np.float32))
    put("causal", np.where(q > p, NEG, 0.0))
    put("strict", np.where(p >= q, NEG, 0.0))
    put("strict01", (p < q))
    masks = [(p == q)]
    for m in HG_LEVELS:
        masks.append((p // (2 * m) == q // (2 * m)) & (p % (2 * m) < m) & (q % (2 * m) >= m))
    put("hgmask", np.concatenate(masks, 1))
    n = np.arange(16)
    put("blk", (np.arange(P)[:, None] // 16 == np.arange(HEADS)[None]) & ((np.arange(P) % 16 < N_CMP)[:, None]))
    seen = [((n * CMP_STRIDE + CMP_LEN - 1)[None, :] <= (p + tb * P)) & (n < N_CMP)[None] for tb in range(TB)]
    put("cmpadd", np.concatenate([np.where(s, 0.0, NEG) for s in seen], 1))
    put("cmp01", np.concatenate(seen, 1))
    half = HD // 2
    put("invf", np.float32(10000.0) ** (-np.arange(half, dtype=np.float32) / np.float32(half)))
    keep = np.concatenate([np.eye(P), np.broadcast_to(np.arange(P), (P, P))], 1).astype(np.float32)
    return c, keep


def _weights(i):
    w_in = i["w_in"][0]
    splits = np.cumsum([512] + [128] * 6 + [24, 512, 64, 64, 256, 64, 4])[:-1]
    (qn, kc, vc, ks, vs, kw, vw, gl, qd, kd, vd, qi, ki, wi) = np.split(w_in, splits, 1)
    order = [h for r in range(4) for h in (r, r + 4)]
    qn = qn.reshape(D, 8, HD)[:, order].reshape(D, 512)
    first = np.concatenate([qn, qd, qi, kc, ks, kw, kd, ki, vc, vs, vw, vd, gl, wi], 1)
    w2 = i["w_in_2"][0]
    sbq, sbk, sbv, hq, hf, hi, hg, mq = np.split(w2, np.cumsum([512] * 5 + [256] * 2), 1)
    second = np.concatenate([sbq, sbk, sbv, hq, hf, hi, hg], 1)
    parts = {
        "mem_kv": _chunks(i["w_mem_kv_2"][0], 512, 2),
        "ada": _chunks(i["w_ada"][0], 512, 2),
        "in": _chunks(first, 512, 2),
        "cmp1": np.stack([i[n][0].reshape(16, P, P).transpose(1, 0, 2).reshape(1, P, SLOTW)
                          for n in ("cmp_w1_k", "cmp_w1_v")]),
        "out": _chunks(i["w_out"][0], 512, 2),
        "up": _chunks(i["w_up"][0], 512, 2),
        "down": _chunks(i["w_down"][0], 512, 8).transpose(1, 0, 2, 3),
        "in2": _chunks(second, 512, 2),
        "in2m": _chunks(mq, 256, 1),
        "out2": _chunks(i["w_out_2"][0], 512, 2),
        "wq": _chunks(i["peer_w_query_2"][0], 512, 2),
        "keys": i["peer_sub_keys_2"][0].transpose(3, 0, 1, 2).reshape(1, 1, P, SLOTW),
    }
    return np.stack([parts[name][a, b] for name, a, b in TILES])


def kernel(**inputs):
    import concourse.bacc as _bacc
    from concourse.bass_utils import run_bass_kernel_spmd as _run

    i = {k: np.asarray(v) for k, v in inputs.items()}
    const, keep = _constants()
    pe = [i[n][0].reshape(16, 2 * HD).T for n in ("cmp_pe_k", "cmp_pe_v")]
    vec = np.concatenate(
        [_features(i["c"][0]), _features(i["b_ada"][0]), _features(i["g_pre_mix"][0]),
         _features(i["g_post_mix"][0]), _features(i["g_pre_ffn"][0]), _features(i["g_post_ffn"][0]),
         _features(i["norm_mix_gain_2"][0]), _features(i["norm_ffn_gain_2"][0]),
         _features(i["mem_norm_gain_2"]), _features(i["sb_out_gain_2"].reshape(-1)),
         _features(i["hg_out_gain_2"].reshape(-1)),
         np.concatenate([i["mem_q_gain_2"][0]] * 2)[:, None], np.concatenate([i["mem_k_gain_2"][0]] * 2)[:, None],
         _features(i["gamma_lb_2"][0]), _features(i["gamma_lb_2"][1]), pe[0], pe[1],
         i["cmp_w2_k"][0], i["cmp_w2_v"][0]], 1)
    u = i["peer_u_2"][0].reshape(P, N_PAIRS, 2, KD, P)
    v = i["peer_v_2"][0].reshape(P, N_PAIRS, SLOTW)
    arrays = {
        "x_dram": i["x"][0], "mem_dram": i["mem_2"][0],
        "pos_dram": i["positions"].reshape(TB, P).T,
        "vec_dram": vec, "ident_dram": keep, "const_dram": const,
        "w_dram": _weights(i),
        "u_dram": u.transpose(1, 4, 2, 3, 0).reshape(N_PAIRS, P, SLOTW),
        "v_dram": v.transpose(1, 0, 2),
    }
    arrays = {k: np.ascontiguousarray(a) for k, a in arrays.items()}
    nc = _bacc.Bacc("TRN2", target_bir_lowering=False, num_devices=1)
    args = [nc.dram_tensor(n, a.shape, mybir.dt.from_np(a.dtype), kind="ExternalInput").ap()
            for n, a in arrays.items()]
    out = nc.dram_tensor("out_dram", (T, D), F32, kind="ExternalOutput").ap()
    build(nc, *args, out)
    r = _run(nc, [arrays], core_ids=[0])
    return r.results[0]["out_dram"].reshape(1, T, D)
```

```python
from contextlib import ExitStack
import math

import numpy as np

import concourse.bass as bass
from concourse import mybir

ALU = mybir.AluOpType
ACT = mybir.ActivationFunctionType
AX = mybir.AxisListType
F32 = mybir.dt.float32
F32R = mybir.dt.float32r
BF16 = mybir.dt.bfloat16
I32 = mybir.dt.int32
U32 = mybir.dt.uint32

P = 128
T = 256
TB = T // P
D = 1024
KD = D // P
HD = 64
HEADS = 8
EPS = 1e-6
NEG = -1e30
TAKEN = -3e38
D_FF = 4 * D

CMP_LEN, CMP_STRIDE = 32, 16
N_CMP = (T - CMP_LEN) // CMP_STRIDE + 1
IDX_HEADS = 4
IDX_SCALE = (IDX_HEADS ** -0.5) * (HD ** -0.5)
DSA_K = min(256, T // 4)
SCALE = HD ** -0.5
N_ROT = 28
ROT_KC, ROT_KD, ROT_KI = 20, 26, 27
PAIR_QN, PAIR_QD, PAIR_QI, PAIR_KS, PAIR_KW, PAIR_KD, PAIR_KI = 0, 4, 8, 10, 11, 12, 13
N_PAIR = 14
PL_VC, PL_VS, PL_VW, PL_VD, PL_GL, PL_WI, N_PLAIN = 0, 128, 256, 384, 448, 472, 476

HG_HEADS = 4
PEER_HEADS = 8
N_KEYS = 128
TOPK = 16
SLOTS = PEER_HEADS * TOPK

_V = {}


def _columns(table, widths):
    at = 0
    for name, w in widths:
        table[name] = (at, at + w)
        at += w
    return at


N_VEC = _columns(_V, [
    ("c", 8), ("b_ada", 48), ("g_pre_mix", 8), ("g_post_mix", 8), ("g_pre_ffn", 8),
    ("g_post_ffn", 8), ("mix2", 8), ("ffn2", 8), ("memg", 8), ("headg", 6), ("qg", 1), ("kg", 1),
    ("gamma", 8), ("pe_k", 16), ("pe_v", 16), ("w2k", 64), ("w2v", 64)])

_C = {}
HG_LEVELS = (1, 2, 4, 8, 16, 32, 64)
N_CONST = _columns(_C, [
    ("tri", P), ("causal", P), ("strict", P), ("strict01", P), ("hgmask", 8 * P),
    ("blk", HEADS), ("cmpadd", TB * 16), ("cmp01", TB * 16), ("invf", HD // 2)])

PI2_A = 6.28125
PI2_B = round((2 * math.pi - PI2_A) * 2 ** 21) / 2 ** 21
PI2_C = 2 * math.pi - PI2_A - PI2_B
ROUND = 1.5 * 2 ** 23
PI_IN = 3.1415925

SLOTW = 2048
RING = 4


def weight_tiles():
    tiles = [("ada", n, k) for n in range(4) for k in range(2)]
    tiles += [("mem_kv", 0, k) for k in range(2)]
    tiles += [("in", n, k) for n in range(5) for k in range(2)]
    tiles += [("cmp1", n, 0) for n in range(2)]
    tiles += [("ada", n, k) for n in range(4, 12) for k in range(2)]
    tiles += [("out", n, k) for n in range(2) for k in range(2)]
    tiles += [("up", n, k) for n in range(8) for k in range(2)]
    tiles += [("down", kg, n) for kg in range(8) for n in range(2)]
    tiles += [("in2", n, k) for n in range(6) for k in range(2)] + [("in2m", 0, 0)]
    tiles += [("out2", n, k) for n in range(2) for k in range(2)]
    tiles += [("wq", n, k) for n in range(4) for k in range(2)]
    tiles += [("keys", 0, 0)]
    return tiles


TILES = weight_tiles()
TILE_AT = {t: n for n, t in enumerate(TILES)}
N_TILES = len(TILES)
HALF_PAIRS = N_KEYS // 4
STREAM = N_TILES + 4 * HALF_PAIRS
EARLY = 16


def psum_plan():
    used, plan = [0] * 8, {}

    def group(name, bank):
        used[bank] += 1
        plan[name] = (bank, used[bank])

    turn = [0]

    def rotate(name, banks):
        group(name, banks[turn[0] % len(banks)])
        turn[0] += 1

    every = list(range(8))

    def transposed(what):
        for q in range(4):
            rotate((what, q), every)

    transposed("memT")
    rotate(("ada", 0), every)
    for tb in range(TB):
        rotate(("mkv", tb), every)
    transposed("h1T")
    for n in range(5):
        for tb in range(TB):
            rotate(("in", n, tb), every)
    rotate(("mkT",), every)
    for n in range(7):
        rotate(("pairT", n), every)
    rotate(("kcT",), every)
    rotate(("vcT",), every)
    rotate(("cmp", 0), every)
    rotate(("cmp", 1), every)
    rotate(("kcmp",), every)
    rotate(("vblk",), every)
    rotate(("Sc", 0), every)
    rotate(("Sc", 1), every)
    for n in range(4):
        rotate(("L", n), every)
    rotate(("pcT",), every)
    group(("Oc", 0), 6)
    group(("Oc", 1), 7)
    attention_groups(group, UNITS1)
    rotate(("ada", 1), every)
    transposed("oT")
    for n in range(2):
        for tb in range(TB):
            rotate(("out", n, tb), every)
    for n in range(4):
        rotate(("gg", n), every)
    transposed("h2T")
    for n in range(16):
        rotate(("up", n), [0, 1, 2, 3])
    for tb in range(TB):
        for n in range(2):
            group(("down", n, tb), 4 + 2 * tb + n)
    transposed("h3T")
    for name in ("sbq", "sbk"):
        for n in range(2):
            rotate((name, n), every)
    for tb in range(TB):
        rotate(("sbv", tb), every)
    for name in ("hgq", "hgf"):
        for n in range(2):
            rotate((name, n), every)
    for tb in range(TB):
        rotate(("hig", tb), every)
    for tb in range(TB):
        rotate(("mq", tb), every)
    rotate(("mqT",), every)
    for i in range(HEADS):
        group(("z", i), i % 2)
    for i in range(HEADS + 1):
        if i < HEADS:
            group(("ca", i), 2 + i % 2)
        if i == 1:
            group(("sbo", 0), 4)
            group(("sbo", 1), 5)
    for lv in range(len(HG_LEVELS) + 2):
        if lv < 8:
            group(("hg", lv, 0), 2 * (lv % 2))
            group(("hg", lv, 1), 2 * (lv % 2) + 1)
        else:
            group(("hgx",), 0)
    group(("hgo", 0), 6)
    group(("hgo", 1), 7)
    attention_groups(group, UNITS2)
    transposed("mixT")
    for n in range(2):
        for tb in range(TB):
            rotate(("out2", n, tb), every)
    transposed("h4T")
    for n in range(8):
        rotate(("wq", n), every)
    for n in range(8):
        group(("keys", n), 2 + n % 6)
    group(("idT", 0), 2)
    group(("idT", 1), 3)
    return plan, used


UNITS1 = [(kind, h) for kind in ("slc", "win", "dsa") for h in range(HEADS)]
UNITS2 = [("mem", h) for h in range(4)]
O_BANK = {"slc": 4, "win": 6, "dsa": 4, "mem": 4}


def attention_groups(group, units):
    n = len(units)
    for i in range(n + 2):
        if i < n:
            group(("S", *units[i]), i % 2)
        if 1 <= i <= n:
            group(("PT", *units[i - 1]), 2 + (i - 1) % 2)
        if i >= 2 and units[i - 2][1] == 0:
            for tb in range(TB):
                group(("O", units[i - 2][0], tb), O_BANK[units[i - 2][0]] + tb)


PLAN, USED = psum_plan()


def build(nc, x_in, mem_in, pos_in, vec_in, ident_in, const_in, w_in, out):
    with ExitStack() as ctx:
        def sb(name, shape, dt=F32):
            return ctx.enter_context(nc.sbuf_tensor(name, [P] + shape, dt))

        def sem(name):
            return ctx.enter_context(nc.semaphore(name))

        ring = sb("ring", [RING, SLOTW])
        x_at = nc.sbuf_base
        x = sb("x", [TB, D])
        hT_at = nc.sbuf_base
        hT = sb("hT", [KD, T])
        ident = sb("ident", [P])
        iota = sb("iota", [P])
        keyT = sb("keyT", [2, T], BF16)
        gateT = sb("gateT", [T])
        gates = sb("gates", [T, 3], BF16)
        iotab = sb("iotab", [P], BF16)
        hot1 = sb("hot1", [2, 4, P], BF16)
        hot2 = sb("hot2", [2, 4, HD], BF16)
        hotg = sb("hotg", [2, 4, 3, HD], BF16)
        stat = sb("stat", [160])
        ada_at = nc.sbuf_base
        ada = sb("ada", [4, 512])
        mix_at = nc.sbuf_base
        mix_hi = sb("mix_hi", [2, 2 * T], F32R)
        mix_lo = sb("mix_lo", [2, 2 * T], F32R)
        arena = sb("arena", [P * T])
        area = [arena[:, n * P * HD * 2:(n + 1) * P * HD * 2] for n in range(2)]

        where = [0]

        def take(*shape, at=None):
            if at is not None:
                where[0] = at
            n = int(np.prod(shape))
            start = where[0]
            where[0] += n
            assert where[0] <= P * T, where[0]
            v = arena[:, start:start + n]
            if len(shape) == 2:
                v = v.rearrange("p (a b) -> p a b", a=shape[0])
            if len(shape) == 3:
                v = v.rearrange("p (a b c) -> p a b c", a=shape[0], b=shape[1])
            return v

        const = take(N_CONST)
        vec = take(N_VEC)
        mkv = take(TB, 512)
        mkT = take(2, T)
        tmp = take(TB, D)
        junk = take(D)
        negones = take(P)
        identb = take(P // 2).bitcast(BF16)
        causalb = take(P // 2).bitcast(BF16)
        strictb = take(P // 2).bitcast(BF16)
        mod = take(48)
        gain1 = take(KD)
        gain2 = take(KD)
        gg = take(2 * KD)
        prob_at = where[0]
        prob = take(2, 512)
        probT = take(2, 512)
        osum = take(TB, D)
        common = where[0]
        rot = take(TB, N_ROT * HD)
        plain = take(TB, N_PLAIN)
        pairT = take(N_PAIR, T)
        kvT = [take(3, T), take(3, T)]
        trig = take(8, HD)
        cosd = take(TB, HD)
        sind = take(TB, HD)
        rtmp = take(2, 512)
        hidk = take(2, 16)
        hidv = take(HEADS, 16)
        hbias = take(2)
        kcmpT = take(16)
        vblk = take(HEADS, HD)
        sc = take(TB * HEADS, 16)
        pcT = take(TB, P)
        relu = take(4, 512)
        score = take(TB, T)
        work = take(TB, T)
        maskd = take(TB, T // 2).bitcast(BF16)
        otmp = take(HEADS * HD)
        sig = take(TB, 24)
        wsc = take(TB, 4)
        posf = take(TB)
        posi = take(TB).bitcast(I32)
        ggb = take(2, D)
        addb = take(4, 512)
        block1_end = where[0]
        upT = take(D_FF // P, T, at=common)
        assert where[0] <= block1_end - 2 * D - 4 * 512
        sbqT = take(4, T, at=common)
        sbkT = take(4, T)
        sbv = take(TB, 512)
        hq = take(4 * T)
        hf = take(4 * T)
        hk = take(4 * T)
        hb = take(4 * T)
        hsig = take(4 * T)
        hones = take(T)
        hig = take(TB, 512)
        mqn = take(TB, T)
        mqT = take(2, T)
        zabs = take(2, 384)
        zexp_at = where[0]
        zexp = take(HEADS, 384)
        zsp = take(HEADS, 384)
        aT = take(2, 384)
        hqe = take(2, 4 * T)
        lb = take(16)
        hacc = take(TB, 512, at=zexp_at)
        hx = take(512)
        htmp = take(512)
        harg = take(4 * T)
        hke = take(2, 4 * T, at=prob_at)
        pqT = take(16, T, at=N_CONST + N_VEC)
        keytmp = take(2, P)
        best1 = take(TB, 16, TOPK)
        idx1 = take(TB, 16 * TOPK).bitcast(U32)
        idx1f = take(TB, 16, TOPK)
        cand = take(PEER_HEADS, T)
        candtmp = take(2, T)
        best2 = take(TB, SLOTS)
        idx2 = take(TB, SLOTS).bitcast(U32)
        idx2p = take(2 * TB, SLOTS).bitcast(U32)
        idx2f = take(2 * TB, SLOTS)
        pick = take(2048)
        slot = take(TB, 3, SLOTS)
        gsum = take(TB, PEER_HEADS)
        assert where[0] <= P * T // 2

        keep = area[1][:, 7 * SLOTW:8 * SLOTW]

        def vcol(name, i=0, n=1):
            return vec[:, _V[name][0] + i:_V[name][0] + i + n]

        def vall(name):
            return vec[:, _V[name][0]:_V[name][1]]

        def con(name):
            return const[:, _C[name][0]:_C[name][1]]

        ssq = stat[:, 0:12]
        rms = stat[:, 12:24]
        rstd = stat[:, 24:36]
        nmax = stat[:, 36:44]
        lsum = stat[:, 44:100]
        eps = stat[:, 100:101]
        one = stat[:, 101:102]
        cmax = stat[:, 104:120]
        coef = stat[:, 120:136]
        rl = stat[:, 136:152]
        KINDS = {"cmp": 0, "slc": 16, "win": 32, "dsa": 0, "mem": 16}
        hstat = [zabs[:, 0, 0:48], zabs[:, 0, 48:96], zabs[:, 0, 96:144]]

        banks = [ctx.enter_context(nc.psum_tensor(f"bank{i}", [P, 512], F32)) for i in range(8)]

        full = [sem(f"bank{i}_full") for i in range(8)]
        drained = [sem(f"bank{i}_drained") for i in range(8)]
        loaded = [sem(f"slot{i}_loaded") for i in range(RING)]
        w_used = sem("w_used")
        s_small = sem("small_loaded")
        s_x = sem("x_loaded")
        s_mem = sem("mem_loaded")
        s_const = sem("const_ready")
        s_eps = sem("eps_set")
        s_ssq = sem("norm_root")
        s_xn = sem("norm_rows")
        s_mkn = sem("mem_keys_normed")
        s_mksq = sem("mem_keys_root")
        s_gain = sem("gains_ready")
        s_trig = sem("trig_args")
        s_sin = sem("trig_ready")
        s_rot = sem("rotated")
        s_vblk = sem("cmp_values")
        s_sc = sem("cmp_scores")
        s_pc = sem("cmp_exp")
        s_pcz = sem("cmp_probs")
        s_pv = sem("values_copied")
        s_maskd = sem("dsa_mask")
        s_nmax = sem("row_max")
        s_pvd = sem("unit_done")
        s_o = sem("heads_summed")
        s_ggf = sem("post_gain")
        s_x1 = sem("residual")
        s_upsq = sem("up_squared")
        s_lb1 = sem("lb_max")
        s_lb2 = sem("lb_exp")
        s_hf = sem("hg_forget")
        s_hlog = sem("hg_log")
        s_harg = sem("hg_arg")
        s_hexp = sem("hg_decay")
        s_hqe = sem("hg_operands")
        s_hsc = sem("hg_scores")
        s_zln = sem("z_log")
        s_zsp = sem("z_softplus")
        s_sbd = sem("stick_done")
        s_hsq = sem("head_sumsq")
        s_hrt = sem("head_root")
        s_mix = sem("mixed_ready")
        s_mqs = sem("mem_q_normed")
        s_gsig = sem("hg_gate_sig")
        s_slot = sem("slots_ready")
        s_gexp = sem("gate_args")
        s_gex2 = sem("gate_exp")
        s_oh = sem("onehots_ready")
        s_gfull = sem("gate_tokens_full")
        s_gdr = sem("gate_tokens_drained")
        s_keys = sem("keys_copied")
        s_eq = sem("first_keys_compared")
        s_gelu = sem("expert_gelu")
        s_w = sem("expert_weights")
        s_seed = sem("sums_seeded")
        s_mhi = sem("weights_high")
        s_mlo = sem("weights_low")
        s_vhi = sem("tile_high")
        s_vlo = sem("tile_low")
        s_vused = sem("tile_parts_used")
        s_hhi = sem("hT_high")
        s_hlo = sem("hT_low")
        s_res = sem("result_ready")
        s_out = sem("result_stored")
        v_step = sem("vector_step")
        a_step = sem("scalar_step")

        block = ctx.enter_context(nc.Block())

        def tokens(tb):
            return slice(tb * P, (tb + 1) * P)

        def wait_full(eng, name):
            bank, use = PLAN[name]
            eng.wait_ge(full[bank], use)
            return banks[bank]

        def free(ins, name):
            ins.then_inc(drained[PLAN[name][0]], 1)

        def wait_read(eng, name):
            bank, use = PLAN[name]
            eng.wait_ge(drained[bank], use)

        def tile(name):
            n = TILE_AT[name]
            return ring[:, n % RING, :]

        def ada_sum(n):
            return ada[:, n % 4, :] if n < 8 else addb[:, n - 8, :]

        v_hi = nc.alloc_sbuf_tensor_at("v_hi", [P, 2, D], F32R, offset=x_at)
        v_lo = nc.alloc_sbuf_tensor_at("v_lo", [P, 2, D], F32R, offset=ada_at)
        hT_hi = nc.alloc_sbuf_tensor_at("hT_hi", [P, KD, T], F32R, offset=mix_at)
        hT_lo = nc.alloc_sbuf_tensor_at("hT_lo", [P, KD, T], F32R, offset=hT_at)

        def km(name, n=512):
            return tile(name).rearrange("p (k n) -> p k n", n=n)

        def pair_weights(half, index):
            w = area[1 - half].rearrange("p (q n) -> p q n", q=HALF_PAIRS)
            return w[:, bass.ds(index, 1), :].rearrange("p o n -> p (o n)")

        SPLIT_V = (0, 2 * HALF_PAIRS)
        SPLIT_U = HALF_PAIRS

        def j_rows(first, i, jj):
            return ring[:, (first + i) % RING, jj * D:(jj + 1) * D]

        def above_zero(eng, sem_, value):
            if not isinstance(value, int) or value > 0:
                eng.wait_ge(sem_, value)

        NORMS = ["mem", "h1", "post1", "h2", "post2", "h3", "h4"]

        @block.sync
        def _(sp):
            sp.dma_start(x[:, :, :], x_in.rearrange("(b p) d -> p b d", p=P)).then_inc(s_x, 16)
            for n in range(RING):
                sp.dma_start(ring[:, n, :], w_in[n]).then_inc(loaded[n], 16)
            rounds = STREAM // RING
            with sp.Fori(1, rounds, 1) as r:
                for n in range(RING):
                    sp.wait_ge(w_used, (r - 1) * RING + n + 1)
                    sp.dma_start(ring[:, n, :], w_in[bass.ds(r * RING + n, 1)].rearrange("o p n -> p (o n)")
                                 ).then_inc(loaded[n], 16)
            for n in range(rounds * RING, STREAM):
                sp.wait_ge(w_used, n - RING + 1)
                sp.dma_start(ring[:, n % RING, :], w_in[n]).then_inc(loaded[n % RING], 16)
            sp.wait_ge(s_res, 4)
            sp.dma_start(out.rearrange("(b p) d -> p b d", p=P), x[:, :, :]).then_inc(s_out, 16)
            sp.wait_ge(s_out, 16)

        SMALL = 5 * 16

        @block.tensor
        def _(pe):
            order = iter(PLAN)

            def begin(name):
                assert next(order) == name, name
                bank, use = PLAN[name]
                if use > 1:
                    pe.wait_ge(drained[bank], use - 1)
                return banks[bank]

            def end(ins, name):
                ins.then_inc(full[PLAN[name][0]], 1)

            def arrived(*names):
                for name in names:
                    n = TILE_AT[name]
                    pe.wait_ge(loaded[n % RING], 16 * (n // RING + 1))

            def mm(out_, lhsT, rhs, start=True, stop=True):
                return nc.tensor.matmul(out_, lhsT, rhs, start=start, stop=stop)

            def both_halves(ps, cols, head):
                mm(ps[0:HD, cols], head, ident[:, :])
                return mm(ps[HD:P, cols], head, ident[:, :])

            def rows_to_features(what, src):
                for q in range(4):
                    ps = begin((what, q))
                    for kk in range(2):
                        for tb in range(TB):
                            k = 2 * q + kk
                            last = nc.tensor.transpose(ps[:, kk * T + tb * P:kk * T + (tb + 1) * P],
                                                       src[:, tb, k * P:(k + 1) * P], ident[:, :])
                    end(last, (what, q))

            def wait_hT(what):
                for q in range(4):
                    wait_read(pe, (what, q))

            def project_rows(what, group, n, width=512):
                out_ = [begin((group, n, tb)) for tb in range(TB)]
                for half in range(2):
                    arrived((what, n, half))
                    w = km((what, n, half))
                    for tb in range(TB):
                        for kk in range(4):
                            k = 4 * half + kk
                            last = mm(out_[tb][:, 0:width], hT[:, k, tokens(tb)], w[:, kk, 0:width],
                                      start=(k == 0), stop=(k == KD - 1))
                        if half == 1:
                            end(last, (group, n, tb))
                    if half == 0:
                        last.then_inc(w_used, 1)
                    else:
                        pe.drain().then_inc(w_used, 1)

            def project_features(what, n, groups):
                arrived((what, n, 0), (what, n, 1))
                w = [km((what, n, half)) for half in range(2)]
                for g in range(2):
                    ps = begin(groups[g])
                    for s in range(2):
                        c = (2 * g + s) * P
                        for k in range(KD):
                            last = mm(ps[:, s * T:(s + 1) * T], w[k // 4][:, k % 4, c:c + P],
                                      hT[:, k, :], start=(k == 0), stop=(k == KD - 1))
                    end(last, groups[g])
                pe.drain().then_inc(w_used, 2)

            def modulation(part, columns):
                pe.wait_ge(w_used, TILE_AT[("ada", columns[-1], 1)] + 1)
                ps = begin(("ada", part))
                for n in columns:
                    for s in range(4):
                        last = mm(ps[:, 4 * n + s:4 * n + s + 1], ada_sum(n)[:, s * P:(s + 1) * P], one)
                end(last, ("ada", part))

            def attention(units, operands, v_of, cols, mask):
                n = len(units)

                def scores(i):
                    ps = begin(("S", *units[i]))
                    for tb in range(TB):
                        q, k = operands(units[i], tb)
                        a, b = cols[tb]
                        m = mask(units[i], tb)
                        last = mm(ps[:, a:b], q, k, stop=(m is None))
                        if m is not None:
                            lo, mat = m
                            last = mm(ps[:, a + lo:b], identb, mat, start=False)
                    end(last, ("S", *units[i]))

                def turn(i):
                    wait_read(pe, ("S", *units[i]))
                    ps = begin(("PT", *units[i]))
                    for c in range(cols[1][1] // P):
                        last = nc.tensor.transpose(ps[:, c * P:(c + 1) * P],
                                                   prob[:, i % 2, c * P:(c + 1) * P], ident[:, :])
                    end(last, ("PT", *units[i]))

                def values(i):
                    kind, h = units[i]
                    if h == 0:
                        for tb in range(TB):
                            begin(("O", kind, tb))
                    wait_read(pe, ("PT", kind, h))
                    for tb in range(TB):
                        ps = banks[PLAN[("O", kind, tb)][0]]
                        a, b = cols[tb]
                        for c in range(a // P, b // P):
                            last = mm(ps[:, h * HD:(h + 1) * HD], probT[:, i % 2, c * P:(c + 1) * P],
                                      v_of(units[i], c - a // P), start=(c == a // P), stop=(c == b // P - 1))
                        if i + 1 == n or units[i + 1][0] != kind:
                            end(last, ("O", kind, tb))
                    pe.drain().then_inc(s_pvd, 1)

                base = 0 if units is UNITS1 else len(UNITS1)
                for i in range(n + 2):
                    if i < n:
                        scores(i)
                    if 1 <= i <= n:
                        turn(i - 1)
                    if i >= 2:
                        values(i - 2)

            pe.wait_ge(s_small, SMALL)
            pe.wait_ge(s_const, 1)
            pe.wait_ge(s_xn, 1)
            rows_to_features("memT", tmp)
            modulation(0, range(4))
            wait_hT("memT")
            out_ = [begin(("mkv", tb)) for tb in range(TB)]
            for half in range(2):
                arrived(("mem_kv", 0, half))
                for tb in range(TB):
                    for kk in range(4):
                        k = 4 * half + kk
                        last = mm(out_[tb][:, :], hT[:, k, tokens(tb)], km(("mem_kv", 0, half))[:, kk, :],
                                  start=(k == 0), stop=(k == KD - 1))
                    if half == 1:
                        end(last, ("mkv", tb))
            pe.drain().then_inc(w_used, 2)
            pe.wait_ge(s_xn, 2)
            rows_to_features("h1T", tmp)
            wait_hT("h1T")
            for n in range(5):
                project_rows("in", "in", n, 512 if n < 4 else 220)
            pe.wait_ge(s_mkn, 1)
            ps = begin(("mkT",))
            for pr in range(2):
                for tb in range(TB):
                    last = nc.tensor.transpose(ps[:, pr * T + tb * P:pr * T + (tb + 1) * P],
                                               mkv[:, tb, pr * P:(pr + 1) * P], ident[:, :])
            end(last, ("mkT",))
            pe.wait_ge(s_rot, 1)
            for n in range(7):
                ps = begin(("pairT", n))
                for s in range(2):
                    pair = 2 * n + s
                    for tb in range(TB):
                        cols = slice(s * T + tb * P, s * T + (tb + 1) * P)
                        if pair < PAIR_KD:
                            first = 2 * pair if pair < PAIR_KS else 2 * pair + 2
                            last = nc.tensor.transpose(ps[:, cols], rot[:, tb, first * HD:(first + 2) * HD],
                                                       ident[:, :])
                        else:
                            r = ROT_KD if pair == PAIR_KD else ROT_KI
                            last = both_halves(ps, cols, rot[:, tb, r * HD:(r + 1) * HD])
                end(last, ("pairT", n))
            pe.wait_ge(s_pv, 4)
            for which, src, first in (("kcT", rot, ROT_KC * HD), ("vcT", plain, PL_VC)):
                ps = begin((which,))
                for g in range(2):
                    for tb in range(TB):
                        a = first + g * HD
                        last = both_halves(ps, slice(g * T + tb * P, g * T + (tb + 1) * P), src[:, tb, a:a + HD])
                end(last, (which,))
            for which in range(2):
                arrived(("cmp1", which, 0))
                wait_read(pe, (("kcT",), ("vcT",))[which])
                w1 = km(("cmp1", which, 0), P)
                ps = begin(("cmp", which))
                for m in range(16):
                    last = mm(ps[:, 0:45], w1[:, m, :], kvT[which][:, :, 2 * m:2 * m + 225:16],
                              start=(m == 0), stop=(m == 15))
                end(last, ("cmp", which))
            pe.drain().then_inc(w_used, 2)
            wait_read(pe, ("cmp", 0))
            ps = begin(("kcmp",))
            for g in range(2):
                last = mm(ps[g * HD:(g + 1) * HD, 0:N_CMP], vall("w2k"), hidk[:, g, 0:N_CMP])
            end(last, ("kcmp",))
            wait_read(pe, ("cmp", 1))
            ps = begin(("vblk",))
            end(mm(ps[:, 0:HD], hidv.rearrange("p h n -> p (h n)"), vall("w2v")), ("vblk",))
            wait_read(pe, ("kcmp",))
            for n in range(7):
                wait_read(pe, ("pairT", n))
            for g in range(2):
                ps = begin(("Sc", g))
                rows = slice(g * HD, (g + 1) * HD)
                for tb in range(TB):
                    for r in range(4):
                        c = (tb * 4 + r) * 16
                        last = mm(ps[:, c:c + N_CMP], pairT[rows, PAIR_QN + r, tokens(tb)], kcmpT[rows, 0:N_CMP])
                end(last, ("Sc", g))
            for n in range(4):
                tb, odd = n // 2, n % 2
                width = (tb + 1) * P
                ps = begin(("L", n))
                rows = slice(odd * HD, (odd + 1) * HD)
                for i in range(2):
                    last = mm(ps[:, i * width:(i + 1) * width], pairT[rows, PAIR_QI + i, tokens(tb)],
                              pairT[rows, PAIR_KI, 0:width])
                end(last, ("L", n))
            pe.wait_ge(s_pcz, 1)
            ps = begin(("pcT",))
            for tb in range(TB):
                last = nc.tensor.transpose(ps[:, tb * P:(tb + 1) * P],
                                           sc[:, tb * HEADS:(tb + 1) * HEADS, :].rearrange("p h n -> p (h n)"),
                                           ident[:, :])
            end(last, ("pcT",))
            wait_read(pe, ("pcT",))
            pe.wait_ge(s_vblk, 1)
            for tb in range(TB):
                ps = begin(("Oc", tb))
                end(mm(ps[:, :], pcT[:, tb, :], vblk.rearrange("p h d -> p (h d)")), ("Oc", tb))

            def operands1(unit, tb):
                kind, h = unit
                if kind == "dsa":
                    rows, q, k = slice((h % 2) * HD, (h % 2 + 1) * HD), PAIR_QD + h // 2, PAIR_KD
                else:
                    g, r = h // 4, h % 4
                    rows, q = slice(g * HD, (g + 1) * HD), PAIR_QN + r
                    k = PAIR_KS if kind == "slc" else PAIR_KW
                return pairT[rows, q, tokens(tb)], pairT[rows, k, 0:(tb + 1) * P]

            def values1(unit, c):
                kind, h = unit
                a = {"slc": PL_VS + (h // 4) * HD, "win": PL_VW + (h // 4) * HD, "dsa": PL_VD}[kind]
                return plain[:, c, a:a + HD]

            def mask1(unit, tb):
                if unit == ("dsa", 0):
                    pe.wait_ge(s_maskd, tb + 1)
                if unit[0] == "dsa":
                    return 0, maskd[:, tb, 0:(tb + 1) * P]
                return tb * P, causalb

            attention(UNITS1, operands1, values1, [(0, P), (P, P + T)], mask1)
            modulation(1, range(4, 12))
            pe.wait_ge(s_o, 1)
            rows_to_features("oT", osum)
            wait_hT("oT")
            for n in range(2):
                project_rows("out", "out", n)
            pe.wait_ge(s_ggf, 1)
            for n in range(4):
                ps = begin(("gg", n))
                for k in range(4):
                    last = mm(ps[:, k * P:(k + 1) * P],
                              gg[:, 4 * n + k:4 * n + k + 1].to_broadcast([P, P]), ident[:, :])
                end(last, ("gg", n))
            pe.wait_ge(s_xn, 3)
            rows_to_features("h2T", tmp)
            wait_hT("h2T")
            for n in range(8):
                project_features("up", n, [("up", 2 * n), ("up", 2 * n + 1)])
            out_ = {}
            for tb in range(TB):
                for n in range(2):
                    out_[n, tb] = begin(("down", n, tb))
            for kg in range(8):
                pe.wait_ge(s_upsq, 2 * kg + 2)
                for n in range(2):
                    arrived(("down", kg, n))
                    for tb in range(TB):
                        for kk in range(4):
                            k = 4 * kg + kk
                            last = mm(out_[n, tb][:, :], upT[:, k, tokens(tb)], km(("down", kg, n))[:, kk, :],
                                      start=(k == 0), stop=(k == D_FF // P - 1))
                        if kg == 7:
                            end(last, ("down", n, tb))
                    pe.drain().then_inc(w_used, 1)

            pe.wait_ge(s_xn, 4)
            rows_to_features("h3T", tmp)
            wait_hT("h3T")
            project_features("in2", 0, [("sbq", 0), ("sbq", 1)])
            project_features("in2", 1, [("sbk", 0), ("sbk", 1)])

            def rows2(n, group):
                out_ = [begin((group, tb)) for tb in range(TB)]
                arrived(("in2", n, 0), ("in2", n, 1))
                for tb in range(TB):
                    for k in range(KD):
                        last = mm(out_[tb][:, :], hT[:, k, tokens(tb)], km(("in2", n, k // 4))[:, k % 4, :],
                                  start=(k == 0), stop=(k == KD - 1))
                    end(last, (group, tb))
                pe.drain().then_inc(w_used, 2)

            rows2(2, "sbv")
            project_features("in2", 3, [("hgq", 0), ("hgq", 1)])
            project_features("in2", 4, [("hgf", 0), ("hgf", 1)])
            rows2(5, "hig")
            arrived(("in2m", 0, 0))
            for tb in range(TB):
                ps = begin(("mq", tb))
                for k in range(KD):
                    last = mm(ps[:, 0:T], hT[:, k, tokens(tb)], km(("in2m", 0, 0), T)[:, k, :],
                              start=(k == 0), stop=(k == KD - 1))
                end(last, ("mq", tb))
            pe.drain().then_inc(w_used, 1)
            pe.wait_ge(s_mqs, 1)
            ps = begin(("mqT",))
            for pr in range(2):
                for tb in range(TB):
                    last = nc.tensor.transpose(ps[:, pr * T + tb * P:pr * T + (tb + 1) * P],
                                               mqn[:, tb, pr * P:(pr + 1) * P], ident[:, :])
            end(last, ("mqT",))
            for name in (("sbq", 0), ("sbq", 1), ("sbk", 0), ("sbk", 1), ("sbv", 0), ("sbv", 1)):
                wait_read(pe, name)
            for h in range(HEADS):
                rows, pr = slice((h % 2) * HD, (h % 2 + 1) * HD), h // 2
                ps = begin(("z", h))
                mm(ps[:, 0:T], sbkT[rows, pr, 0:P], sbqT[rows, pr, :])
                end(mm(ps[:, T:T + P], sbkT[rows, pr, P:T], sbqT[rows, pr, P:T]), ("z", h))
            pe.wait_ge(s_zsp, 1)
            for i in range(HEADS + 1):
                if i < HEADS:
                    h = i
                    rows, pr = slice((h % 2) * HD, (h % 2 + 1) * HD), h // 2
                    ps = begin(("ca", h))
                    L = zsp[:, h, :]
                    mm(ps[:, 0:P], sbkT[rows, pr, 0:P], sbqT[rows, pr, 0:P], stop=False)
                    mm(ps[:, 0:P], con("tri"), L[:, 0:P], start=False, stop=False)
                    mm(ps[:, 0:P], identb, strictb, start=False)
                    mm(ps[:, P:T], sbkT[rows, pr, 0:P], sbqT[rows, pr, P:T], stop=False)
                    mm(ps[:, P:T], con("tri"), L[:, P:T], start=False, stop=False)
                    mm(ps[:, P:T], negones, L[:, T:T + P], start=False)
                    mm(ps[:, T:T + P], sbkT[rows, pr, P:T], sbqT[rows, pr, P:T], stop=False)
                    mm(ps[:, T:T + P], con("tri"), L[:, T:T + P], start=False, stop=False)
                    end(mm(ps[:, T:T + P], identb, strictb, start=False), ("ca", h))
                if i >= 1:
                    h = i - 1
                    if h == 0:
                        so = [begin(("sbo", tb)) for tb in range(TB)]
                    wait_read(pe, ("ca", h))
                    col = slice(h * HD, (h + 1) * HD)
                    a = aT[:, h % 2, :]
                    m0 = mm(so[0][:, col], a[:, 0:P], sbv[:, 0, col])
                    mm(so[1][:, col], a[:, P:T], sbv[:, 0, col], stop=False)
                    m1 = mm(so[1][:, col], a[:, T:T + P], sbv[:, 1, col], start=False)
                    if h == HEADS - 1:
                        end(m0, ("sbo", 0))
                        end(m1, ("sbo", 1))
                    else:
                        m1.then_inc(s_sbd, 1)
            for lv in range(9):
                pe.wait_ge(s_hqe, lv + 1)
                q = hqe[:, lv % 2, :].rearrange("p (h t) -> p h t", h=HG_HEADS)
                k = hke[:, lv % 2, :].rearrange("p (h t) -> p h t", h=HG_HEADS)
                if lv < 8:
                    for tb in range(TB):
                        ps = begin(("hg", lv, tb))
                        for h in range(HG_HEADS):
                            last = mm(ps[:, h * P:(h + 1) * P], k[:, h, tokens(tb)], q[:, h, tokens(tb)])
                        end(last, ("hg", lv, tb))
                else:
                    ps = begin(("hgx",))
                    for h in range(HG_HEADS):
                        last = mm(ps[:, h * P:(h + 1) * P], k[:, h, 0:P], q[:, h, P:T])
                    end(last, ("hgx",))
            pe.wait_ge(s_hsc, 1)
            wait_read(pe, ("hig", 0))
            wait_read(pe, ("hig", 1))
            for tb in range(TB):
                ps = begin(("hgo", tb))
                for h in range(HG_HEADS):
                    col = slice(h * HD, (h + 1) * HD)
                    last = mm(ps[:, col], hacc[:, tb, h * P:(h + 1) * P], hig[:, tb, col], stop=(tb == 0))
                    if tb == 1:
                        last = mm(ps[:, col], hx[:, h * P:(h + 1) * P], hig[:, 0, col], start=False)
                end(last, ("hgo", tb))
            wait_read(pe, ("mqT",))
            wait_read(pe, ("mkT",))

            def operands2(unit, tb):
                h = unit[1]
                rows = slice((h % 2) * HD, (h % 2 + 1) * HD)
                return mqT[rows, h // 2, tokens(tb)], mkT[rows, h // 2, :]

            attention(UNITS2, operands2, lambda unit, c: mkv[:, c, T + unit[1] * HD:T + (unit[1] + 1) * HD],
                      [(0, T), (T, 2 * T)], lambda unit, tb: None)
            pe.wait_ge(s_mix, 1)
            rows_to_features("mixT", osum)
            wait_hT("mixT")
            for n in range(2):
                project_rows("out2", "out2", n)
            pe.wait_ge(s_xn, 5)
            rows_to_features("h4T", tmp)
            wait_hT("h4T")
            for n in range(4):
                project_features("wq", n, [("wq", 2 * n), ("wq", 2 * n + 1)])
            for n in range(8):
                wait_read(pe, ("wq", n))
            pe.wait_ge(s_keys, 1)
            keysT = keep.rearrange("p (c n) -> p c n", c=16)
            def key_scores(n):
                tb, q = n // 4, n % 4
                ps = begin(("keys", n))
                for i in range(4):
                    hc = 4 * q + i
                    last = mm(ps[:, i * P:(i + 1) * P], pqT[:, hc, tokens(tb)], keysT[:, hc, :])
                end(last, ("keys", n))

            def expert_scores(tile_, pair):
                (slot_, at), q = tile_
                pe.wait_ge(loaded[slot_], at)
                if q is not None:
                    pe.wait_ge(s_gelu, q)
                u = ring[:, slot_, :].rearrange("p (j k i) -> p j k i", j=2, k=KD)
                for jj in range(2):
                    for k in range(KD):
                        last = mm(banks[pair % 2][:, jj * T:(jj + 1) * T], u[:, jj, k, :], hT[:, k, :],
                                  start=(k == 0), stop=(k == KD - 1))
                last.then_inc(w_used, 1)

            def tile_at(first, r, i):
                n = first + i
                return n % RING, r * 16 + 16 * (n // RING + 1)

            U1, V1, U2, V2 = (N_TILES + n * HALF_PAIRS for n in range(4))

            for n in range(6):
                key_scores(n)
            pe.drain().then_inc(w_used, 1)
            for i in range(4):
                expert_scores((tile_at(U1, 0, i), i - 1 if i >= 2 else None), i)
            for n in range(6, 8):
                key_scores(n)
            with pe.Fori(1, EARLY // 4, 1) as r:
                for i in range(4):
                    expert_scores((tile_at(U1, r, i), r * 4 + i - 1), i)
            pe.wait_ge(s_slot, 1)
            ps = begin(("idT", 0))
            for c in range(2):
                for tb in range(TB):
                    last = nc.tensor.transpose(ps[:, c * T + tb * P:c * T + (tb + 1) * P],
                                               slot[:, tb, c, :], ident[:, :])
            end(last, ("idT", 0))
            ps = begin(("idT", 1))
            for tb in range(TB):
                last = nc.tensor.transpose(ps[:, tb * P:(tb + 1) * P], slot[:, tb, 2, :], ident[:, :])
            end(last, ("idT", 1))
            for b in range(2, 8):
                pe.wait_ge(drained[b], USED[b])

            def gate_tokens(e, b, waits=True):
                for g in range(2):
                    pe.wait_ge(s_oh, e * 2 + g + 1)
                    if g == 0 and waits:
                        pe.wait_ge(s_gdr, e - 1)
                    for i in range(4):
                        c = (4 * g + i) * HD
                        for part in range(3):
                            last = mm(banks[2 + b][:, c:c + HD], hot1[:, g, i, :], hotg[:, g, i, part, :],
                                      start=(part == 0), stop=(part == 2))
                    last.then_inc(s_gfull, 1)

            acc = {(tb, c): banks[4 + 2 * tb + c] for tb in range(TB) for c in range(2)}

            for tb in range(TB):
                for c in range(2):
                    last = nc.tensor.matmul(acc[tb, c][:, :], ident[:, :], x[:, tb, c * 512:(c + 1) * 512],
                                            start=True, stop=False, skip_group_check=True)
            last.then_inc(s_seed, 1)

            def expert_values(first, half, r, i, stop=False):
                q = r * 4 + i
                pe.wait_ge(s_mlo, q + half * HALF_PAIRS + 1)
                for jj in range(2):
                    if jj == 0:
                        pe.wait_ge(s_vlo, q + SPLIT_V[half] + 1)
                    else:
                        pe.wait_ge(w_used, q + first + 1)
                    for tb in range(TB):
                        t = slice(jj * T + tb * P, jj * T + (tb + 1) * P)
                        for w, parts in ((mix_hi, (v_hi, v_lo)), (mix_lo, (v_hi,))):
                            for c in range(2):
                                for v in parts:
                                    last = nc.tensor.matmul(
                                        acc[tb, c][:, :], w[:, i % 2, t], v[:, jj, c * 512:(c + 1) * 512],
                                        start=False, stop=stop and jj == 1 and w is mix_lo,
                                        skip_group_check=True)
                    last.then_inc(s_vused, 1)

            def split_scores(first, r, i):
                q = r * 4 + i
                pe.wait_ge(s_gelu, q + HALF_PAIRS - 1)
                for jj in range(2):
                    if jj == 0:
                        pe.wait_ge(s_vlo, q + SPLIT_U + 1)
                    else:
                        pe.wait_ge(w_used, q + first + 1)
                    parts = ((v_hi, hT_hi), (v_hi, hT_lo), (v_lo, hT_hi))
                    for k in range(KD):
                        for n, (u, h) in enumerate(parts):
                            last = mm(banks[i % 2][:, jj * T:(jj + 1) * T], u[:, jj, k * P:(k + 1) * P],
                                      h[:, k, :], start=(k == 0 and n == 0), stop=(k == KD - 1 and n == 2))
                    last.then_inc(s_vused, 1)

            def first_gates(r, first=False):
                for i in range(4):
                    for b in range(2):
                        gate_tokens(r * 8 + 2 * i + b, b, not (first and i == 0))
                    expert_scores((tile_at(U1 + EARLY, r, i), r * 4 + EARLY + i - 1), i)

            first_gates(0, True)
            with pe.Fori(1, (HALF_PAIRS - EARLY) // 4, 1) as r:
                first_gates(r)
            with pe.Fori(0, HALF_PAIRS // 4, 1) as r:
                for i in range(4):
                    expert_values(V1, 0, r, i)
            pe.wait_ge(s_hlo, 1)
            with pe.Fori(0, HALF_PAIRS // 4, 1) as r:
                for i in range(4):
                    gate_tokens(r * 4 + i + T // 8, i % 2)
                    split_scores(U2, r, i)
            with pe.Fori(0, HALF_PAIRS // 4 - 1, 1) as r:
                for i in range(4):
                    expert_values(V2, 1, r, i)
            for i in range(4):
                expert_values(V2, 1, HALF_PAIRS // 4 - 1, i, stop=(i == 3))

        @block.scalar
        def _(act):
            steps = [0]

            def link(ins):
                steps[0] += 1
                ins.then_inc(a_step, 1)
                act.wait_ge(a_step, steps[0])

            def root(i, src):
                for tb in range(TB):
                    link(nc.scalar.activation(junk, src[:, tb, :], ACT.Square,
                                              accum_out=ssq[:, 2 * i + tb:2 * i + tb + 1]))
                nc.scalar.activation(rms[:, 2 * i:2 * i + 2], ssq[:, 2 * i:2 * i + 2], ACT.Sqrt,
                                     bias=eps, scale=1.0 / D).then_inc(s_ssq, 1)

            def features_out(what, gain, bias=None, plain_from=KD):
                for q in (0, 2):
                    ps = wait_full(act, (what, q))
                    for kk in range(2):
                        k = 2 * q + kk
                        src = ps[:, kk * T:(kk + 1) * T]
                        if gain is None or k >= plain_from:
                            ins = nc.scalar.copy(hT[:, k, :], src)
                        elif bias is None:
                            ins = nc.scalar.activation(hT[:, k, :], src, ACT.Copy, scale=gain[:, k:k + 1])
                        else:
                            ins = nc.scalar.activation(hT[:, k, :], src, ACT.Identity,
                                                       scale=gain[:, k:k + 1], bias=bias[:, k:k + 1])
                    free(ins, (what, q))

            def attention(units, l_col, cols):
                base = 0 if units is UNITS1 else len(UNITS1)
                for i, unit in enumerate(units):
                    ps = wait_full(act, ("S", *unit))
                    act.wait_ge(s_nmax, base + i + 1)
                    if i >= 2:
                        wait_full(act, ("PT", *units[i - 2]))
                    for tb in range(TB):
                        a, b = cols[tb]
                        c = l_col(unit, tb)
                        ins = nc.scalar.activation(
                            prob[:, i % 2, a:b], ps[:, a:b], ACT.Exp,
                            bias=nmax[:, 2 * (i % 4) + tb:2 * (i % 4) + tb + 1],
                            accum_out=lsum[:, c:c + 1])
                    free(ins, ("S", *unit))

            act.dma_start(tmp[:, :, :], mem_in.rearrange("(b p) d -> p b d", p=P)).then_inc(s_mem, 16)
            act.dma_start(ident[:, :], ident_in[:, 0:P]).then_inc(s_small, 16)
            act.dma_start(iota[:, :], ident_in[:, P:2 * P]).then_inc(s_small, 16)
            act.dma_start(vec, vec_in).then_inc(s_small, 16)
            act.dma_start(const, const_in).then_inc(s_small, 16)
            act.dma_start(posi, pos_in).then_inc(s_small, 16)
            act.wait_ge(s_eps, 1)
            act.wait_ge(s_mem, 16)
            root(0, tmp)
            act.wait_ge(s_x, 16)
            act.wait_ge(s_ssq, 1)
            root(1, x)
            features_out("memT", vall("memg"))
            for tb in range(TB):
                ps = wait_full(act, ("mkv", tb))
                free(nc.scalar.copy(mkv[:, tb, :], ps[:, :]), ("mkv", tb))
            act.wait_ge(s_trig, 1)
            for src, dst, scale in ((trig[:, 3, :], sind[:, :, 32:64], 1.0), (trig[:, 3, :], sind[:, :, 0:32], -1.0),
                                    (trig[:, 5, :], cosd[:, :, 0:32], 1.0), (trig[:, 5, :], cosd[:, :, 32:64], 1.0)):
                nc.scalar.activation(dst, src.rearrange("p (b f) -> p b f", b=TB), ACT.Sin,
                                     scale=scale).then_inc(s_sin, 1)
            act.wait_ge(s_gain, 1)
            features_out("h1T", gain1, mod[:, 0:KD])
            act.wait_ge(s_mksq, 1)
            nc.scalar.activation(stat[:, 104:112], stat[:, 104:112], ACT.Sqrt, bias=eps,
                                 scale=1.0 / HD).then_inc(s_hrt, 1)
            for tb in range(TB):
                ps = wait_full(act, ("in", 3, tb))
                nc.scalar.copy(plain[:, tb, 0:256], ps[:, 256:512]).then_inc(s_pv, 1)
            for tb in range(TB):
                ps = wait_full(act, ("in", 4, tb))
                ins = nc.scalar.copy(plain[:, tb, 256:476], ps[:, 0:220])
                ins.then_inc(s_pv, 1)
                act.wait_ge(s_pv, 3 + tb)
                free(nc.scalar.activation(sig[:, tb, :], plain[:, tb, PL_GL:PL_WI], ACT.Sigmoid), ("in", 4, tb))
            ps = wait_full(act, ("mkT",))
            free(nc.scalar.activation(mkT.rearrange("p a t -> p (a t)"), ps[:, :], ACT.Copy,
                                      scale=vcol("kg")), ("mkT",))
            for n in range(7):
                ps = wait_full(act, ("pairT", n))
                dst = pairT[:, 2 * n:2 * n + 2, :].rearrange("p a t -> p (a t)")
                if 2 * n < PAIR_QI:
                    ins = nc.scalar.mul(dst, ps[:, :], SCALE)
                else:
                    ins = nc.scalar.copy(dst, ps[:, :])
                free(ins, ("pairT", n))
            for which in range(2):
                ps = wait_full(act, ("cmp", which))
                link(nc.scalar.copy(hbias[:, which:which + 1], ps[:, 30:31]))
                for g in range(2):
                    src = ps[:, g * N_CMP:(g + 1) * N_CMP]
                    if which == 0:
                        dst = hidk[:, g, 0:N_CMP]
                    else:
                        dst = hidv[:, 4 * g:4 * g + 4, 0:N_CMP]
                        src = src.unsqueeze(1).to_broadcast([P, 4, N_CMP])
                    ins = nc.scalar.activation(dst, src, ACT.Gelu_apprx_tanh, bias=hbias[:, which:which + 1])
                free(ins, ("cmp", which))
            ps = wait_full(act, ("kcmp",))
            free(nc.scalar.copy(kcmpT[:, 0:N_CMP], ps[:, 0:N_CMP]), ("kcmp",))
            act.wait_ge(s_sc, 1)
            nc.scalar.activation(sc[:, :, 0:N_CMP], sc[:, :, 0:N_CMP], ACT.Exp).then_inc(s_pc, 1)
            for n in range(4):
                ps = wait_full(act, ("L", n))
                w = (n // 2 + 1) * T
                free(nc.scalar.activation(relu[:, n, 0:w], ps[:, 0:w], ACT.Relu), ("L", n))
            ps = wait_full(act, ("pcT",))
            free(nc.scalar.copy(pcT.rearrange("p b t -> p (b t)"), ps[:, 0:T]), ("pcT",))
            attention(UNITS1, lambda u, tb: KINDS[u[0]] + tb * HEADS + u[1], [(0, P), (P, P + T)])
            features_out("oT", None)

            def rows_out(what, i):
                for n in range(2):
                    for tb in range(TB):
                        ps = wait_full(act, (what, n, tb))
                        ins = nc.scalar.copy(tmp[:, tb, n * 512:(n + 1) * 512], ps[:, :])
                        free(ins, (what, n, tb))
                for n in range(2):
                    for tb in range(TB):
                        wait_read(act, (what, n, tb))
                root(i, tmp)

            rows_out("out", 2)
            for n in range(4):
                ps = wait_full(act, ("gg", n))
                free(nc.scalar.copy(ggb[:, n // 2, (n % 2) * 512:(n % 2 + 1) * 512], ps[:, :]), ("gg", n))
            act.wait_ge(s_x1, 1)
            root(3, x)
            features_out("h2T", gain2, mod[:, 24:32])
            for n in range(16):
                ps = wait_full(act, ("up", n))
                free(nc.scalar.activation(upT[:, 2 * n:2 * n + 2, :].rearrange("p a t -> p (a t)"),
                                          ps[:, :], ACT.Relu), ("up", n))
            rows_out("down", 4)
            act.wait_ge(s_x1, 2)
            root(5, x)
            features_out("h3T", vall("mix2"))
            for name, dst, scale in (("sbq", sbqT, SCALE), ("sbk", sbkT, 1.0)):
                for n in range(2):
                    ps = wait_full(act, (name, n))
                    free(nc.scalar.mul(dst[:, 2 * n:2 * n + 2, :].rearrange("p a t -> p (a t)"), ps[:, :], scale),
                         (name, n))
            for tb in range(TB):
                ps = wait_full(act, ("sbv", tb))
                free(nc.scalar.copy(sbv[:, tb, :], ps[:, :]), ("sbv", tb))
            for n in range(2):
                ps = wait_full(act, ("hgq", n))
                link(nc.scalar.copy(hq[:, n * 512:(n + 1) * 512], ps[:, :]))
                free(nc.scalar.activation(hsig[:, n * 512:(n + 1) * 512], ps[:, :], ACT.Sigmoid), ("hgq", n))
            for n in range(2):
                ps = wait_full(act, ("hgf", n))
                free(nc.scalar.activation(hf[:, n * 512:(n + 1) * 512], ps[:, :], ACT.Sigmoid), ("hgf", n))
            for tb in range(TB):
                ps = wait_full(act, ("hig", tb))
                free(nc.scalar.copy(hig[:, tb, :], ps[:, :]), ("hig", tb))
            for tb in range(TB):
                wait_read(act, ("hig", tb))
                ins = nc.scalar.activation(tmp[:, tb, 0:256], hig[:, tb, 256:512], ACT.Sigmoid)
            ins.then_inc(s_gsig, 1)
            for tb in range(TB):
                ps = wait_full(act, ("mq", tb))
                free(nc.scalar.copy(mqn[:, tb, :], ps[:, 0:T]), ("mq", tb))
            act.wait_ge(s_mksq, 2)
            nc.scalar.activation(stat[:, 104:112], stat[:, 104:112], ACT.Sqrt, bias=eps,
                                 scale=1.0 / HD).then_inc(s_hrt, 1)
            ps = wait_full(act, ("mqT",))
            free(nc.scalar.activation(mqT.rearrange("p a t -> p (a t)"), ps[:, :], ACT.Copy,
                                      scale=vcol("qg")), ("mqT",))
            act.wait_ge(s_lb1, 1)
            nc.scalar.activation(lb[:, 0:8], lb[:, 0:8], ACT.Exp).then_inc(s_lb2, 1)
            for h in range(HEADS):
                ps = wait_full(act, ("z", h))
                link(nc.scalar.activation(zabs[:, h % 2, :], ps[:, 0:384], ACT.Abs))
                nc.scalar.activation(zexp[:, h, :], zabs[:, h % 2, :], ACT.Exp, scale=-1.0).then_inc(s_zln, 1)
            act.wait_ge(s_zln, HEADS)
            nc.scalar.activation(zexp, zexp, ACT.Ln, bias=one).then_inc(s_zln, 1)
            act.wait_ge(s_hf, 1)
            nc.scalar.activation(hb, hf, ACT.Ln).then_inc(s_hlog, 1)
            for h in range(HEADS):
                ps = wait_full(act, ("ca", h))
                if h >= 2:
                    act.wait_ge(s_sbd, h - 1)
                free(nc.scalar.activation(aT[:, h % 2, :], ps[:, 0:384], ACT.Exp), ("ca", h))
            for lv in range(1, 9):
                act.wait_ge(s_harg, lv)
                nc.scalar.activation(harg, harg, ACT.Exp).then_inc(s_hexp, 1)
            attention(UNITS2, lambda u, tb: KINDS["mem"] + tb * 4 + u[1], [(0, T), (T, 2 * T)])
            act.wait_ge(s_hsq, 1)
            nc.scalar.activation(hstat[1][:, 0:24], hstat[0][:, 0:24], ACT.Sqrt, bias=eps,
                                 scale=1.0 / HD).then_inc(s_hrt, 1)
            features_out("mixT", vall("headg"), plain_from=6)
            act.wait_ge(s_x1, 3)
            root(0, x)
            features_out("h4T", vall("ffn2"))
            for n in range(0, 8, 2):
                ps = wait_full(act, ("wq", n))
                free(nc.scalar.copy(pqT[:, 2 * n:2 * n + 2, :].rearrange("p a t -> p (a t)"), ps[:, :]), ("wq", n))

            def gelu(done, half, index, bank):
                act.wait_ge(*done)
                dst = area[1 - half].rearrange("p (q n) -> p q n", q=HALF_PAIRS)
                piece = dst[:, index, :] if isinstance(index, int) else \
                    dst[:, bass.ds(index, 1), :].rearrange("p o n -> p (o n)")
                nc.scalar.activation(piece, banks[bank][:, :], ACT.Gelu).then_inc(s_gelu, 1)

            def copy_gates(e, half, b, t0):
                act.wait_ge(s_gfull, e * 2 + 2)
                dst = area[half].rearrange("p (t j) -> p t j", t=T)
                nc.scalar.copy(dst[:, bass.ds(t0, 8), :],
                               banks[2 + b][:, :].rearrange("p (t j) -> p t j", t=8)).then_inc(s_gdr, 1)

            n = TILE_AT[("keys", 0, 0)]
            act.wait_ge(loaded[n % RING], 16 * (n // RING + 1))
            nc.scalar.copy(keep, tile(("keys", 0, 0))).then_inc(s_keys, 1)
            U1, U2 = N_TILES, N_TILES + 2 * HALF_PAIRS
            with act.Fori(0, EARLY // 4, 1) as r:
                for i in range(4):
                    gelu((w_used, r * 4 + U1 + i + 1), 0, r * 4 + i, i % 2)
            act.wait_ge(s_gexp, 1)
            nc.scalar.activation(best2, best2, ACT.Exp).then_inc(s_gex2, 1)
            for n in range(2):
                ps = wait_full(act, ("idT", n))
                if n == 0:
                    dst, src = keyT.rearrange("p r t -> p (r t)"), ps[:, :]
                else:
                    dst, src = gateT[:, :], ps[:, 0:T]
                free(nc.scalar.copy(dst, src), ("idT", n))
            with act.Fori(0, (HALF_PAIRS - EARLY) // 4, 1) as r:
                for i in range(4):
                    for b in range(2):
                        copy_gates(r * 8 + 2 * i + b, 0, b, r * 64 + (2 * i + b) * 8)
                    gelu((w_used, r * 4 + U1 + EARLY + i + 1), 0, r * 4 + EARLY + i, i % 2)

            def high_weights(half, index, i, first=False):
                act.wait_ge(s_w, index + half * HALF_PAIRS + 1)
                above_zero(act, s_vused, (index + SPLIT_V[half] - (0 if first else 1)) * 2)
                nc.scalar.copy(mix_hi[:, i % 2, :], pair_weights(half, index)).then_inc(s_mhi, 1)

            def high_tile(first, before, r, i):
                q = r * 4 + i
                act.wait_ge(loaded[(first + i) % RING], r * 16 + 16 * ((first + i) // RING + 1))
                for jj in range(2):
                    above_zero(act, s_vused, (q + before) * 2 + jj - 1)
                    nc.scalar.copy(v_hi[:, jj, :], j_rows(first, i, jj)).then_inc(s_vhi, 1)

            def high_parts(first, half):
                rounds = HALF_PAIRS // 4
                high_weights(half, 0, 0, True)
                for i in range(4):
                    high_tile(first, SPLIT_V[half], 0, i)
                    high_weights(half, i + 1, i + 1)
                with act.Fori(1, rounds - 1, 1) as r:
                    for i in range(4):
                        high_tile(first, SPLIT_V[half], r, i)
                        high_weights(half, r * 4 + i + 1, i + 1)
                for i in range(4):
                    high_tile(first, SPLIT_V[half], rounds - 1, i)
                    if i < 3:
                        high_weights(half, (rounds - 1) * 4 + i + 1, i + 1)

            act.wait_ge(s_seed, 1)
            high_parts(U1 + HALF_PAIRS, 0)
            act.wait_ge(s_vused, 2 * SPLIT_U)
            nc.scalar.copy(hT_hi[:, :, :], hT[:, :, :]).then_inc(s_hhi, 1)

            def second_scores(r, i, first=False):
                high_tile(U2, SPLIT_U, r, i)
                if not first:
                    gelu((s_vused, (r * 4 + SPLIT_U + i) * 2), 1, r * 4 + i - 1, (i - 1) % 2)
                copy_gates(r * 4 + i + T // 8, 1, i % 2, r * 32 + i * 8)

            for i in range(4):
                second_scores(0, i, i == 0)
            with act.Fori(1, HALF_PAIRS // 4, 1) as r:
                for i in range(4):
                    second_scores(r, i)
            gelu((s_vused, (SPLIT_U + HALF_PAIRS) * 2), 1, HALF_PAIRS - 1, 1)
            high_parts(U2 + HALF_PAIRS, 1)
            act.wait_ge(s_vused, 6 * HALF_PAIRS)
            for tb in range(TB):
                nc.scalar.copy(x[:, tb, 512:1024], banks[4 + 2 * tb + 1][:, :]).then_inc(s_res, 1)

        @block.vector
        def _(dve):
            steps = [0]

            def link(ins):
                steps[0] += 1
                ins.then_inc(v_step, 1)
                dve.wait_ge(v_step, steps[0])

            tt = nc.vector.tensor_tensor
            ts = nc.vector.tensor_scalar
            stt = nc.vector.scalar_tensor_tensor

            def normed(i, src, dst=tmp):
                j = i % 6
                dve.wait_ge(s_ssq, i + 1)
                link(nc.vector.reciprocal(rstd[:, 2 * j:2 * j + 2], rms[:, 2 * j:2 * j + 2]))
                for tb in range(TB):
                    ins = ts(dst[:, tb, :], src[:, tb, :], rstd[:, 2 * j + tb:2 * j + tb + 1], None, ALU.mult)
                    if tb == 0:
                        link(ins)
                ins.then_inc(s_xn, 1)

            def features_out(what, gain, bias=None, plain_from=KD):
                for q in (1, 3):
                    ps = wait_full(dve, (what, q))
                    for kk in range(2):
                        k = 2 * q + kk
                        src = ps[:, kk * T:(kk + 1) * T]
                        if gain is None or k >= plain_from:
                            ins = nc.vector.tensor_copy(hT[:, k, :], src)
                        elif bias is None:
                            ins = ts(hT[:, k, :], src, gain[:, k:k + 1], None, ALU.mult)
                        else:
                            ins = ts(hT[:, k, :], src, gain[:, k:k + 1], bias[:, k:k + 1], ALU.mult, ALU.add)
                    free(ins, (what, q))

            def head_norm(src, n_heads, stats):
                sq = junk[:, 0:n_heads * HD].rearrange("p (h d) -> p h d", h=n_heads)
                link(tt(sq, src, src, ALU.mult))
                link(nc.vector.tensor_reduce(stats, sq, AX.X, ALU.add))

            def residual(i, ggrow):
                dve.wait_ge(s_ssq, i + 1)
                j = i % 6
                link(nc.vector.reciprocal(rstd[:, 2 * j:2 * j + 2], rms[:, 2 * j:2 * j + 2]))
                for tb in range(TB):
                    link(stt(tmp[:, tb, :], tmp[:, tb, :], rstd[:, 2 * j + tb:2 * j + tb + 1], ggrow,
                             ALU.mult, ALU.mult))
                    link(tt(x[:, tb, :], x[:, tb, :], tmp[:, tb, :], ALU.add))
                nc.vector.memset(coef[:, 0:1], 0.0).then_inc(s_x1, 1)

            nc.vector.memset(eps, EPS).then_inc(s_eps, 1)
            link(nc.vector.memset(one, 1.0))
            link(nc.vector.memset(negones, -1.0))
            for w in range(2):
                link(nc.vector.memset(kvT[w], 0.0))
            link(nc.vector.memset(hidv, 0.0))
            link(nc.vector.memset(sc, 0.0))
            dve.wait_ge(s_small, SMALL)
            link(nc.vector.tensor_copy(identb, ident[:, :]))
            link(nc.vector.tensor_copy(causalb, con("causal")))
            link(nc.vector.tensor_copy(strictb, con("strict")))
            for w, name in enumerate(("pe_k", "pe_v")):
                link(nc.vector.tensor_copy(kvT[w][:, 2, 0:32:2], vall(name)))
            link(nc.vector.tensor_copy(posf, posi))
            nc.vector.memset(coef[:, 0:1], 0.0).then_inc(s_const, 1)

            def weigh(name):
                _, n, half = name
                at = TILE_AT[name]
                acc = ada_sum(n)
                dve.wait_ge(loaded[at % RING], 16 * (at // RING + 1))
                for kk in range(4):
                    k = 4 * half + kk
                    w = km(name)[:, kk, :]
                    if k == 0:
                        ins = ts(acc, w, vcol("c", k), None, ALU.mult)
                    else:
                        ins = stt(acc, w, vcol("c", k), acc, ALU.mult, ALU.add)
                    if kk < 3:
                        link(ins)
                ins.then_inc(w_used, 1)
                dve.wait_ge(w_used, at + 1)

            dve.wait_ge(s_mem, 16)
            normed(0, tmp)
            weigh(("ada", 0, 0))
            weigh(("ada", 0, 1))
            features_out("memT", vall("memg"))
            for n in range(1, 4):
                for half in range(2):
                    weigh(("ada", n, half))
            def tr(i):
                return trig[:, i, :]
            for tb in range(TB):
                link(ts(tr(0)[:, tb * 32:(tb + 1) * 32], con("invf"), posf[:, tb:tb + 1], None, ALU.mult))
            link(ts(tr(1), tr(0), 1.0 / (2 * math.pi), ROUND, ALU.mult, ALU.add))
            link(ts(tr(2), tr(1), -ROUND, None, ALU.add))
            link(stt(tr(3), tr(2), -PI2_A, tr(0), ALU.mult, ALU.add))
            link(stt(tr(3), tr(2), -PI2_B, tr(3), ALU.mult, ALU.add))
            link(stt(tr(3), tr(2), -PI2_C, tr(3), ALU.mult, ALU.add))
            link(ts(tr(5), tr(3), math.pi / 2, None, ALU.add))
            link(ts(tr(6), tr(5), math.pi, -2 * math.pi, ALU.is_gt, ALU.mult))
            link(tt(tr(5), tr(5), tr(6), ALU.add))
            link(ts(tr(3), tr(3), PI_IN, -PI_IN, ALU.min, ALU.max))
            ts(tr(5), tr(5), PI_IN, -PI_IN, ALU.min, ALU.max).then_inc(s_trig, 1)

            ps = wait_full(dve, ("ada", 0))
            link(tt(mod[:, 0:16], ps[:, 0:16], vcol("b_ada", 0, 16), ALU.add))
            free(stt(gain1, mod[:, 8:16], 1.0, vall("g_pre_mix"), ALU.add, ALU.mult), ("ada", 0))
            wait_read(dve, ("ada", 0))
            nc.vector.memset(coef[:, 0:1], 0.0).then_inc(s_gain, 1)
            wait_full(dve, ("memT", 3))
            normed(1, x)
            wait_full(dve, ("mkv", 1))
            features_out("h1T", gain1, mod[:, 0:KD])
            for tb in range(TB):
                wait_read(dve, ("mkv", tb))
                head_norm(mkv[:, tb, 0:T].rearrange("p (h d) -> p h d", h=4), 4, stat[:, 104 + 4 * tb:108 + 4 * tb])
            nc.vector.memset(coef[:, 0:1], 0.0).then_inc(s_mksq, 1)
            dve.wait_ge(s_hrt, 1)
            link(nc.vector.reciprocal(stat[:, 112:120], stat[:, 104:112]))
            for tb in range(TB):
                v = mkv[:, tb, 0:T].rearrange("p (h d) -> p h d", h=4)
                ins = tt(v, v, stat[:, 112 + 4 * tb:116 + 4 * tb].unsqueeze(2).to_broadcast([P, 4, HD]), ALU.mult)
                if tb == 0:
                    link(ins)
            ins.then_inc(s_mkn, 1)
            dve.wait_ge(s_sin, 4)
            for n in range(4):
                nh = 8 if n < 3 else 4
                for tb in range(TB):
                    name = ("in", n, tb)
                    ps = wait_full(dve, name)
                    if n == 3:
                        dve.wait_ge(s_pv, tb + 1)
                    src = ps[:, 0:nh * HD].rearrange("p (h d) -> p h d", h=nh)
                    dst = rot[:, tb, n * 512:n * 512 + nh * HD].rearrange("p (h d) -> p h d", h=nh)
                    t2 = rtmp[:, tb, 0:nh * HD].rearrange("p (h d) -> p h d", h=nh)

                    def table(t, a, b):
                        return t[:, tb, a:b].unsqueeze(1).to_broadcast([P, nh, b - a])

                    tt(dst, src, table(cosd, 0, HD), ALU.mult)
                    tt(t2[:, :, 0:32], src[:, :, 32:64], table(sind, 0, 32), ALU.mult)
                    link(tt(t2[:, :, 32:64], src[:, :, 0:32], table(sind, 32, 64), ALU.mult))
                    ins = tt(dst, dst, t2, ALU.add)
                    free(ins, name)
                    wait_read(dve, name)
            nc.vector.memset(coef[:, 0:1], 0.0).then_inc(s_rot, 1)
            for which, name in enumerate((("kcT",), ("vcT",))):
                ps = wait_full(dve, name)
                v = ps[:, :].rearrange("p (g t) -> p g t", g=2)
                nc.vector.tensor_copy(kvT[which][0:HD, 0:2, :], v[0:HD, :, :])
                free(nc.vector.tensor_copy(kvT[which][HD:P, 0:2, 0:T - 1], v[HD:P, :, 1:T]), name)
            ps = wait_full(dve, ("vblk",))
            ins = tt(vblk, ps[:, 0:HD].unsqueeze(1).to_broadcast([P, HEADS, HD]),
                     con("blk").unsqueeze(2).to_broadcast([P, HEADS, HD]), ALU.mult)
            free(ins, ("vblk",))
            wait_read(dve, ("vblk",))
            nc.vector.memset(coef[:, 0:1], 0.0).then_inc(s_vblk, 1)
            sv = sc[:, :, 0:N_CMP]

            def per_block(name):
                return con(name).rearrange("p (b n) -> p b n", b=TB)[:, :, 0:N_CMP]
            for g in range(2):
                ps = wait_full(dve, ("Sc", g))
                for tb in range(TB):
                    hs = slice(tb * HEADS + 4 * g, tb * HEADS + 4 * g + 4)
                    ins = tt(sv[:, hs, :],
                             ps[:, tb * 64:(tb + 1) * 64].rearrange("p (h n) -> p h n", h=4)[:, :, 0:N_CMP],
                             per_block("cmpadd")[:, tb, :].unsqueeze(1).to_broadcast([P, 4, N_CMP]), ALU.add)
                free(ins, ("Sc", g))
                wait_read(dve, ("Sc", g))
            link(nc.vector.tensor_reduce(cmax, sv, AX.X, ALU.max))
            tt(sv, sv, cmax.unsqueeze(2).to_broadcast([P, 16, N_CMP]), ALU.subtract).then_inc(s_sc, 1)
            for tb in range(TB):
                link(ts(wsc[:, tb, :], plain[:, tb, PL_WI:PL_WI + 4], IDX_SCALE, None, ALU.mult))
            for tb in range(TB):
                width = (tb + 1) * P
                wait_read(dve, ("L", 2 * tb))
                wait_read(dve, ("L", 2 * tb + 1))
                for h in range(IDX_HEADS):
                    r = relu[:, 2 * tb + h % 2, (h // 2) * width:(h // 2 + 1) * width]
                    if h == 0:
                        ins = ts(score[:, tb, 0:width], r, wsc[:, tb, h:h + 1], None, ALU.mult)
                    else:
                        ins = stt(score[:, tb, 0:width], r, wsc[:, tb, h:h + 1], score[:, tb, 0:width],
                                  ALU.mult, ALU.add)
                    link(ins)
            dve.wait_ge(s_pc, 1)
            link(nc.vector.tensor_reduce(lsum[:, 0:16], sv, AX.X, ALU.add))
            for tb in range(TB):
                hs = slice(tb * HEADS, (tb + 1) * HEADS)
                ins = tt(sv[:, hs, :], sv[:, hs, :],
                         per_block("cmp01")[:, tb, :].unsqueeze(1).to_broadcast([P, HEADS, N_CMP]), ALU.mult)
            ins.then_inc(s_pcz, 1)
            def key_round(i):
                tb, r = i // 8, i % 8
                width = (tb + 1) * P
                s, w = score[:, tb, 0:width], work[:, tb, 0:width]
                if r == 0:
                    link(tt(score[:, tb, tb * P:width], score[:, tb, tb * P:width], con("causal"), ALU.add))
                src = s if r == 0 else w
                link(nc.vector.max(cmax[:, 0:8], src))
                link(nc.vector.match_replace(w, cmax[:, 0:8], src, TAKEN))
                if r == DSA_K // 8 - 1:
                    link(ts(w, w, 0.5 * TAKEN, NEG, ALU.is_ge, ALU.mult))
                    if tb:
                        nc.vector.tensor_copy(maskd[:, tb, 0:P], w[:, 0:P])
                    tt(maskd[:, tb, tb * P:width], w[:, tb * P:width], con("causal"), ALU.add).then_inc(s_maskd, 1)

            def weighted(kind, psname, tb, col, add, gated=True):
                ps = wait_full(dve, psname)
                dst = osum[:, tb, col:col + 512].rearrange("p (h d) -> p h d", h=HEADS)
                src = ps[:, :].rearrange("p (h d) -> p h d", h=HEADS)
                c = coef[:, tb * 8:(tb + 1) * 8].unsqueeze(2).to_broadcast([P, HEADS, HD])
                if not add:
                    free(tt(dst, src, c, ALU.mult), psname)
                    wait_read(dve, psname)
                else:
                    t = otmp.rearrange("p (h d) -> p h d", h=HEADS)
                    free(tt(t, src, c, ALU.mult), psname)
                    wait_read(dve, psname)
                    link(tt(dst, dst, t, ALU.add))

            def coefficients(kind, gate):
                a = KINDS[kind]
                link(nc.vector.reciprocal(rl, lsum[:, a:a + 16]))
                if gate is None:
                    link(nc.vector.tensor_copy(coef, rl))
                else:
                    g = sig.rearrange("p b (h c) -> p b h c", c=3)[:, :, :, gate]
                    link(tt(coef.rearrange("p (b h) -> p b h", b=TB), rl.rearrange("p (b h) -> p b h", b=TB), g,
                            ALU.mult))

            def attention(units, cols, after):
                base = 0 if units is UNITS1 else len(UNITS1)
                for i in range(len(units) + 3):
                    if i < len(units):
                        ps = wait_full(dve, ("S", *units[i]))
                        if i >= 4:
                            wait_read(dve, ("S", *units[i - 4]))
                        for tb in range(TB):
                            a, b = cols[tb]
                            ins = nc.vector.tensor_reduce(nmax[:, 2 * (i % 4) + tb:2 * (i % 4) + tb + 1],
                                                          ps[:, a:b], AX.X, ALU.max, negate=True)
                        ins.then_inc(s_nmax, 1)
                    if 1 <= i <= len(units):
                        ps = wait_full(dve, ("PT", *units[i - 1]))
                        if i >= 3:
                            dve.wait_ge(s_pvd, base + i - 2)
                        w = cols[1][1]
                        free(nc.vector.tensor_copy(probT[:, (i - 1) % 2, 0:w], ps[:, 0:w]), ("PT", *units[i - 1]))
                    after(i - 2)

            wait_read(dve, ("in", 4, 0))
            wait_read(dve, ("in", 4, 1))
            coefficients("cmp", 0)
            for tb in range(TB):
                weighted("cmp", ("Oc", tb), tb, 0, False)
            dve.wait_ge(w_used, TILE_AT[("ada", 4, 0)])
            rest = [("ada", n, half) for n in range(4, 12) for half in range(2)]

            def after1(i):
                if 0 <= i + 2 < TB * DSA_K // 8:
                    key_round(i + 2)
                if i + 2 >= 16 or i % 2 == 0:
                    if rest:
                        weigh(rest.pop(0))
                if i in (8, 16):
                    kind = UNITS1[i - 1][0]
                    coefficients(kind, 1 if kind == "slc" else 2)
                    for tb in range(TB):
                        weighted(kind, ("O", kind, tb), tb, 0, True)

            attention(UNITS1, [(0, P), (P, P + T)], after1)
            assert not rest
            ps = wait_full(dve, ("ada", 1))
            link(tt(mod[:, 16:48], ps[:, 16:48], vcol("b_ada", 16, 32), ALU.add))
            link(stt(gain2, mod[:, 32:40], 1.0, vall("g_pre_ffn"), ALU.add, ALU.mult))
            link(tt(gg[:, 0:8], mod[:, 16:24], vall("g_post_mix"), ALU.mult))
            free(tt(gg[:, 8:16], mod[:, 40:48], vall("g_post_ffn"), ALU.mult), ("ada", 1))
            wait_read(dve, ("ada", 1))
            nc.vector.memset(coef[:, 0:1], 0.0).then_inc(s_ggf, 1)

            coefficients("dsa", None)
            for tb in range(TB):
                weighted("dsa", ("O", "dsa", tb), tb, 512, False)
            nc.vector.memset(coef[:, 0:1], 0.0).then_inc(s_o, 1)
            features_out("oT", None)
            for n in range(2):
                wait_read(dve, ("gg", n))
            residual(2, ggb[:, 0, :])
            normed(3, x)
            features_out("h2T", gain2, mod[:, 24:32])
            for n in range(16):
                wait_read(dve, ("up", n))
                v = upT[:, 2 * n:2 * n + 2, :]
                tt(v, v, v, ALU.mult).then_inc(s_upsq, 1)
            for n in range(2, 4):
                wait_read(dve, ("gg", n))
            residual(4, ggb[:, 1, :])
            normed(5, x)
            features_out("h3T", vall("mix2"))
            link(nc.vector.memset(hones, 1.0))
            g0, g1 = vcol("gamma", 0, 4), vcol("gamma", 4, 4)
            link(tt(lb[:, 8:12], g0, g1, ALU.max))
            link(tt(lb[:, 0:4], g0, lb[:, 8:12], ALU.subtract))
            tt(lb[:, 4:8], g1, lb[:, 8:12], ALU.subtract).then_inc(s_lb1, 1)
            for tb in range(TB):
                wait_read(dve, ("mq", tb))
                head_norm(mqn[:, tb, :].rearrange("p (h d) -> p h d", h=4), 4, stat[:, 104 + 4 * tb:108 + 4 * tb])
            nc.vector.memset(coef[:, 0:1], 0.0).then_inc(s_mksq, 1)
            dve.wait_ge(s_hrt, 2)
            link(nc.vector.reciprocal(stat[:, 112:120], stat[:, 104:112]))
            link(ts(stat[:, 112:120], stat[:, 112:120], SCALE, None, ALU.mult))
            for tb in range(TB):
                v = mqn[:, tb, :].rearrange("p (h d) -> p h d", h=4)
                ins = tt(v, v, stat[:, 112 + 4 * tb:116 + 4 * tb].unsqueeze(2).to_broadcast([P, 4, HD]), ALU.mult)
                if tb == 0:
                    link(ins)
            ins.then_inc(s_mqs, 1)
            dve.wait_ge(s_lb2, 1)
            link(tt(lb[:, 8:12], lb[:, 0:4], lb[:, 4:8], ALU.add))
            link(nc.vector.reciprocal(lb[:, 8:12], lb[:, 8:12]))
            link(tt(lb[:, 8:12], lb[:, 0:4], lb[:, 8:12], ALU.mult))
            link(ts(lb[:, 12:16], lb[:, 8:12], -1.0, 1.0, ALU.mult, ALU.add))
            for n in range(2):
                wait_read(dve, ("hgf", n))
                wait_read(dve, ("hgq", n))
            for h in range(HG_HEADS):
                cols = slice(h * T, (h + 1) * T)
                link(ts(hf[:, cols], hf[:, cols], lb[:, 12 + h:13 + h], lb[:, 8 + h:9 + h], ALU.mult, ALU.add))
            nc.vector.memset(coef[:, 0:1], 0.0).then_inc(s_hf, 1)
            link(ts(hk, hf, -1.0, 1.0, ALU.mult, ALU.add))
            link(tt(hq, hq, hsig, ALU.mult))

            for h in range(HEADS):
                ps = wait_full(dve, ("z", h))
                dve.wait_ge(s_zln, h + 1)
                ins = ts(zsp[:, h, :], ps[:, 0:384], 0.0, None, ALU.max)
                free(ins, ("z", h))
            wait_read(dve, ("z", HEADS - 2))
            wait_read(dve, ("z", HEADS - 1))
            dve.wait_ge(s_zln, HEADS + 1)
            link(tt(zsp, zsp, zexp, ALU.add))
            strict01 = con("strict01").unsqueeze(1).to_broadcast([P, HEADS, P])
            tt(zsp[:, :, 0:P], zsp[:, :, 0:P], strict01, ALU.mult)
            tt(zsp[:, :, T:T + P], zsp[:, :, T:T + P], strict01, ALU.mult).then_inc(s_zsp, 1)

            dve.wait_ge(s_hlog, 1)
            for h in range(HG_HEADS):
                cols = slice(h * T, (h + 1) * T)
                link(nc.vector.tensor_tensor_scan(hsig[:, cols], hones, hb[:, cols], 0.0, ALU.mult, ALU.add))
            cum = hsig
            for lv in range(9):
                if lv >= 2:
                    wait_full(dve, ("hg", lv - 2, 1))
                if lv == 0:
                    link(nc.vector.tensor_copy(hqe[:, 0, :], hq))
                    nc.vector.tensor_copy(hke[:, 0, :], hk).then_inc(s_hqe, 1)
                else:
                    m = 1 << (lv - 1)
                    ns = 4 * T // (2 * m)
                    c = cum.rearrange("p (s w m) -> p s w m", w=2, m=m)
                    a = harg.rearrange("p (s w m) -> p s w m", w=2, m=m)
                    ref = c[:, :, 0, m - 1:m].to_broadcast([P, ns, m])
                    tt(a[:, :, 1, :], c[:, :, 1, :], ref, ALU.subtract)
                    tt(a[:, :, 0, :], ref, c[:, :, 0, :], ALU.subtract).then_inc(s_harg, 1)
                    dve.wait_ge(s_hexp, lv)
                    link(tt(hqe[:, lv % 2, :], hq, harg, ALU.mult))
                    tt(hke[:, lv % 2, :], hk, harg, ALU.mult).then_inc(s_hqe, 1)
                    dve.wait_ge(s_hqe, lv + 1)
                if lv >= 1:
                    masked(dve, lv - 1, link, tt, stt, hacc, htmp, con, wait_full, wait_read, free)
            ps = wait_full(dve, ("hgx",))
            free(nc.vector.tensor_copy(hx, ps[:, :]), ("hgx",))
            wait_read(dve, ("hgx",))
            nc.vector.memset(coef[:, 0:1], 0.0).then_inc(s_hsc, 1)
            for tb in range(TB):
                ps = wait_full(dve, ("sbo", tb))
                free(nc.vector.tensor_copy(osum[:, tb, 0:512], ps[:, :]), ("sbo", tb))
            for tb in range(TB):
                ps = wait_full(dve, ("hgo", tb))
                free(nc.vector.tensor_copy(osum[:, tb, 512:768], ps[:, 0:256]), ("hgo", tb))
            for name in ("sbo", "hgo"):
                for tb in range(TB):
                    wait_read(dve, (name, tb))
            attention(UNITS2, [(0, T), (T, 2 * T)], lambda i: None)
            link(nc.vector.reciprocal(rl[:, 0:8], lsum[:, 16:24]))
            for tb in range(TB):
                ps = wait_full(dve, ("O", "mem", tb))
                free(tt(osum[:, tb, 768:1024].rearrange("p (h d) -> p h d", h=4),
                        ps[:, 0:256].rearrange("p (h d) -> p h d", h=4),
                        rl[:, tb * 4:(tb + 1) * 4].unsqueeze(2).to_broadcast([P, 4, HD]), ALU.mult),
                     ("O", "mem", tb))
            for tb in range(TB):
                head_norm(osum[:, tb, 0:768].rearrange("p (h d) -> p h d", h=12), 12, hstat[0][:, 12 * tb:12 * tb + 12])
            nc.vector.memset(coef[:, 0:1], 0.0).then_inc(s_hsq, 1)
            dve.wait_ge(s_hrt, 3)
            link(nc.vector.reciprocal(hstat[2][:, 0:24], hstat[1][:, 0:24]))
            dve.wait_ge(s_gsig, 1)
            for tb in range(TB):
                v = osum[:, tb, 0:768].rearrange("p (h d) -> p h d", h=12)
                link(tt(v, v, hstat[2][:, 12 * tb:12 * tb + 12].unsqueeze(2).to_broadcast([P, 12, HD]), ALU.mult))
                link(tt(tmp[:, tb, 0:256], tmp[:, tb, 0:256], hig[:, tb, 256:512], ALU.mult))
                link(tt(osum[:, tb, 512:768], osum[:, tb, 512:768], tmp[:, tb, 0:256], ALU.mult))
            for tb in range(TB):
                wait_read(dve, ("O", "mem", tb))
            nc.vector.memset(coef[:, 0:1], 0.0).then_inc(s_mix, 1)
            features_out("mixT", vall("headg"), plain_from=6)
            for n in range(2):
                for tb in range(TB):
                    ps = wait_full(dve, ("out2", n, tb))
                    v = x[:, tb, n * 512:(n + 1) * 512]
                    free(tt(v, v, ps[:, :], ALU.add), ("out2", n, tb))
            for n in range(2):
                for tb in range(TB):
                    wait_read(dve, ("out2", n, tb))
            nc.vector.memset(coef[:, 0:1], 0.0).then_inc(s_x1, 1)
            normed(6, x)
            features_out("h4T", vall("ffn2"))
            for n in range(1, 8, 2):
                ps = wait_full(dve, ("wq", n))
                free(nc.vector.tensor_copy(pqT[:, 2 * n:2 * n + 2, :].rearrange("p a t -> p (a t)"), ps[:, :]),
                     ("wq", n))

            def top16(src, values, index, scratch):
                v = [values[:, 0:8], values[:, 8:16]]
                i = [index[:, 0:8], index[:, 8:16]]
                link(nc.vector.max(v[0], src))
                nc.vector.max_index(i[0], v[0], src)
                link(nc.vector.match_replace(scratch, v[0], src, TAKEN))
                link(nc.vector.max(v[1], scratch))
                return nc.vector.max_index(i[1], v[1], scratch)

            for tb in range(TB):
                for q in range(4):
                    name = ("keys", 4 * tb + q)
                    ps = wait_full(dve, name)
                    for i in range(4):
                        hc = 4 * q + i
                        ins = top16(ps[:, i * P:(i + 1) * P], best1[:, tb, hc, :],
                                    idx1[:, tb, hc * TOPK:(hc + 1) * TOPK], keytmp[:, i % 2, :])
                        if i < 3:
                            link(ins)
                    free(ins, name)
                    wait_read(dve, name)
                link(nc.vector.tensor_copy(idx1f[:, tb, :, :].rearrange("p a b -> p (a b)"), idx1[:, tb, :]))
                halves = best1[:, tb, :, :].rearrange("p (h c) a -> p h c a", c=2)
                link(tt(cand.rearrange("p h (a b) -> p h a b", a=TOPK),
                        halves[:, :, 0, :].unsqueeze(3).to_broadcast([P, PEER_HEADS, TOPK, TOPK]),
                        halves[:, :, 1, :].unsqueeze(2).to_broadcast([P, PEER_HEADS, TOPK, TOPK]), ALU.add))
                for h in range(PEER_HEADS):
                    link(top16(cand[:, h, :], best2[:, tb, h * TOPK:(h + 1) * TOPK],
                               idx2[:, tb, h * TOPK:(h + 1) * TOPK], candtmp[:, h % 2, :]))
                link(ts(idx2p[:, 2 * tb, :], idx2[:, tb, :], 4, None, ALU.logical_shift_right))
                link(ts(idx2p[:, 2 * tb + 1, :], idx2[:, tb, :], TOPK - 1, None, ALU.bitwise_and))
                for c in range(2):
                    link(nc.vector.tensor_copy(idx2f[:, 2 * tb + c, :], idx2p[:, 2 * tb + c, :]))
                    pk = pick.rearrange("p (h k a) -> p h k a", h=PEER_HEADS, k=TOPK)
                    full_shape = [P, PEER_HEADS, TOPK, TOPK]
                    pos = idx2f[:, 2 * tb + c, :].rearrange("p (h k) -> p h k", h=PEER_HEADS)
                    link(tt(pk.rearrange("p h k a -> p (h k) a"),
                            idx2f[:, 2 * tb + c, :].unsqueeze(2).to_broadcast([P, SLOTS, TOPK]),
                            iota[:, 0:TOPK].unsqueeze(1).to_broadcast([P, SLOTS, TOPK]), ALU.is_equal))
                    keys = idx1f[:, tb, :, :].rearrange("p (h c) a -> p h c a", c=2)[:, :, c, :]
                    link(tt(pk, pk, keys.unsqueeze(2).to_broadcast(full_shape), ALU.mult))
                    link(nc.vector.tensor_reduce(slot[:, tb, c, :], pk.rearrange("p h k a -> p (h k) a"),
                                                 AX.X, ALU.add))
                b2 = best2[:, tb, :].rearrange("p (h k) -> p h k", h=PEER_HEADS)
                link(nc.vector.tensor_copy(gsum[:, tb, :], b2[:, :, 0]))
                link(tt(b2, b2, gsum[:, tb, :].unsqueeze(2).to_broadcast([P, PEER_HEADS, TOPK]), ALU.subtract))
            nc.vector.memset(coef[:, 0:1], 0.0).then_inc(s_gexp, 1)
            dve.wait_ge(s_gex2, 1)
            for tb in range(TB):
                b2 = best2[:, tb, :].rearrange("p (h k) -> p h k", h=PEER_HEADS)
                link(nc.vector.tensor_reduce(gsum[:, tb, :], b2, AX.X, ALU.add))
                link(nc.vector.reciprocal(gsum[:, tb, :], gsum[:, tb, :]))
                link(tt(slot[:, tb, 2, :].rearrange("p (h k) -> p h k", h=PEER_HEADS), b2,
                        gsum[:, tb, :].unsqueeze(2).to_broadcast([P, PEER_HEADS, TOPK]), ALU.mult))
            nc.vector.memset(coef[:, 0:1], 0.0).then_inc(s_slot, 1)
            link(nc.vector.tensor_copy(iotab[:, :], iota[:, :]))
            wait_read(dve, ("idT", 0))
            wait_read(dve, ("idT", 1))
            for part in range(3):
                link(nc.vector.tensor_copy(gates[:, :, part], gateT[:, :]))
                if part < 2:
                    link(tt(gateT[:, :], gateT[:, :], gates[:, :, part], ALU.subtract))

            def one_hots(e, t, half, b, waits=True):
                if waits:
                    dve.wait_ge(s_gfull, e - 1)
                def wide(row, n):
                    return keyT[:, row, bass.ds(t, 4)].unsqueeze(2).to_broadcast([P, 4, n])
                tt(hot2[:, b, :, :], iotab[:, half * HD:(half + 1) * HD].unsqueeze(1).to_broadcast([P, 4, HD]),
                   wide(1, HD), ALU.is_equal).then_inc(s_eq, 1)
                tt(hot1[:, b, :, :], iotab[:, :].unsqueeze(1).to_broadcast([P, 4, P]), wide(0, P), ALU.is_equal)
                dve.wait_ge(s_eq, e + 1)
                tt(hotg[:, b, :, :, :], hot2[:, b, :, :].unsqueeze(2).to_broadcast([P, 4, 3, HD]),
                   gates[:, bass.ds(t, 4), :].unsqueeze(3).to_broadcast([P, 4, 3, HD]), ALU.mult).then_inc(s_oh, 1)

            def gated(half, index):
                dve.wait_ge(s_gelu, index + half * HALF_PAIRS + 1)
                w = pair_weights(half, index).rearrange("p (j t) -> p j t", j=2)
                g = area[half].rearrange("p (t j) -> p j t", t=T)[:, bass.ds(index * 2, 2), :]
                tt(w, w, g, ALU.mult).then_inc(s_w, 1)

            def low_weights(half, index, i):
                dve.wait_ge(s_mhi, index + half * HALF_PAIRS + 1)
                tt(mix_lo[:, i % 2, :], pair_weights(half, index), mix_hi[:, i % 2, :],
                   ALU.subtract).then_inc(s_mlo, 1)

            def low_tile(tiles, before, q, i):
                for jj in range(2):
                    dve.wait_ge(s_vhi, (q + before) * 2 + jj + 1)
                    ins = tt(v_lo[:, jj, :], j_rows(tiles, i, jj), v_hi[:, jj, :], ALU.subtract)
                    ins.then_inc(s_vlo if jj == 0 else w_used, 1)

            def low_values(tiles, half, r, i, last=False):
                q = r * 4 + i
                if not last:
                    gated(half, q + 1)
                low_tile(tiles, SPLIT_V[half], q, i)
                if not last:
                    low_weights(half, q + 1, i + 1)

            for half in range(2):
                first = half * T // 4
                if half == 0:
                    for b in range(2):
                        one_hots(first + b, 4 * b, half, b, False)
                    with dve.Fori(1, T // 8, 1) as r:
                        for b in range(2):
                            one_hots(r * 2 + b + first, r * 8 + 4 * b, half, b)
                else:
                    dve.wait_ge(s_hhi, 1)
                    tt(hT_lo[:, :, :], hT[:, :, :], hT_hi[:, :, :], ALU.subtract).then_inc(s_hlo, 1)
                    with dve.Fori(0, HALF_PAIRS // 4, 1) as r:
                        for i in range(4):
                            for b in range(2):
                                one_hots(r * 8 + 2 * i + b + first, r * 32 + 8 * i + 4 * b, half, b)
                            low_tile(N_TILES + 2 * HALF_PAIRS, SPLIT_U, r * 4 + i, i)
                dve.wait_ge(s_gdr, (half + 1) * T // 8)
                tiles = N_TILES + (2 * half + 1) * HALF_PAIRS
                gated(half, 0)
                low_weights(half, 0, 0)
                dve.wait_ge(w_used, tiles)
                with dve.Fori(0, HALF_PAIRS // 4 - 1, 1) as r:
                    for i in range(4):
                        low_values(tiles, half, r, i)
                for i in range(4):
                    low_values(tiles, half, HALF_PAIRS // 4 - 1, i, i == 3)
            dve.wait_ge(s_vused, 6 * HALF_PAIRS)
            for tb in range(TB):
                nc.vector.tensor_copy(x[:, tb, 0:512], banks[4 + 2 * tb][:, :]).then_inc(s_res, 1)


def masked(dve, lv, link, tt, stt, hacc, htmp, con, wait_full, wait_read, free):
    m = con("hgmask").rearrange("p (l t) -> p l t", l=8)[:, lv, :]
    m = m.unsqueeze(1).to_broadcast([P, HG_HEADS, P])
    for tb in range(TB):
        name = ("hg", lv, tb)
        ps = wait_full(dve, name)
        src = ps[:, :].rearrange("p (h t) -> p h t", h=HG_HEADS)
        acc = hacc[:, tb, :].rearrange("p (h t) -> p h t", h=HG_HEADS)
        if lv == 0:
            free(tt(acc, src, m, ALU.mult), name)
            wait_read(dve, name)
        else:
            t = htmp.rearrange("p (h t) -> p h t", h=HG_HEADS)
            free(tt(t, src, m, ALU.mult), name)
            wait_read(dve, name)
            link(tt(acc, acc, t, ALU.add))


def _chunks(w, cols, kgroups):
    k, n = w.shape
    pad = -n % cols
    if pad:
        w = np.concatenate([w, np.zeros((k, pad), w.dtype)], 1)
        n += pad
    t = w.reshape(kgroups, k // P // kgroups, P, n // cols, cols)
    return t.transpose(3, 0, 2, 1, 4).reshape(n // cols, kgroups, P, -1)


def _features(v):
    return v.reshape(-1, P).T


def _constants():
    c = np.zeros((P, N_CONST), np.float32)
    p, q = np.arange(P)[:, None], np.arange(P)[None, :]

    def put(name, a):
        c[:, _C[name][0]:_C[name][1]] = a
    put("tri", -(p >= q).astype(np.float32))
    put("causal", np.where(q > p, NEG, 0.0))
    put("strict", np.where(p >= q, NEG, 0.0))
    put("strict01", (p < q))
    masks = [(p == q)]
    for m in HG_LEVELS:
        masks.append((p // (2 * m) == q // (2 * m)) & (p % (2 * m) < m) & (q % (2 * m) >= m))
    put("hgmask", np.concatenate(masks, 1))
    n = np.arange(16)
    put("blk", (np.arange(P)[:, None] // 16 == np.arange(HEADS)[None]) & ((np.arange(P) % 16 < N_CMP)[:, None]))
    seen = [((n * CMP_STRIDE + CMP_LEN - 1)[None, :] <= (p + tb * P)) & (n < N_CMP)[None] for tb in range(TB)]
    put("cmpadd", np.concatenate([np.where(s, 0.0, NEG) for s in seen], 1))
    put("cmp01", np.concatenate(seen, 1))
    half = HD // 2
    put("invf", np.float32(10000.0) ** (-np.arange(half, dtype=np.float32) / np.float32(half)))
    keep = np.concatenate([np.eye(P), np.broadcast_to(np.arange(P), (P, P))], 1).astype(np.float32)
    return c, keep


def _weights(i):
    w_in = i["w_in"][0]
    splits = np.cumsum([512] + [128] * 6 + [24, 512, 64, 64, 256, 64, 4])[:-1]
    (qn, kc, vc, ks, vs, kw, vw, gl, qd, kd, vd, qi, ki, wi) = np.split(w_in, splits, 1)
    order = [h for r in range(4) for h in (r, r + 4)]
    qn = qn.reshape(D, 8, HD)[:, order].reshape(D, 512)
    first = np.concatenate([qn, qd, qi, kc, ks, kw, kd, ki, vc, vs, vw, vd, gl, wi], 1)
    w2 = i["w_in_2"][0]
    sbq, sbk, sbv, hq, hf, hi, hg, mq = np.split(w2, np.cumsum([512] * 5 + [256] * 2), 1)
    second = np.concatenate([sbq, sbk, sbv, hq, hf, hi, hg], 1)
    parts = {
        "mem_kv": _chunks(i["w_mem_kv_2"][0], 512, 2),
        "ada": _chunks(i["w_ada"][0], 512, 2),
        "in": _chunks(first, 512, 2),
        "cmp1": np.stack([i[n][0].reshape(16, P, P).transpose(1, 0, 2).reshape(1, P, SLOTW)
                          for n in ("cmp_w1_k", "cmp_w1_v")]),
        "out": _chunks(i["w_out"][0], 512, 2),
        "up": _chunks(i["w_up"][0], 512, 2),
        "down": _chunks(i["w_down"][0], 512, 8).transpose(1, 0, 2, 3),
        "in2": _chunks(second, 512, 2),
        "in2m": _chunks(mq, 256, 1),
        "out2": _chunks(i["w_out_2"][0], 512, 2),
        "wq": _chunks(i["peer_w_query_2"][0], 512, 2),
        "keys": i["peer_sub_keys_2"][0].transpose(3, 0, 1, 2).reshape(1, 1, P, SLOTW),
    }
    tiles = [parts[name][a, b] for name, a, b in TILES]
    pairs = 2 * HALF_PAIRS
    u = i["peer_u_2"][0].reshape(P, pairs, 2, KD, P)
    u = u.transpose(1, 4, 2, 3, 0).reshape(pairs, P, SLOTW)
    v = i["peer_v_2"][0].reshape(P, pairs, SLOTW).transpose(1, 0, 2)
    for half in (slice(0, HALF_PAIRS), slice(HALF_PAIRS, pairs)):
        tiles += list(u[half]) + list(v[half])
    return np.stack(tiles)


def kernel(**inputs):
    import concourse.bacc as _bacc
    from concourse.bass_utils import run_bass_kernel_spmd as _run

    i = {k: np.asarray(v) for k, v in inputs.items()}
    const, keep = _constants()
    pe = [i[n][0].reshape(16, 2 * HD).T for n in ("cmp_pe_k", "cmp_pe_v")]
    vec = np.concatenate(
        [_features(i["c"][0]), _features(i["b_ada"][0]), _features(i["g_pre_mix"][0]),
         _features(i["g_post_mix"][0]), _features(i["g_pre_ffn"][0]), _features(i["g_post_ffn"][0]),
         _features(i["norm_mix_gain_2"][0]), _features(i["norm_ffn_gain_2"][0]),
         _features(i["mem_norm_gain_2"]), _features(i["sb_out_gain_2"].reshape(-1)),
         _features(i["hg_out_gain_2"].reshape(-1)),
         np.concatenate([i["mem_q_gain_2"][0]] * 2)[:, None], np.concatenate([i["mem_k_gain_2"][0]] * 2)[:, None],
         _features(i["gamma_lb_2"][0]), _features(i["gamma_lb_2"][1]), pe[0], pe[1],
         i["cmp_w2_k"][0], i["cmp_w2_v"][0]], 1)
    arrays = {
        "x_dram": i["x"][0], "mem_dram": i["mem_2"][0],
        "pos_dram": i["positions"].reshape(TB, P).T,
        "vec_dram": vec, "ident_dram": keep, "const_dram": const,
        "w_dram": _weights(i),
    }
    arrays = {k: np.ascontiguousarray(a) for k, a in arrays.items()}
    nc = _bacc.Bacc("TRN2", target_bir_lowering=False, num_devices=1)
    args = [nc.dram_tensor(n, a.shape, mybir.dt.from_np(a.dtype), kind="ExternalInput").ap()
            for n, a in arrays.items()]
    out = nc.dram_tensor("out_dram", (T, D), F32, kind="ExternalOutput").ap()
    build(nc, *args, out)
    r = _run(nc, [arrays], core_ids=[0])
    return r.results[0]["out_dram"].reshape(1, T, D)
```
